# Optimizing a Trainium2 kernel written in Bass

```python
import jax
import jax.numpy as jnp
from jax import lax
import numpy as np

D_MODEL = 1024
BATCH = 1
SEQ = 128
DEPTH = 1
DEC_BATCH = 1
DEC_SEQ = 512
PAST_LEN = 128

GRID_W = 64
EPS = 1e-6
NEG_BIG = -1e30
MAX_EXP_ARG = 80.0
CHUNK = 32
MIX_W = D_MODEL // 2
H_A = 4
DH_A = MIX_W // H_A
H_B = 4
DK_B = MIX_W // H_B
DV_B = MIX_W // H_B
H_C = 4
DK_C = MIX_W // (2 * H_C)
DV_C = MIX_W // H_C
R_C = 16
GLA_TAU = 16.0
H_D = 4
DH_D = MIX_W // H_D
CONV_W = 4
LRU_C = 8.0
N_BRANCH = 4
MLSTM_F_BIAS = 3.0
N_KEYS = 128
N_EXPERTS = N_KEYS * N_KEYS
PEER_HEADS = 8
PEER_DK = 256
PEER_TOPK = 16
PEER_BLOCK = 128
POS_BASE = 10000.0

SEGMENTS = (
    ('a_q', H_A * DH_A), ('a_k', H_A * DH_A), ('a_v', H_A * DH_A), ('a_o', H_A * DH_A),
    ('a_i', 2 * H_A), ('a_f', 2 * H_A),
    ('b_q', H_B * DK_B), ('b_f', 2 * H_B * DK_B), ('b_i', H_B * DV_B), ('b_g', H_B * DV_B),
    ('c_q', H_C * DK_C), ('c_k', H_C * DK_C), ('c_v', H_C * DV_C), ('c_g', H_C * DV_C),
    ('c_lr', 2 * R_C),
    ('d_x', H_D * DH_D), ('d_g', H_D * DH_D),
    ('gates', N_BRANCH * D_MODEL),
)
N_IN = sum(width for _, width in SEGMENTS)

kernel_name = 'hybrid_bidir_recurrent_peer_diffusion_step'

def segment_bounds(name):
    start = 0
    for seg, width in SEGMENTS:
        if seg == name:
            return start, start + width
        start += width
    raise KeyError(name)

def split_columns(z):
    cols = {}
    start = 0
    for name, width in SEGMENTS:
        cols[name] = z[..., start:start + width]
        start += width
    return cols

def rmsnorm(x, g):
    xf = x.astype(jnp.float32)
    return xf * lax.rsqrt(jnp.mean(xf * xf, axis=-1, keepdims=True) + EPS) * g.astype(jnp.float32)

def head_rms_norm(h):
    return h * lax.rsqrt(jnp.mean(h * h, axis=-1, keepdims=True) + EPS)

def flip(a):
    return jnp.flip(a, axis=1)

def to_chunks(a):
    bsz, t = a.shape[0], a.shape[1]
    a = a.reshape(bsz, t // CHUNK, CHUNK, *a.shape[2:])
    return jnp.moveaxis(a, (1, 3), (0, 2))

def from_chunks(a):
    a = jnp.moveaxis(a, (0, 2), (1, 3))
    return a.reshape(a.shape[0], a.shape[1] * a.shape[2], *a.shape[3:])

def mlstm_scan(q, k, v, log_i, log_f, C0, n0, m0):
    causal = jnp.tril(jnp.ones((CHUNK, CHUNK), dtype=bool))

    def step(carry, xs):
        C, n, m = carry
        qc, kc, vc, li, lf = xs
        b = jnp.cumsum(lf, axis=-1)
        logw = jnp.where(causal, b[..., :, None] - b[..., None, :] + li[..., None, :], NEG_BIG)
        from_state = b + m[..., None]
        m_t = jnp.maximum(from_state, jnp.max(logw, axis=-1))
        w_state = jnp.exp(from_state - m_t)
        scores = jnp.einsum('bhtd,bhsd->bhts', qc, kc) * jnp.exp(logw - m_t[..., None])
        num = (w_state[..., None] * jnp.einsum('bhtd,bhde->bhte', qc, C)
               + jnp.einsum('bhts,bhse->bhte', scores, vc))
        den = w_state * jnp.einsum('bhtd,bhd->bht', qc, n) + jnp.sum(scores, axis=-1)
        floor = jnp.exp(jnp.minimum(-m_t, MAX_EXP_ARG))
        h = num / jnp.maximum(jnp.abs(den), floor)[..., None]
        m_new = m_t[..., -1]
        w_new = jnp.exp(b[..., -1:] - b + li - m_new[..., None])
        decay = jnp.exp(b[..., -1] + m - m_new)
        C_new = decay[..., None, None] * C + jnp.einsum('bhs,bhsd,bhse->bhde', w_new, kc, vc)
        n_new = decay[..., None] * n + jnp.einsum('bhs,bhsd->bhd', w_new, kc)
        return (C_new, n_new, m_new), h

    xs = tuple(to_chunks(a) for a in (q, k, v, log_i, log_f))
    (C, n, m), h = lax.scan(step, (C0, n0, m0), xs)
    return from_chunks(h), (C, n, m)

def gla_scan(q, k, v, log_a, S0):
    causal = jnp.tril(jnp.ones((CHUNK, CHUNK), dtype=bool))[:, :, None]

    def step(S, xs):
        qc, kc, vc, la = xs
        b = jnp.cumsum(la, axis=2)
        rel = jnp.where(causal, b[:, :, :, None, :] - b[:, :, None, :, :], 0.0)
        decay_ts = jnp.where(causal, jnp.exp(rel), 0.0)
        scores = jnp.einsum('bhtsd,bhsd->bhts', qc[:, :, :, None, :] * decay_ts, kc)
        o = (jnp.einsum('bhtd,bhde->bhte', qc * jnp.exp(b), S)
             + jnp.einsum('bhts,bhse->bhte', scores, vc))
        b_last = b[:, :, -1]
        S_new = (jnp.exp(b_last)[..., None] * S
                 + jnp.einsum('bhsd,bhse->bhde', kc * jnp.exp(b_last[:, :, None] - b), vc))
        return S_new, o

    xs = tuple(to_chunks(a) for a in (q, k, v, log_a))
    S, o = lax.scan(step, S0, xs)
    return from_chunks(o), (S,)

def hgrn_scan(q, v, k, log_f, S0):
    return gla_scan(q, k, v, log_f, S0)

def lru_scan(a, u, h0):
    def combine(left, right):
        a_l, u_l = left
        a_r, u_r = right
        return a_l * a_r, a_r * u_l + u_r
    a_cum, u_cum = lax.associative_scan(combine, (a, u), axis=1)
    h = a_cum * h0[:, None, :] + u_cum
    return h, (h[:, -1],)

def run_bidirectional(scan_fn, shared, per_dir, state):
    out_f, st_f = scan_fn(*shared, *(a[:, :, 0] for a in per_dir), *(s[:, 0] for s in state))
    out_b, st_b = scan_fn(*(flip(a) for a in shared), *(flip(a[:, :, 1]) for a in per_dir),
                          *(s[:, 1] for s in state))
    new_state = tuple(jnp.stack([f, b], axis=1) for f, b in zip(st_f, st_b))
    return out_f + flip(out_b), new_state

def depthwise_conv(x, w, b):
    left = (CONV_W - 1) // 2
    y = lax.conv_general_dilated(x, w.astype(x.dtype)[:, None, :], window_strides=(1,),
                                 padding=[(left, CONV_W - 1 - left)],
                                 dimension_numbers=('NWC', 'WIO', 'NWC'),
                                 feature_group_count=x.shape[-1])
    return y + b.astype(x.dtype)

def grid_position_embedding(rows):
    quarter = D_MODEL // 4
    omega = 1.0 / (POS_BASE ** (jnp.arange(quarter, dtype=jnp.float32) / quarter))
    r, col = jnp.meshgrid(jnp.arange(rows, dtype=jnp.float32),
                          jnp.arange(GRID_W, dtype=jnp.float32), indexing='ij')

    def enc(pos):
        ang = pos.reshape(-1, 1) * omega
        return jnp.concatenate([jnp.sin(ang), jnp.cos(ang)], axis=-1)
    return jnp.concatenate([enc(r), enc(col)], axis=-1)

def token_mixers(h, lp, state):
    bsz, t, _ = h.shape
    p = split_columns((h @ lp['w_in'] + lp['b_in']).astype(jnp.float32))
    C0, n0, m0, Sb0, Sc0, hd0 = state

    qa = p['a_q'].reshape(bsz, t, H_A, DH_A)
    ka = p['a_k'].reshape(bsz, t, H_A, DH_A) * DH_A ** -0.5
    va = p['a_v'].reshape(bsz, t, H_A, DH_A)
    li = p['a_i'].reshape(bsz, t, 2, H_A)
    lf = jax.nn.log_sigmoid(p['a_f'].reshape(bsz, t, 2, H_A))
    ha, st_a = run_bidirectional(mlstm_scan, (qa, ka, va), (li, lf), (C0, n0, m0))
    ya = jax.nn.sigmoid(p['a_o']) * head_rms_norm(ha).reshape(bsz, t, H_A * DH_A)

    lb = lp['hgrn_lb']
    zf = p['b_f'].reshape(bsz, t, 2, H_B * DK_B)
    log_fb = jax.nn.log_sigmoid(zf) + jnp.log1p(lb * jnp.exp(jnp.minimum(-zf, MAX_EXP_ARG)))
    kb = (1.0 - lb) * jax.nn.sigmoid(-zf)
    log_fb = log_fb.reshape(bsz, t, 2, H_B, DK_B)
    kb = kb.reshape(bsz, t, 2, H_B, DK_B)
    qb = p['b_q'].reshape(bsz, t, H_B, DK_B) * DK_B ** -0.5
    vb = p['b_i'].reshape(bsz, t, H_B, DV_B)
    hb, st_b = run_bidirectional(hgrn_scan, (qb, vb), (kb, log_fb), (Sb0,))
    yb = jax.nn.silu(p['b_g']) * head_rms_norm(hb).reshape(bsz, t, H_B * DV_B)

    qc = p['c_q'].reshape(bsz, t, H_C, DK_C) * DK_C ** -0.5
    kc = p['c_k'].reshape(bsz, t, H_C, DK_C)
    vc = p['c_v'].reshape(bsz, t, H_C, DV_C)
    lr = p['c_lr'].reshape(bsz, t, 2, R_C)
    zg = jnp.einsum('btnr,nrk->btnk', lr, lp['gla_up'].astype(jnp.float32)) + lp['gla_up_b']
    gc = (jax.nn.log_sigmoid(zg) / GLA_TAU).reshape(bsz, t, 2, H_C, DK_C)
    hc, st_c = run_bidirectional(gla_scan, (qc, kc, vc), (gc,), (Sc0,))
    yc = jax.nn.silu(p['c_g']) * head_rms_norm(hc).reshape(bsz, t, H_C * DV_C)

    xd = depthwise_conv(p['d_x'], lp['conv_w'], lp['conv_b'])
    xdh = xd.reshape(bsz, t, H_D, DH_D)
    r = jax.nn.sigmoid(jnp.einsum('bthi,nhij->btnhj', xdh, lp['lru_w_a'].astype(jnp.float32))
                       .reshape(bsz, t, 2, H_D * DH_D) + lp['lru_b_a'])
    ig = jax.nn.sigmoid(jnp.einsum('bthi,nhij->btnhj', xdh, lp['lru_w_x'].astype(jnp.float32))
                        .reshape(bsz, t, 2, H_D * DH_D) + lp['lru_b_x'])
    log_a = -LRU_C * r * jax.nn.softplus(-lp['lru_lambda'].astype(jnp.float32))
    a = jnp.exp(log_a)
    u = jnp.sqrt(jnp.maximum(-jnp.expm1(2.0 * log_a), 0.0)) * (ig * xd[:, :, None, :])
    hd, st_d = run_bidirectional(lru_scan, (), (a, u), (hd0,))
    yd = hd * jax.nn.gelu(p['d_g'])

    branches = jnp.stack([ya, yb, yc, yd], axis=0)
    proj = jnp.einsum('nbtw,nwd->nbtd', branches, lp['w_branch'])
    gates = jax.nn.sigmoid(p['gates'].reshape(bsz, t, N_BRANCH, D_MODEL))
    merged = jnp.einsum('btnd,nbtd->btd', gates, proj)
    out = merged @ lp['w_out']
    return out, (*st_a, *st_b, *st_c, *st_d)

def peer_ffn(h, w_q, sub_keys, u, v):
    bsz, t, d = h.shape

    def block(xb):
        q = (xb @ w_q).astype(jnp.float32).reshape(-1, PEER_HEADS, 2, PEER_DK // 2)
        s = jnp.einsum('nhpk,hpek->nhpe', q, sub_keys.astype(jnp.float32))
        s1, i1 = lax.top_k(s[:, :, 0], PEER_TOPK)
        s2, i2 = lax.top_k(s[:, :, 1], PEER_TOPK)
        cand_s = (s1[..., :, None] + s2[..., None, :]).reshape(-1, PEER_HEADS, PEER_TOPK * PEER_TOPK)
        cand_i = (i1[..., :, None] * N_KEYS + i2[..., None, :]).reshape(-1, PEER_HEADS, PEER_TOPK * PEER_TOPK)
        top_s, pos = lax.top_k(cand_s, PEER_TOPK)
        idx = jnp.take_along_axis(cand_i, pos, axis=-1)
        g = jax.nn.softmax(top_s, axis=-1)
        act = jax.nn.gelu(jnp.einsum('nd,nhkd->nhk', xb, u[idx]).astype(jnp.float32)) * g
        return jnp.einsum('nhk,nhkd->nd', act, v[idx])

    y = lax.map(block, h.reshape(-1, PEER_BLOCK, d))
    return y.reshape(bsz, t, d)

def trunk_layer(x, cond, lp, state):
    mod = (jax.nn.silu(cond.astype(jnp.float32)) @ lp['w_mod'] + lp['b_mod'])[:, None, :]
    sh1, sc1, g1, sh2, sc2, g2 = jnp.split(mod, 6, axis=-1)
    h = rmsnorm(x, lp['norm1_g']) * (1.0 + sc1) + sh1
    mix, new_state = token_mixers(h, lp, state)
    x = x + (g1 * mix).astype(x.dtype)
    h = rmsnorm(x, lp['norm2_g']) * (1.0 + sc2) + sh2
    ffn = peer_ffn(h, lp['peer_w_q'], lp['peer_sub_keys'], lp['peer_u'], lp['peer_v'])
    x = x + (g2 * ffn).astype(x.dtype)
    return x, new_state

def setup_inputs(seed: int = 0) -> dict:
    key = jax.random.key(seed)
    ks = jax.random.split(key, 40)
    f32 = jnp.float32
    d = D_MODEL
    w_mix = H_D * DH_D

    def nrm(i, shape, scale):
        return jax.random.normal(ks[i], shape, f32) * scale

    f0, f1 = segment_bounds('a_f')
    b_in = nrm(16, (DEPTH, N_IN), 0.02).at[:, f0:f1].add(MLSTM_F_BIAS)
    a0 = jax.random.uniform(ks[26], (DEPTH, 2, w_mix), f32, 0.9, 0.999) ** (1.0 / LRU_C)
    lru_lambda = jnp.log(a0) - jnp.log1p(-a0)
    return {
        'x_prompt': nrm(0, (BATCH, SEQ, d), 1.0),
        'x_sample': nrm(1, (DEC_BATCH, DEC_SEQ, d), 1.0),
        'state_mlstm_C': nrm(2, (DEC_BATCH, DEPTH, 2, H_A, DH_A, DH_A), 0.5),
        'state_mlstm_n': nrm(3, (DEC_BATCH, DEPTH, 2, H_A, DH_A), 0.5),
        'state_mlstm_m': nrm(4, (DEC_BATCH, DEPTH, 2, H_A), 1.0),
        'state_hgrn_S': nrm(5, (DEC_BATCH, DEPTH, 2, H_B, DK_B, DV_B), 0.5),
        'state_gla_S': nrm(6, (DEC_BATCH, DEPTH, 2, H_C, DK_C, DV_C), 1.0),
        'state_lru_h': nrm(7, (DEC_BATCH, DEPTH, 2, w_mix), 0.5),
        'c': nrm(8, (DEC_BATCH, d), 1.0),
        'c_ctx': nrm(9, (d,), 1.0),
        'norm1_g': 1.0 + nrm(10, (DEPTH, d), 0.02),
        'norm2_g': 1.0 + nrm(11, (DEPTH, d), 0.02),
        'final_norm_g': 1.0 + nrm(12, (d,), 0.02),
        'w_mod': nrm(13, (DEPTH, d, 6 * d), 0.5 * d ** -0.5),
        'b_mod': nrm(14, (DEPTH, 6 * d), 0.02),
        'w_in': nrm(15, (DEPTH, d, N_IN), d ** -0.5),
        'b_in': b_in,
        'w_gla_up': nrm(17, (DEPTH, 2, R_C, H_C * DK_C), R_C ** -0.5),
        'b_gla_up': nrm(18, (DEPTH, 2, H_C * DK_C), 0.02),
        'hgrn_lower_bounds': nrm(19, (DEPTH, 2, H_B * DK_B), 0.1),
        'conv_w': nrm(20, (DEPTH, CONV_W, w_mix), CONV_W ** -0.5),
        'conv_b': nrm(21, (DEPTH, w_mix), 0.02),
        'lru_w_a': nrm(22, (DEPTH, 2, H_D, DH_D, DH_D), DH_D ** -0.5),
        'lru_b_a': nrm(23, (DEPTH, 2, w_mix), 0.02),
        'lru_w_x': nrm(24, (DEPTH, 2, H_D, DH_D, DH_D), DH_D ** -0.5),
        'lru_b_x': nrm(25, (DEPTH, 2, w_mix), 0.02),
        'lru_lambda': lru_lambda,
        'w_branch': nrm(27, (DEPTH, N_BRANCH, MIX_W, d), MIX_W ** -0.5),
        'w_out': nrm(28, (DEPTH, d, d), d ** -0.5),
        'peer_w_q': nrm(29, (DEPTH, d, PEER_HEADS * PEER_DK), d ** -0.5),
        'peer_sub_keys': nrm(30, (DEPTH, PEER_HEADS, 2, N_KEYS, PEER_DK // 2), (PEER_DK // 2) ** -0.5),
        'peer_u': nrm(31, (DEPTH, N_EXPERTS, d), d ** -0.5),
        'peer_v': nrm(32, (DEPTH, N_EXPERTS, d), PEER_HEADS ** -0.5),
    }

def reference(x_prompt, x_sample, state_mlstm_C, state_mlstm_n, state_mlstm_m, state_hgrn_S,
              state_gla_S, state_lru_h, c, c_ctx, norm1_g, norm2_g, final_norm_g, w_mod, b_mod,
              w_in, b_in, w_gla_up, b_gla_up, hgrn_lower_bounds, conv_w, conv_b, lru_w_a, lru_b_a,
              lru_w_x, lru_b_x, lru_lambda, w_branch, w_out, peer_w_q, peer_sub_keys, peer_u, peer_v):
    f32 = jnp.float32
    lb_soft = jax.nn.softmax(hgrn_lower_bounds.astype(f32), axis=0)
    lb_all = jnp.cumsum(lb_soft, axis=0) - lb_soft[0:1]

    def layer_params(l):
        return {
            'norm1_g': norm1_g[l], 'norm2_g': norm2_g[l], 'w_mod': w_mod[l], 'b_mod': b_mod[l],
            'w_in': w_in[l], 'b_in': b_in[l], 'gla_up': w_gla_up[l], 'gla_up_b': b_gla_up[l],
            'hgrn_lb': lb_all[l], 'conv_w': conv_w[l], 'conv_b': conv_b[l],
            'lru_w_a': lru_w_a[l], 'lru_b_a': lru_b_a[l], 'lru_w_x': lru_w_x[l],
            'lru_b_x': lru_b_x[l], 'lru_lambda': lru_lambda[l], 'w_branch': w_branch[l],
            'w_out': w_out[l], 'peer_w_q': peer_w_q[l], 'peer_sub_keys': peer_sub_keys[l],
            'peer_u': peer_u[l], 'peer_v': peer_v[l],
        }

    bp = x_prompt.shape[0]
    w_mix = H_D * DH_D
    zero_state = (
        jnp.zeros((bp, 2, H_A, DH_A, DH_A), f32), jnp.zeros((bp, 2, H_A, DH_A), f32),
        jnp.zeros((bp, 2, H_A), f32), jnp.zeros((bp, 2, H_B, DK_B, DV_B), f32),
        jnp.zeros((bp, 2, H_C, DK_C, DV_C), f32), jnp.zeros((bp, 2, w_mix), f32),
    )
    x = x_prompt
    ctx_states = []
    for l in range(DEPTH):
        x, st = trunk_layer(x, c_ctx[None, :], layer_params(l), zero_state)
        ctx_states.append(st)
    y_prompt = rmsnorm(x, final_norm_g)
    new_mlstm_C = jnp.stack([s[0] for s in ctx_states], axis=1)
    new_mlstm_n = jnp.stack([s[1] for s in ctx_states], axis=1)
    new_mlstm_m = jnp.stack([s[2] for s in ctx_states], axis=1)
    new_hgrn_S = jnp.stack([s[3] for s in ctx_states], axis=1)
    new_gla_S = jnp.stack([s[4] for s in ctx_states], axis=1)
    new_lru_h = jnp.stack([s[5] for s in ctx_states], axis=1)

    rows = x_sample.shape[1] // GRID_W
    x = x_sample + grid_position_embedding(rows).astype(x_sample.dtype)[None]
    for l in range(DEPTH):
        cached = (state_mlstm_C[:, l].astype(f32), state_mlstm_n[:, l].astype(f32),
                  state_mlstm_m[:, l].astype(f32), state_hgrn_S[:, l].astype(f32),
                  state_gla_S[:, l].astype(f32), state_lru_h[:, l].astype(f32))
        x, _ = trunk_layer(x, c, layer_params(l), cached)
    y_sample = rmsnorm(x, final_norm_g)
    return (y_prompt, y_sample, new_mlstm_C, new_mlstm_n, new_mlstm_m, new_hgrn_S, new_gla_S, new_lru_h)


_drawn_inputs = setup_inputs


def setup_inputs(seed=0):
    import zlib

    import numpy as np

    out = dict(_drawn_inputs(seed))
    spreads = {}
    factors = {'state_mlstm_C': 5.952,
     'state_mlstm_n': 8.0,
     'state_mlstm_m': 8.0,
     'state_hgrn_S': 8.0,
     'state_gla_S': 8.0,
     'state_lru_h': 3.171,
     'norm2_g': 7.059,
     'final_norm_g': 2.882,
     'b_gla_up': 6.353,
     'lru_b_a': 8.0,
     'lru_b_x': 6.887}
    for name, (base, spread) in spreads.items():
        noise = np.random.default_rng([zlib.crc32(name.encode()), seed]).standard_normal(out[name].shape)
        drawn = base * np.exp(spread * noise) if base else spread * noise
        out[name] = jnp.asarray(drawn.astype(out[name].dtype))
    for name, factor in factors.items():
        out[name] = (out[name] * factor).astype(out[name].dtype)
    return out
```

```python
from contextlib import ExitStack

import numpy as np
import concourse.bass as bass
from concourse import mybir

F32 = mybir.dt.float32
U32 = mybir.dt.uint32
U8 = mybir.dt.uint8
ALU = mybir.AluOpType
ACT = mybir.ActivationFunctionType
AX = mybir.AxisListType

P = 128
D = 1024
KD = D // P
TS, TP = 512, 128
TOK = TS + TP
NT = TOK // P
W = 512
HEADS = 4
HALF = TOK // 2
EPS = 1e-6
LEVELS = [64, 32, 16, 8, 4, 2, 1]
GRID_W = 64
NBR = 4
PH = 8
TOPK = 16
NKEY = 128
RING = 4
SLAB = KD * 256

SEG = (('a_q', 512), ('a_k', 512), ('a_v', 512), ('a_o', 512), ('a_i', 8), ('a_f', 8), ('b_q', 512), ('b_f', 1024),
       ('b_i', 512), ('b_g', 512), ('c_q', 256), ('c_k', 256), ('c_v', 512), ('c_g', 512), ('c_lr', 32),
       ('d_x', 512), ('d_g', 512), ('gates', 4096))
COL = {}
_at = 0
for _n, _w in SEG:
    COL[_n] = (_at, _at + _w)
    _at += _w

SLABS = {}
_at = 0
for _n, _c in (('mod', 24), ('a_q', 2), ('a_k', 2), ('a_v', 2), ('a_o', 2), ('b_q', 2), ('b_i', 2), ('b_g', 2),
               ('b_f', 4), ('c_q', 1), ('c_k', 1), ('c_v', 2), ('c_g', 2), ('d_x', 2), ('d_g', 2),
               ('merge', 24), ('w_out', 4), ('w_q', 8)):
    SLABS[_n] = _at
    _at += _c
NSLAB = _at

VEC = {}
_at = 0
for _n, _c in (('b_mod', 48), ('norm1', 8), ('norm2', 8), ('normf', 8), ('a_q', 4), ('a_k', 4), ('a_o', 4),
               ('b_q', 4), ('b_f', 8), ('b_g', 4), ('c_q', 2), ('c_k', 2), ('c_g', 4), ('d_x', 4), ('d_g', 4),
               ('gates', 32), ('b_up', 4), ('lb', 8), ('conv_w', 16), ('conv_b', 4), ('lru_b_a', 8),
               ('lru_b_x', 8), ('lam', 8), ('h0', 8), ('n0', 8), ('cond', 16), ('pos_r', 32), ('pos_c', 256)):
    VEC[_n] = (_at, _at + _c)
    _at += _c
NVEC = _at

CST = {}
_at = 0
for _n, _c in (('ident', 128), ('ones', 128), ('iota', 128), ('over0', 128), ('over1', 128), ('reset0', 640),
               ('reset1', 640), ('sel', 512), ('jota', 16), ('epsD', 1), ('epsP', 1)):
    CST[_n] = (_at, _at + _c)
    _at += _c
NCST = _at


def mod_of(ntile, j):
    return ntile * KD + j


def build_kernel(nc, x_in, slabs, vec_in, cst_in, lvl_in, wsm_in, rowv_in, up_in, tokb_in, c0_in, s0b_in, s0c_in,
                 lruw_in, sk_in, u_in, v_in, y_out, c_out, n_out, m_out, sb_out, sc_out, h_out, gmap):
    with ExitStack() as ctx:
        def sem(name):
            return ctx.enter_context(nc.semaphore(name))

        def sb(name, shape, dt=F32):
            return ctx.enter_context(nc.sbuf_tensor(name, shape, dt))

        ps = ctx.enter_context(nc.psum_tensor("ps", [P, 8, 512], F32))

        x = sb("x", [P, KD, TOK])
        h = sb("h", [P, KD, TOK])
        ybr = sb("ybr", [P, NBR, HEADS, TOK])
        wring = sb("wring", [P, RING, SLAB])
        vec = sb("vec", [P, NVEC])
        cst = sb("cst", [P, NCST])
        lvl = sb("lvl", [P, 2, len(LEVELS), P], U8)
        modv = sb("modv", [P, 48, 2])
        cs = sb("cs", [P, KD, 2])
        amul = sb("amul", [P, KD, 2])
        small = sb("small", [P, 64])
        scr = sb("scr", [P, 128])
        work = sb("work", [P, 20750])

        def V(name, j=0, n=1):
            return vec[:, VEC[name][0] + j:VEC[name][0] + j + n]

        def C(name):
            return cst[:, CST[name][0]:CST[name][1]]

        ident, ones = C('ident'), C('ones')
        cepsD, cepsP = C('epsD'), C('epsP')

        class Carve:
            def __init__(self, base, size):
                self.base, self.at, self.size = base, 0, size

            def take(self, n, part=P):
                a = self.base[0:part, self.at:self.at + n]
                self.at += n
                assert self.at <= self.size, self.at
                return a

        y2 = ybr[:].rearrange("p n h t -> p n (h t)")

        def gl_memory(J):
            lo = Carve(work, 5760)
            hi = Carve(work[:, 6152:], 20750 - 6152)
            m = {'J': J, 'X': [lo.take(J * TOK) for _ in range(2)], 'dec': work[:, 5120:5120 + J * NT]}
            m['q'] = hi.take(J * TOK)
            m['k'] = hi.take(J * TOK)
            m['b'] = hi.take(J * TOK)
            m['P'] = hi.take(NT * W).rearrange("p (n c) -> p n c", n=NT)
            m['v'] = hi.take(NT * W).rearrange("p (n c) -> p n c", n=NT)
            m['kT'] = [hi.take(J * P) for _ in range(2)]
            m['hi'] = hi
            src = Carve(y2[:, 2, :], 2560) if J == 4 else hi
            m['S'] = src.take(2 * J * P).rearrange("p (d j e) -> p d j e", d=2, j=J)
            m['Snew'] = src.take(2 * J * P).rearrange("p (d j e) -> p d j e", d=2, j=J)
            m['vb'] = src.take(512)
            m['o'] = y2[:, 3, :].rearrange("p (h t) -> p h t", h=4)
            return m

        mB, mC = gl_memory(4), gl_memory(2)
        c_lr = mC['hi'].take(2 * TOK, 16).rearrange("p (d t) -> p d t", d=2)
        c_up = mC['hi'].take(512, 16).rearrange("p (d c) -> p d c", d=2)
        lbw = work[:, 5200:5232]

        def rows(J, hh):
            return (hh, slice(0, P)) if J == 4 else (hh // 2, slice((hh % 2) * 64, (hh % 2) * 64 + 64))

        def place(J, hh):
            return hh if J == 4 else (hh % 2) * 2 + hh // 2

        def head_out(J, g, hh):
            if J == 4:
                return ps[:, 2 * g[0], hh * P:(hh + 1) * P]
            return ps[:, 2 * g[0] + hh % 2, (hh // 2) * P:(hh // 2 + 1) * P]

        def heads_psum(J, g):
            if J == 4:
                return ps[:, 2 * g[0], :].rearrange("p (h t) -> p h t", t=P)
            return ps[:, 2 * g[0]:2 * g[0] + 2, 0:2 * P].rearrange("p a (j t) -> p a j t", t=P)

        def heads_row(J, ap):
            return ap.rearrange("p (h t) -> p h t", t=P) if J == 4 else ap.rearrange("p (a j t) -> p a j t", t=P, a=2)

        def heads_same(J, ap):
            if J == 4:
                return ap.unsqueeze(1).to_broadcast([P, 4, P])
            return ap.unsqueeze(1).unsqueeze(1).to_broadcast([P, 2, 2, P])

        def tiles_of(d):
            return ([0, 1, 2, 3] if d == 0 else [3, 2, 1, 0]) + [4]

        dk = Carve(work, 20750)
        d_x, d_xd, d_R, d_U, d_T, d_Q, d_H = (dk.take(2560).rearrange("p (h t) -> p h t", h=4) for _ in range(7))
        d_w = dk.take(2048).rearrange("p (w d h j) -> p w d h j", w=2, d=2, h=4)
        d_new = dk.take(8)
        d_spl = dk.take(8)
        d_tmp = dk.take(8)
        d_nspl = dk.take(8)

        mrg = work[:, 6152:11272].rearrange("p (k t) -> p k t", k=KD)
        m_sg = work[:, 11272:12552].rearrange("p (r t) -> p r t", r=2)
        m_tmp = work[:, 12552:13192]

        r_sk = work[:, 13192:15240].rearrange("p (g e) -> p g e", g=16)
        r_qT = work[:, 15240:16520].rearrange("p (r t) -> p r t", r=2)
        r_s = ybr[:].rearrange("p n h t -> p (n h t)").rearrange("p (n g e) -> p n g e", n=NT, g=16)
        rk = Carve(wring[:].rearrange("p r c -> p (r c)"), RING * SLAB)
        r_v = rk.take(256).rearrange("p (g k) -> p g k", g=16)
        r_i = rk.take(256).bitcast(U32).rearrange("p (g k) -> p g k", g=16)
        r_if = rk.take(256).rearrange("p (g k) -> p g k", g=16)
        r_s2 = rk.take(256)
        r_c = rk.take(2048).rearrange("p (h c) -> p h c", h=PH)
        r_t = rk.take(128).rearrange("p (h k) -> p h k", h=PH)
        r_p = rk.take(128).bitcast(U32).rearrange("p (h k) -> p h k", h=PH)
        r_ab = rk.take(256).bitcast(U32).rearrange("p (w c) -> p w c", w=2)
        r_abf = rk.take(256).rearrange("p (w c) -> p w c", w=2)
        r_e = rk.take(384).rearrange("p (w c) -> p w c", w=3)
        r_sum = rk.take(16)
        r_T = rk.take(768).rearrange("p (r w c) -> p r w c", r=2, w=3)
        NOH = 8
        r_L = rk.take(NOH * P).rearrange("p (r c) -> p r c", r=NOH)
        r_R = rk.take(NOH * P).rearrange("p (r c) -> p r c", r=NOH)
        g_stage = work[:, 0:16384].rearrange("p (r e n) -> p r e n", r=2, e=P)
        g_one = r_c.rearrange("p h c -> p (h c)")

        NB = NKEY // 4
        p_u = work[:, 0:8192].rearrange("p (r c k e) -> p r c k e", r=2, c=4, k=KD)
        p_g = work[:, 8192:13312].rearrange("p (r q c n) -> p r q c n", r=2, q=2 * NT, c=4)
        p_a = work[:, 13312:18432].rearrange("p (r c t) -> p r c t", r=2, c=4)
        p_t = work[:, 18432:19712].rearrange("p (r t) -> p r t", r=2)
        p_v = wring[:].rearrange("p r c -> p (r c)").rearrange("p (r c d) -> p r c d", r=2, c=4)

        marks = [0]

        def mark():
            marks[0] += 1
            return nc.vector.memset(scr[:, marks[0] - 1:marks[0]], 0.0)

        full = [sem(f"psum_full{i}") for i in range(4)]
        free = [sem(f"psum_free{i}") for i in range(4)]
        slab_in = [sem(f"slab_in{i}") for i in range(RING)]
        load = sem("loaded")
        load_x = sem("loaded_x")
        phase_v, phase_a = sem("phase_vector"), sem("phase_scalar")
        vch, ach = sem("vector_chain"), sem("scalar_chain")
        silu_done = sem("cond_silu_done")
        x_ready = sem("x_ready")
        sq_done = sem("squares_done")
        hm_done = sem("h_scaled")
        h_done = sem("h_ready")
        stored = sem("stored")
        phload = sem("phase_loads")
        names = {}

        def S(name):
            if name not in names:
                names[name] = sem(name)
            return names[name]

        class Slots:
            def __init__(self):
                self.n, self.r = [0] * 4, 0

            def next(self, among=(0, 1, 2, 3)):
                s = among[self.r % len(among)]
                self.r += 1
                self.n[s] += 1
                return s, self.n[s]

        def halves(slot):
            return ps[:, 2 * slot:2 * slot + 2, 0:HALF]

        def two(ap):
            return ap.rearrange("p (a b) -> p a b", a=2)

        def bank(slot):
            return ps[:, 2 * slot, :]

        def bank2(slot):
            return ps[:, 2 * slot + 1, :]

        slab_last = {}

        def slab(i):
            return wring[:, i % RING, :].rearrange("p (k c) -> p k c", k=KD)

        lvl_f = ybr[:, 0].rearrange("p h t -> p (h t)")[:, 0:2 * len(LEVELS) * P]\
            .rearrange("p (d l t) -> p d l t", d=2, l=len(LEVELS))

        wk = Carve(work, 20750)
        sq = wk.take(5120).rearrange("p (k t) -> p k t", k=KD)
        rstd = wk.take(TOK)
        wsm = wk.take(KD * 48).rearrange("p (k c) -> p k c", k=KD)

        wk = Carve(work, 20750)
        wk.take(5120 + TOK)
        wk.take(KD * 48)
        rowv = wk.take(8, 16)
        a_q = wk.take(2560).rearrange("p (h t) -> p h t", h=4)
        a_k = wk.take(2560).rearrange("p (h t) -> p h t", h=4)
        a_v = wk.take(2560).rearrange("p (n c) -> p n c", n=NT)
        a_C0 = wk.take(1024).rearrange("p (d h e) -> p d h e", d=2, h=4)
        a_kT = wk.take(512)
        a_gc = wk.take(40).rearrange("p (d n h) -> p d n h", d=2, n=NT)
        a_st = wk.take(8 * 129).rearrange("p (g e) -> p g e", g=8)
        a_E = wk.take(1280).rearrange("p (r t) -> p r t", r=2)
        a_P = wk.take(1280).rearrange("p (r t) -> p r t", r=2)
        a_o = y2[:, 0, :].rearrange("p (h t) -> p h t", h=4)
        a_ha = y2[:, 1, :].rearrange("p (h t) -> p h t", h=4)
        yk = Carve(y2[:, 2, :], 2560)
        a_rI = yk.take(1280, 4).rearrange("p (d t) -> p d t", d=2)
        a_rF = yk.take(1280, 4).rearrange("p (d t) -> p d t", d=2)
        wk2 = Carve(work, 5120)
        a_rG = wk2.take(1280, 4).rearrange("p (d t) -> p d t", d=2)
        a_rM = wk2.take(1280, 4).rearrange("p (d t) -> p d t", d=2)
        a_rFl = wk2.take(1280, 4).rearrange("p (d t) -> p d t", d=2)
        a_rW = wk2.take(1280, 4).rearrange("p (d t) -> p d t", d=2)
        yk = Carve(y2[:, 3, :], 2560)
        a_Mb = yk.take(640)
        a_Fb = yk.take(640)
        a_D = yk.take(640)
        a_qt = yk.take(512)
        a_n0 = yk.take(128)
        wk3 = Carve(work[:, 5120:5760], 640)
        a_dm = wk3.take(256).rearrange("p (r t) -> p r t", r=2)
        a_kw = wk3.take(128)
        a_vb = wk.take(512)
        a_T = wk.take(640)

        def a_range(d, i):
            if i == 4:
                return TS, TOK
            return (i * P, TS) if d == 0 else (0, (i + 1) * P)

        num, den = 2, 3

        def head_roots(sl, got):
            for hh in range(HEADS):
                g = sl.next((0, 1))
                got(g)
                nc.scalar.activation(two(sq[:, 4 + hh, :]), halves(g[0]), ACT.Sqrt, bias=cepsP)\
                    .then_inc(free[g[0]], 1)

        def head_norm(dve, link, g, val, gate, r, t):
            vv = nc.vector
            dve.wait_ge(free[g[0]], g[1])
            link(vv.reciprocal(r, r))
            link(vv.scalar_tensor_tensor(out=t, in0=r, scalar=P ** 0.5, in1=val, op0=ALU.mult, op1=ALU.mult))
            link(vv.tensor_tensor(gate, gate, t, ALU.mult))

        STORES = [0]
        LOADS = {'B': 4, 'C': 7, 'D': 8, 'sk': 9}
        map_slots = {'T': [], 'q': []}
        u_sem, v_sem, g_sem = ([sem(f'{n}_in{i}') for i in range(2)] for n in ('expert_u', 'expert_v', 'map'))
        map_out = [sem(f'map_out{i}') for i in range(2)]
        block = ctx.enter_context(nc.Block())

        def phase(eng, k):
            eng.wait_ge(phase_v, k)
            eng.wait_ge(phase_a, k)

        @block.tensor
        def _(pe):
            sl = Slots()

            def slab_wait(i):
                pe.wait_ge(slab_in[i % RING], 16 * (i // RING + 1))

            def claim(g):
                if g[1] > 1:
                    pe.wait_ge(free[g[0]], g[1] - 1)

            def wide(g, pairs, m=P):
                claim(g)
                for a in range(2):
                    for i, (lhs, rhs) in enumerate(pairs):
                        mm = nc.tensor.matmul(ps[0:m, 2 * g[0] + a, 0:HALF], lhs, rhs[:, a * HALF:(a + 1) * HALF],
                                              start=(i == 0), stop=(i == len(pairs) - 1))
                mm.then_inc(full[g[0]], 1)

            def project(name, base=0, n=None):
                for c in range(n):
                    i = SLABS[name] + (base + c) // 2
                    slab_wait(i)
                    w = slab(i)
                    o = ((base + c) % 2) * P
                    g = sl.next()
                    wide(g, [(w[:, k, o:o + P], h[:, k, :]) for k in range(KD)])
                    slab_last[i] = g

            def project_tok(name):
                for c in range(2):
                    i = SLABS[name] + c
                    slab_wait(i)
                    for t in range(NT):
                        g = sl.next()
                        claim(g)
                        for k in range(KD):
                            mm = nc.tensor.matmul(bank(g[0])[:, 0:256], h[:, k, t * P:(t + 1) * P], slab(i)[:, k, :],
                                                  start=(k == 0), stop=(k == KD - 1))
                        mm.then_inc(full[g[0]], 1)
                        slab_last[i] = g

            def norm_sum(base):
                g = sl.next()
                claim(g)
                for k in range(KD):
                    pe.wait_ge(sq_done, base + k + 1)
                    for a in range(2):
                        mm = nc.tensor.matmul(ps[:, 2 * g[0] + a, 0:HALF], ones, sq[:, k, a * HALF:(a + 1) * HALF],
                                              start=(k == 0), stop=(k == KD - 1))
                mm.then_inc(full[g[0]], 1)

            pe.wait_ge(load, 16 * 5)
            pe.wait_ge(silu_done, 1)
            g = sl.next()
            for c in range(48):
                i = SLABS['mod'] + c // 2
                slab_wait(i)
                for k in range(KD):
                    mm = nc.tensor.matmul(bank(g[0])[:, 2 * c:2 * c + 2], slab(i)[:, k, (c % 2) * P:(c % 2) * P + P],
                                          cs[:, k, :], start=(k == 0), stop=(k == KD - 1))
                if c % 2 and c < 47:
                    mm.then_inc(S("mod_slab_used"), 1)
            mm.then_inc(full[g[0]], 1)
            slab_last[23] = g
            norm_sum(0)
            pe.wait_ge(h_done, 16)

            project('a_q', 0, 4)
            project('a_k', 0, 4)
            project_tok('a_v')
            project('a_o', 0, 4)
            for d in range(2):
                for which in range(2):
                    g = sl.next()
                    o = which * 8 + d * 4
                    wide(g, [(wsm[:, k, o:o + 4], h[:, k, :]) for k in range(KD)], m=4)
            g = sl.next()
            claim(g)
            pe.wait_ge(S("a_k_ready"), 4)
            for hh in range(4):
                mm = nc.tensor.transpose(bank(g[0])[:, hh * P:(hh + 1) * P], a_k[:, hh, TS:TOK], ident)
            mm.then_inc(full[g[0]], 1)
            g = sl.next()
            claim(g)
            pe.wait_ge(S("a_rows_g"), 1)
            for d in range(2):
                for t in range(NT):
                    o = (d * NT + t) * 4
                    mm = nc.tensor.matmul(bank(g[0])[:, o:o + 4], a_rG[:, d, t * P:(t + 1) * P], ident[0:4, 0:4],
                                          start=True, stop=True)
            mm.then_inc(full[g[0]], 1)
            pe.wait_ge(S("a_rows_w"), 1)
            pe.wait_ge(S("a_v_ready"), 2 * NT)
            pe.wait_ge(S("a_q_ready"), 4)
            for s in (2, 3):
                pe.wait_ge(free[s], sl.n[s])
            sl.r = 0
            num, den = 2, 3
            for d in range(2):
                for hh in range(4):
                    n = d * 4 + hh
                    sel = cst[0:4, CST['sel'][0] + hh * P:CST['sel'][0] + (hh + 1) * P]
                    g = sl.next((0, 1))
                    claim(g)
                    nc.tensor.matmul(bank(g[0]), sel, a_rW[:, d, 0:TS], start=True, stop=True).then_inc(full[g[0]], 1)
                    for r in (a_rM, a_rFl):
                        g = sl.next((0, 1))
                        wide(g, [(sel, r[:, d, :])])
                    if n:
                        pe.wait_ge(S("a_nd_read"), n)
                    pe.wait_ge(S("a_qt_ready"), n + 1)
                    pe.wait_ge(S("a_n0_ready"), n + 1)
                    nc.tensor.matmul(bank(num), a_C0[:, d, hh, :], a_qt, start=True, stop=False)
                    nc.tensor.matmul(bank(den), a_n0, a_qt, start=True, stop=False).then_inc(S("a_state_used"), 1)
                    order = ([0, 1, 2, 3] if d == 0 else [3, 2, 1, 0]) + [4]

                    def pv(idx, gs):
                        i = order[idx]
                        lo, hi = a_range(d, i)
                        pe.wait_ge(free[gs[0]], gs[1])
                        it = n * 5 + idx
                        po = a_P[:, it % 2, lo:hi]
                        if i < 4:
                            onum, oden = bank(num)[:, lo:hi], bank(den)[:, lo:hi]
                        else:
                            onum, oden = bank2(num)[:, 0:P], bank2(den)[:, 0:P]
                        nc.tensor.matmul(onum, a_v[:, i, hh * P:(hh + 1) * P], po, start=(i == 4), stop=(idx >= 3))
                        nc.tensor.matmul(oden, ones, po, start=(i == 4), stop=(idx >= 3)).then_inc(S("a_pv"), 1)

                    prev = None
                    for idx, i in enumerate(order):
                        lo, hi = a_range(d, i)
                        g = sl.next((0, 1))
                        claim(g)
                        nc.tensor.matmul(bank(g[0])[:, 0:hi - lo], a_k[:, hh, i * P:(i + 1) * P], a_q[:, hh, lo:hi],
                                         start=True, stop=True).then_inc(full[g[0]], 1)
                        if prev is not None:
                            pv(idx - 1, prev)
                        prev = g
                    pv(4, prev)
                    g = sl.next((0, 1))
                    claim(g)
                    pe.wait_ge(S("a_kw_ready"), n + 1)
                    nc.tensor.matmul(bank(g[0])[:, 0:P], a_kw, a_v[:, 4, hh * P:(hh + 1) * P], start=True, stop=True)
                    nc.tensor.matmul(bank(g[0])[:, P:P + 1], a_kw, ones[:, 0:1], start=True, stop=True)\
                        .then_inc(full[g[0]], 1)
            for hh in range(4):
                pe.wait_ge(S("a_sq"), hh + 1)
                g = sl.next((0, 1))
                wide(g, [(ones, sq[:, hh, :])])
            phase(pe, 1)

            def gl_core(m, n):
                J, d = m['J'], n % 2
                t_ = lambda ap, j, t: ap[:, j * TOK + t * P:j * TOK + (t + 1) * P]
                pe.wait_ge(S("g_in"), n + 1)
                for t in range(NT):
                    g = sl.next()
                    claim(g)
                    for hh in range(HEADS):
                        j, r = rows(J, hh)
                        mm = nc.tensor.matmul(head_out(J, g, hh), t_(m['k'], j, t)[r],
                                              t_(m['q'], j, t)[r], start=True, stop=True)
                    mm.then_inc(full[g[0]], 1)
                for li in range(len(LEVELS)):
                    pe.wait_ge(S("g_X"), n * 9 + li + 1)
                    for t in range(NT):
                        g = sl.next()
                        claim(g)
                        for hh in range(HEADS):
                            j, r = rows(J, hh)
                            xt = t_(m['X'][li % 2], j, t)[r]
                            mm = nc.tensor.matmul(head_out(J, g, hh), xt, xt, start=True, stop=True)
                        mm.then_inc(full[g[0]], 1)
                glast = g
                pe.wait_ge(S("g_X"), n * 9 + 9)
                pe.wait_ge(free[glast[0]], glast[1])
                for idx, t in enumerate(tiles_of(d)):
                    gt = sl.next()
                    claim(gt)
                    for j in range(J):
                        mm = nc.tensor.transpose(bank(gt[0])[:, j * P:(j + 1) * P], t_(m['X'][0], j, t), ident)
                    mm.then_inc(full[gt[0]], 1)
                    g = sl.next()
                    claim(g)
                    if 0 < idx < 4:
                        pe.wait_ge(free[gk[0]], gk[1])
                    for hh in range(HEADS):
                        j, r = rows(J, hh)
                        mm = nc.tensor.matmul(head_out(J, g, hh), m['v'][:, t, hh * P:(hh + 1) * P],
                                              m['P'][:, t, place(J, hh) * P:(place(J, hh) + 1) * P], start=True, stop=(t == 4))
                        if t < 4:
                            mm = nc.tensor.matmul(head_out(J, g, hh), m['S'][r, d, j, :],
                                                  t_(m['X'][1], j, t)[r], start=False, stop=True)
                    mm.then_inc(full[g[0]], 1)
                    if idx != 3:
                        gk = sl.next()
                        claim(gk)
                        pe.wait_ge(free[gt[0]], gt[1])
                        for hh in range(HEADS):
                            j, r = rows(J, hh)
                            mm = nc.tensor.matmul(bank(gk[0])[:, hh * P:(hh + 1) * P],
                                                  m['kT'][idx % 2][:, j * P:(j + 1) * P],
                                                  m['v'][:, t, hh * P:(hh + 1) * P], start=True, stop=True)
                        mm.then_inc(full[gk[0]], 1)

            sl.r = 0
            project('b_q', 0, 4)
            project_tok('b_i')
            project('b_g', 0, 4)
            for d in range(2):
                project('b_f', 4 * d, 4)
                gl_core(mB, d)
            for hh in range(HEADS):
                pe.wait_ge(S("g_sq"), hh + 1)
                wide(sl.next((0, 1)), [(ones, sq[:, hh, :])])
            phase(pe, 2)
            sl.r = 0
            project('c_q', 0, 2)
            project('c_k', 0, 2)
            project_tok('c_v')
            project('c_g', 0, 4)
            for d in range(2):
                wide(sl.next(), [(wsm[:, k, 16 + 16 * d:32 + 16 * d], h[:, k, :]) for k in range(KD)], m=16)
            for d in range(2):
                pe.wait_ge(S("c_lr"), 1)
                for j in range(2):
                    wide(sl.next(), [(c_up[:, d, j * P:(j + 1) * P], c_lr[:, d, :])])
                gl_core(mC, 2 + d)
            for hh in range(HEADS):
                pe.wait_ge(S("g_sq"), 4 + hh + 1)
                wide(sl.next((0, 1)), [(ones, sq[:, hh, :])])
            phase(pe, 3)
            sl.r = 0
            project('d_x', 0, 4)
            project('d_g', 0, 4)
            pe.wait_ge(S("d_conv"), 1)
            for d in range(2):
                for hh in range(HEADS):
                    for w in range(2):
                        wide(sl.next(), [(d_w[:, w, d, hh, :], d_xd[:, hh, :])])
            phase(pe, 4)
            sl.r = 0
            for j in range(KD):
                s0 = SLABS['merge'] + 3 * j
                wb = wring[:, (s0 + 2) % RING, :].rearrange("p (k c) -> p k c", k=16)
                for n in range(NBR):
                    slab_wait(s0 + n // 2)
                    wg = slab(s0 + n // 2)
                    o = (n % 2) * P
                    g = sl.next()
                    wide(g, [(wg[:, k, o:o + P], h[:, k, :]) for k in range(KD)])
                    slab_last[s0 + n // 2] = g
                    slab_wait(s0 + 2)
                    g = sl.next()
                    wide(g, [(wb[:, 4 * n + k, :], ybr[:, n, k, :]) for k in range(HEADS)])
                    slab_last[s0 + 2] = g

            def wide2(g, pairs):
                claim(g)
                for o, lo, hi in ((bank(g[0]), 0, TS), (bank2(g[0])[:, 0:TP], TS, TOK)):
                    for i, (lhs, rhs) in enumerate(pairs):
                        mm = nc.tensor.matmul(o, lhs, rhs[:, lo:hi], start=(i == 0), stop=(i == len(pairs) - 1))
                mm.then_inc(full[g[0]], 1)

            for j in range(KD):
                i = SLABS['w_out'] + j // 2
                slab_wait(i)
                g = sl.next()
                pe.wait_ge(S("m_done"), 8)
                wide2(g, [(slab(i)[:, k, (j % 2) * P:(j % 2) * P + P], mrg[:, k, :]) for k in range(KD)])
                slab_last[i] = g
            norm_sum(8)
            pe.wait_ge(h_done, 32)
            sl.r = 0

            def score(hp, gq):
                g = sl.next()
                claim(g)
                pe.wait_ge(free[gq[0]], gq[1])
                for t in range(NT):
                    o = bank(g[0])[:, t * P:(t + 1) * P] if t < 4 else bank2(g[0])[:, 0:P]
                    mm = nc.tensor.matmul(o, r_qT[:, hp % 2, t * P:(t + 1) * P], r_sk[:, hp, :], start=True, stop=True)
                mm.then_inc(full[g[0]], 1)

            gq = None
            pe.wait_ge(phload, 16 * LOADS['sk'])
            for hp in range(16):
                i = SLABS['w_q'] + hp // 2
                slab_wait(i)
                g = sl.next()
                wide(g, [(slab(i)[:, k, (hp % 2) * P:(hp % 2) * P + P], h[:, k, :]) for k in range(KD)])
                slab_last[i] = g
                if gq:
                    score(hp - 1, gq)
                gq = g
            score(15, gq)
            sl.r = 0
            for t in range(NT):
                pe.wait_ge(S("r_e"), t + 1)
                g = sl.next()
                claim(g)
                for w in range(3):
                    mm = nc.tensor.transpose(bank(g[0])[:, w * P:(w + 1) * P], r_e[:, w, :], ident)
                mm.then_inc(full[g[0]], 1)
                for q in range(P // 4):
                    g = sl.next()
                    claim(g)
                    for i in range(4):
                        n = t * P + q * 4 + i
                        if i == 0:
                            pe.wait_ge(S("r_L"), (n + 4) // 4)
                            pe.wait_ge(S("r_R"), (n + 4) // 4)
                        mm = nc.tensor.matmul(bank(g[0])[:, i * P:(i + 1) * P], r_L[:, n % NOH, :], r_R[:, n % NOH, :],
                                              start=True, stop=True)
                    mm.then_inc(full[g[0]], 1)
            sl.r = 0
            for s in (0, 1, 2, 3):
                pe.wait_ge(free[s], sl.n[s])
            base = list(sl.n)
            map_slots['base'] = base

            def first(b, r, lot):
                pe.wait_ge(u_sem[r], lot)
                for c in range(4):
                    s = c % 2
                    use = b * 2 + c // 2
                    pe.wait_ge(free[s], base[s] + use)
                    for a in range(2):
                        for k in range(KD):
                            mm = nc.tensor.matmul(ps[:, 2 * s + a, 0:HALF], p_u[:, r, c, k, :],
                                                  h[:, k, a * HALF:(a + 1) * HALF], start=(k == 0), stop=(k == KD - 1))
                    mm.then_inc(full[s], 1)

            def second(b, r, lot):
                pe.wait_ge(v_sem[r], lot)
                pe.wait_ge(S("p_A"), 4 * (b + 1))
                for j in range(KD):
                    s = 2 + j % 2
                    use = b * 4 + j // 2
                    pe.wait_ge(free[s], base[s] + use)
                    for o, lo, hi in ((bank(s), 0, TS), (bank2(s)[:, 0:TP], TS, TOK)):
                        for c in range(4):
                            mm = nc.tensor.matmul(o, p_v[:, r, c, j * P:(j + 1) * P], p_a[:, r, c, lo:hi],
                                                  start=(c == 0), stop=(c == 3))
                    mm.then_inc(full[s], 1)

            first(0, 0, 16)
            with pe.Fori(0, NB // 2 - 1) as i:
                first(i * 2 + 1, 1, i * 16 + 16)
                second(i * 2, 0, i * 16 + 16)
                first(i * 2 + 2, 0, i * 16 + 32)
                second(i * 2 + 1, 1, i * 16 + 16)
            first(NB - 1, 1, 8 * NB)
            second(NB - 2, 0, 8 * NB)
            second(NB - 1, 1, 8 * NB)
            sl.n = [base[s] + (2 * NB if s < 2 else 4 * NB) for s in range(4)]
            norm_sum(16)

        @block.scalar
        def _(act):
            sl = Slots()
            ch = [0]

            def link(ins):
                ch[0] += 1
                ins.then_inc(ach, 1)
                act.wait_ge(ach, ch[0])

            def got(g):
                act.wait_ge(full[g[0]], g[1])

            A = nc.scalar.activation
            act.wait_ge(load, 16 * 5)
            act.dma_start(x[:], x_in).then_inc(load_x, 16)
            act.dma_start(a_C0, c0_in).then_inc(phload, 16)
            act.dma_start(a_vb, tokb_in[0]).then_inc(phload, 16)
            A(cs[:], V('cond', 0, 16).rearrange("p (k g) -> p k g", g=2), ACT.Silu).then_inc(silu_done, 1)
            sl.next()

            def norm_scalar(m, shift):
                for k in range(KD):
                    act.wait_ge(x_ready, 8 * m + k + 1)
                    A(sq[:, k, :], x[:, k, :], ACT.Square).then_inc(sq_done, 1)
                g = sl.next()
                got(g)
                A(two(rstd), halves(g[0]), ACT.Sqrt, bias=cepsD).then_inc(free[g[0]], 1)
                for k in range(KD):
                    for gq, (lo, hi) in enumerate(((0, TS), (TS, TOK))):
                        act.wait_ge(hm_done, 16 * m + 2 * k + gq + 1)
                        A(h[:, k, lo:hi], h[:, k, lo:hi], ACT.Identity, bias=modv[:, shift + k, gq:gq + 1])\
                            .then_inc(h_done, 1)

            norm_scalar(0, 0)
            for c in range(4):
                g = sl.next()
                got(g)
                A(two(a_q[:, c, :]), halves(g[0]), ACT.Identity, bias=V('a_q', c)).then_inc(free[g[0]], 1)
            act.wait_ge(free[g[0]], g[1])
            A(scr[:, 127:128], a_q[:, 0, 0:1], ACT.Copy).then_inc(S("a_q_ready"), 4)
            for c in range(4 + 2 * NT):
                sl.next()
            for c in range(4):
                g = sl.next()
                got(g)
                A(two(a_o[:, c, :]), halves(g[0]), ACT.Sigmoid, bias=V('a_o', c)).then_inc(free[g[0]], 1)
            for _ in range(4):
                sl.next()
            act.wait_ge(S("a_rows_raw"), 4)
            link(A(a_rM, a_rF, ACT.Abs))
            link(A(a_rM, a_rM, ACT.Exp, scale=-1.0))
            A(a_rM, a_rM, ACT.Ln, bias=1.0).then_inc(S("a_rows_ln"), 1)
            g = sl.next()
            got(g)
            A(a_kT, bank(g[0]), ACT.Copy).then_inc(free[g[0]], 1)
            ggc = sl.next()
            act.wait_ge(S("a_rows_m"), 1)
            link(A(a_rFl, a_rFl, ACT.Exp))
            for d in range(2):
                ins = A(a_rW[:, d, 0:TS], a_rM[:, d, 0:TS], ACT.Exp, scale=-1.0, bias=rowv[0:4, d:d + 1])
            ins.then_inc(S("a_rows_w"), 1)
            sl.r = 0
            hist = []
            act.wait_ge(phload, 32)
            act.wait_ge(free[ggc[0]], ggc[1])
            for d in range(2):
                for hh in range(4):
                    n = d * 4 + hh
                    if n:
                        act.wait_ge(S("a_state_used"), n)
                    A(a_n0, ones, ACT.Copy, scale=V('n0', n)).then_inc(S("a_n0_ready"), 1)
                    sl.next((0, 1))
                    for k, dst in enumerate((a_Mb, a_Fb)):
                        g = sl.next((0, 1))
                        got(g)
                        if n:
                            act.wait_ge(S("a_nd_read"), n)
                        A(two(dst), halves(g[0]), ACT.Copy).then_inc(free[g[0]], 1)
                        if k == 0:
                            gm = g
                    act.wait_ge(free[gm[0]], gm[1])
                    order = ([0, 1, 2, 3] if d == 0 else [3, 2, 1, 0]) + [4]
                    for idx, i in enumerate(order):
                        it = n * 5 + idx
                        lo, hi = a_range(d, i)
                        g = sl.next((0, 1))
                        hist.append(g)
                        if it >= 2:
                            act.wait_ge(free[hist[it - 2][0]], hist[it - 2][1])
                        if idx == 1 and n:
                            act.wait_ge(S("a_kw_ready"), n)
                        bias = a_gc[:, d, i, hh:hh + 1]
                        dl = i * P
                        if hi - lo > P:
                            rl, rh = (dl + P, hi) if d == 0 else (lo, dl)
                            A(a_E[:, it % 2, rl:rh], a_Mb[:, rl:rh], ACT.Exp, scale=-1.0, bias=bias)
                        act.wait_ge(S("a_dm"), it + 1)
                        A(a_E[:, it % 2, dl:dl + P], a_dm[:, it % 2, :], ACT.Exp, scale=-1.0, bias=bias)\
                            .then_inc(S("a_E"), 1)
                    g = sl.next((0, 1))
                    got(g)
                    A(a_st[:, n, :], bank(g[0])[:, 0:P + 1], ACT.Copy).then_inc(free[g[0]], 1)
            act.wait_ge(free[g[0]], g[1])
            for n in range(8):
                act.dma_start(c_out[n], a_st[:, n, 0:P]).then_inc(stored, 16)
                act.dma_start(n_out[n], a_st[:, n, P:P + 1]).then_inc(stored, 16)
            act.dma_start(m_out[0], a_rI[:, 0, TOK - 1:TOK]).then_inc(stored, 16)
            act.dma_start(m_out[1], a_rI[:, 1, TS:TS + 1]).then_inc(stored, 16)
            STORES[0] += 18
            act.wait_ge(stored, 16 * STORES[0])
            act.wait_ge(S("a_ha"), 8)
            for hh in range(4):
                A(sq[:, hh, :], a_ha[:, hh, :], ACT.Square).then_inc(S("a_sq"), 1)
            head_roots(sl, got)
            A(scr[:, 126:127], a_gc[:, 0, 0, 0:1], ACT.Copy).then_inc(phase_a, 1)
            phase(act, 1)

            def gl_core(m, n):
                J, d = m['J'], n % 2
                last = P - 1 if d == 0 else 0
                X, b = m['X'], m['b']
                for t in range(NT):
                    sl.next()
                gs = []
                for li in range(len(LEVELS)):
                    act.wait_ge(S("g_Z"), n * 7 + li + 1)
                    A(X[li % 2], X[li % 2], ACT.Exp).then_inc(S("g_E"), 1)
                    for t in range(NT):
                        gs.append(sl.next())
                bt = b.rearrange("p (n t) -> p n t", t=P)
                act.wait_ge(full[gs[29][0]], gs[29][1])
                A(X[1], b, ACT.Exp).then_inc(S("g_EB"), 1)
                act.wait_ge(full[gs[34][0]], gs[34][1])
                for e in range(J * NT):
                    A(X[0][:, e * P:(e + 1) * P], b[:, e * P:(e + 1) * P], ACT.Exp, scale=-1.0,
                      bias=b[:, e * P + last:e * P + last + 1])
                A(m['dec'], bt[:, :, last], ACT.Exp).then_inc(S("g_EK"), 1)
                for idx, t in enumerate(tiles_of(d)):
                    g = sl.next()
                    got(g)
                    if idx >= 2:
                        act.wait_ge(full[gk[idx - 2][0]], gk[idx - 2][1])
                    elif idx == 0:
                        gk = []
                    A(m['kT'][idx % 2], bank(g[0])[:, 0:J * P], ACT.Copy).then_inc(free[g[0]], 1)
                    g = sl.next()
                    if idx != 3:
                        gk.append(sl.next())
                    else:
                        gk.append(g)

            def gl_end(m, k, base):
                for hh in range(HEADS):
                    if hh == 0:
                        act.wait_ge(S("g_o"), k + 1)
                    A(sq[:, hh, :], m['o'][:, hh, :], ACT.Square).then_inc(S("g_sq"), 1)
                for d in range(2):
                    for hh in range(HEADS):
                        j, r = rows(m['J'], hh)
                        dst = (sb_out, sc_out)[k][d * 4 + hh]
                        act.dma_start(dst, m['Snew'][r, d, j, :]).then_inc(stored, 16)
                        STORES[0] += 1
                head_roots(sl, got)
                act.wait_ge(stored, 16 * STORES[0])
                A(scr[:, 125 - k:126 - k], ones[:, 0:1], ACT.Copy).then_inc(phase_a, 1)

            sl.r = 0
            act.dma_start(mB['S'], s0b_in).then_inc(phload, 16)
            act.dma_start(mB['vb'], tokb_in[1]).then_inc(phload, 16)
            act.wait_ge(S("lb_in"), 1)
            A(lbw[:, 8:16], lbw[:, 0:8], ACT.Exp).then_inc(S("lb_exp"), 1)
            for _ in range(4 + 2 * NT):
                sl.next()
            for c in range(4):
                g = sl.next()
                got(g)
                A(two(ybr[:, 1, c, :]), halves(g[0]), ACT.Silu, bias=V('b_g', c)).then_inc(free[g[0]], 1)

            def logsig(m, n, z):
                X = m['X']
                link(A(X[0], z, ACT.Abs))
                link(A(X[0], X[0], ACT.Exp, scale=-1.0))
                A(X[0], X[0], ACT.Ln, bias=1.0).then_inc(S("g_L"), 1)

            for d in range(2):
                z = mB['k']
                if d:
                    act.wait_ge(S("g_X"), 9)
                    act.wait_ge(S("g_free"), 1)
                for c in range(4):
                    g = sl.next()
                    got(g)
                    A(two(z[:, c * TOK:(c + 1) * TOK]), halves(g[0]), ACT.Identity, bias=V('b_f', 4 * d + c))\
                        .then_inc(free[g[0]], 1)
                act.wait_ge(free[g[0]], g[1])
                logsig(mB, d, z)
                act.wait_ge(S("b_zc"), d + 1)
                link(A(mB['X'][1], mB['X'][1], ACT.Exp, scale=-1.0))
                for c in range(4):
                    xc = mB['X'][1][:, c * TOK:(c + 1) * TOK]
                    ins = A(xc, xc, ACT.Ln, scale=lbw[:, 16 + 4 * d + c:17 + 4 * d + c], bias=1.0)
                ins.then_inc(S("b_L2"), 1)
                act.wait_ge(S("b_lf"), d + 1)
                A(z, z, ACT.Sigmoid, scale=-1.0).then_inc(S("b_sig"), 1)
                gl_core(mB, d)
            gl_end(mB, 0, 0)
            phase(act, 2)
            sl.r = 0
            act.dma_start(mC['S'], s0c_in).then_inc(phload, 16)
            act.dma_start(mC['vb'], tokb_in[2]).then_inc(phload, 16)
            act.dma_start(c_up, up_in).then_inc(phload, 16)
            for _ in range(4 + 2 * NT):
                sl.next()
            for c in range(4):
                g = sl.next()
                got(g)
                A(two(ybr[:, 2, c, :]), halves(g[0]), ACT.Silu, bias=V('c_g', c)).then_inc(free[g[0]], 1)
            for _ in range(2):
                sl.next()
            for d in range(2):
                if d:
                    act.wait_ge(S("g_free"), 3)
                for j in range(2):
                    g = sl.next()
                    got(g)
                    A(two(mC['b'][:, j * TOK:(j + 1) * TOK]), halves(g[0]), ACT.Identity, bias=V('b_up', 2 * d + j))\
                        .then_inc(free[g[0]], 1)
                act.wait_ge(free[g[0]], g[1])
                logsig(mC, 2 + d, mC['b'])
                gl_core(mC, 2 + d)
            gl_end(mC, 1, 4)
            phase(act, 3)
            sl.r = 0
            act.dma_start(d_w, lruw_in).then_inc(phload, 16)
            for c in range(4):
                g = sl.next()
                got(g)
                A(two(d_x[:, c, :]), halves(g[0]), ACT.Identity, bias=V('d_x', c)).then_inc(free[g[0]], 1)
            act.wait_ge(free[g[0]], g[1])
            A(scr[:, 120:121], ones[:, 0:1], ACT.Copy).then_inc(S("d_x"), 1)
            for c in range(4):
                g = sl.next()
                got(g)
                A(two(ybr[:, 3, c, :]), halves(g[0]), ACT.Gelu_apprx_tanh, bias=V('d_g', c)).then_inc(free[g[0]], 1)
            link(A(d_tmp, V('lam', 0, 8), ACT.Abs))
            link(A(d_tmp, d_tmp, ACT.Exp, scale=-1.0))
            A(d_tmp, d_tmp, ACT.Ln, bias=1.0).then_inc(S("d_sp"), 1)
            for d in range(2):
                if d:
                    act.wait_ge(S("d_scanned"), 1)
                for hh in range(HEADS):
                    for w, (dst, bias) in enumerate(((d_R, 'lru_b_a'), (d_U, 'lru_b_x'))):
                        g = sl.next()
                        got(g)
                        A(two(dst[:, hh, :]), halves(g[0]), ACT.Sigmoid, bias=V(bias, 4 * d + hh))\
                            .then_inc(free[g[0]], 1)
                act.wait_ge(free[g[0]], g[1])
                gprev = (g[0] - 1) % 4
                act.wait_ge(free[gprev], g[1])
                act.wait_ge(S("d_spl"), 1)
                for hh in range(HEADS):
                    A(d_T[:, hh, :], d_R[:, hh, :], ACT.Tanh, scale=d_nspl[:, 4 * d + hh:4 * d + hh + 1])
                link(A(scr[:, 118 - d:119 - d], ones[:, 0:1], ACT.Copy))
                for hh in range(HEADS):
                    ins = A(d_R[:, hh, :], d_R[:, hh, :], ACT.Exp, scale=d_spl[:, 4 * d + hh:4 * d + hh + 1])
                ins.then_inc(S("d_a"), 1)
                act.wait_ge(S("d_w2"), d + 1)
                A(d_T, d_T, ACT.Sqrt).then_inc(S("d_rt"), 1)
            act.wait_ge(S("d_scanned"), 2)
            for n in range(8):
                act.dma_start(h_out[n], d_new[:, n:n + 1]).then_inc(stored, 16)
                STORES[0] += 1
            act.wait_ge(stored, 16 * STORES[0])
            A(scr[:, 119:120], ones[:, 0:1], ACT.Copy).then_inc(phase_a, 1)
            phase(act, 4)
            sl.r = 0
            act.dma_start(r_sk, sk_in).then_inc(phload, 16)
            gp = []
            for j in range(KD):
                for n in range(NBR):
                    e = 4 * j + n
                    g = sl.next()
                    got(g)
                    if e >= 2:
                        act.wait_ge(free[gp[-2][0]], gp[-2][1])
                    A(two(m_sg[:, e % 2, :]), halves(g[0]), ACT.Sigmoid, bias=V('gates', n * KD + j))\
                        .then_inc(free[g[0]], 1)
                    gp.append(sl.next())
            for j in range(KD):
                sl.next()
            norm_scalar(1, 24)
            sl.r = 0

            def score(hp):
                g = sl.next()
                got(g)
                A(r_s[:, 0:4, hp, :], bank(g[0]).rearrange("p (n e) -> p n e", n=4), ACT.Copy)
                A(r_s[:, 4, hp, :], bank2(g[0])[:, 0:P], ACT.Copy).then_inc(free[g[0]], 1)
                return g

            gs = []
            for hp in range(16):
                g = sl.next()
                got(g)
                if hp >= 2:
                    act.wait_ge(full[gs[hp - 2][0]], gs[hp - 2][1])
                A(two(r_qT[:, hp % 2, :]), halves(g[0]), ACT.Copy).then_inc(free[g[0]], 1)
                if hp:
                    gs.append(score(hp - 1))
            g = score(15)
            act.wait_ge(free[g[0]], g[1])
            A(scr[:, 121:122], ones[:, 0:1], ACT.Copy).then_inc(S("r_scores"), 1)
            sl.r = 0
            for t in range(NT):
                act.wait_ge(S("r_sub"), t + 1)
                A(r_t, r_t, ACT.Exp).then_inc(S("r_exp"), 1)
                g = sl.next()
                got(g)
                if t >= 2:
                    act.wait_ge(S("r_L"), 32 * (t - 1))
                    act.wait_ge(S("r_R"), 32 * (t - 1))
                A(r_T[:, t % 2], bank(g[0])[:, 0:384].rearrange("p (w c) -> p w c", w=3), ACT.Copy)\
                    .then_inc(free[g[0]], 1)
                for q in range(P // 4):
                    g = sl.next()
                    got(g)
                    hf = 2 * t + q // 16
                    if q % 16 == 0 and hf >= 2:
                        act.wait_ge(map_out[hf % 2], 16 * (hf // 2))
                    n0 = (q % 16) * 4
                    A(g_stage[:, hf % 2, :, n0:n0 + 4].rearrange("p e n -> p n e"),
                      bank(g[0]).rearrange("p (n e) -> p n e", n=4), ACT.Copy).then_inc(free[g[0]], 1)
            base = list(sl.n)

            def first(b, r, lot):
                for c in range(4):
                    s = c % 2
                    act.wait_ge(full[s], base[s] + b * 2 + c // 2 + 1)
                    act.wait_ge(S("p_A"), b * 4 + (c - 1))
                    A(two(p_t[:, c % 2, :]), halves(s), ACT.Gelu_apprx_tanh).then_inc(free[s], 1)

            for c in range(4):
                s = c % 2
                act.wait_ge(full[s], base[s] + c // 2 + 1)
                if c >= 2:
                    act.wait_ge(S("p_A"), c - 1)
                A(two(p_t[:, c % 2, :]), halves(s), ACT.Gelu_apprx_tanh).then_inc(free[s], 1)
            with act.Fori(0, NB // 2 - 1) as i:
                first(i * 2 + 1, 1, i * 16 + 16)
                first(i * 2 + 2, 0, i * 16 + 32)
            first(NB - 1, 1, 8 * NB)
            sl.n = [base[s] + (2 * NB if s < 2 else 4 * NB) for s in range(4)]
            sl.r = 0
            for k in range(KD):
                act.wait_ge(x_ready, 16 + k + 1)
                A(sq[:, k, :], x[:, k, :], ACT.Square).then_inc(sq_done, 1)
            g = sl.next()
            got(g)
            A(two(rstd), halves(g[0]), ACT.Sqrt, bias=cepsD).then_inc(free[g[0]], 1)
            act.wait_ge(S("y_done"), 8)
            act.dma_start(y_out, h[:]).then_inc(stored, 16)
            STORES[0] += 1

        @block.vector
        def _(dve):
            sl = Slots()
            ch = [0]
            vv = nc.vector

            def link(ins):
                ch[0] += 1
                ins.then_inc(vch, 1)
                dve.wait_ge(vch, ch[0])

            def got(g):
                dve.wait_ge(full[g[0]], g[1])

            dve.wait_ge(load, 16 * 5)
            link(vv.tensor_copy(lvl[:], lvl_f))
            dve.wait_ge(load_x, 16)
            for k in range(4):
                xv = x[:, k, 0:TS].rearrange("p (r c) -> p r c", c=GRID_W)
                pr = V('pos_r', 8 * k, 8).unsqueeze(2).to_broadcast([P, 8, GRID_W])
                vv.tensor_tensor(xv, xv, pr, ALU.add).then_inc(x_ready, 1)
            for k in range(4):
                xv = x[:, 4 + k, 0:TS].rearrange("p (r c) -> p r c", c=GRID_W)
                pc = V('pos_c', 64 * k, 64).unsqueeze(1).to_broadcast([P, 8, GRID_W])
                vv.tensor_tensor(xv, xv, pc, ALU.add).then_inc(x_ready, 1)
            g = sl.next()
            got(g)
            link(vv.tensor_tensor(modv[:], bank(g[0])[:, 0:96].rearrange("p (m g) -> p m g", g=2),
                                  V('b_mod', 0, 48).unsqueeze(2).to_broadcast([P, 48, 2]), ALU.add))
            mark().then_inc(free[g[0]], 1)

            def norm_vector(m, gname, scale_at):
                link(vv.tensor_scalar(amul[:], modv[:, scale_at:scale_at + 8, :], 1.0, D ** 0.5, ALU.add, ALU.mult))
                link(vv.tensor_tensor(amul[:], amul[:], V(gname, 0, 8).unsqueeze(2).to_broadcast([P, 8, 2]), ALU.mult))
                g = sl.next()
                dve.wait_ge(free[g[0]], g[1])
                link(vv.reciprocal(rstd, rstd))
                for k in range(KD):
                    for gq, (lo, hi) in enumerate(((0, TS), (TS, TOK))):
                        vv.scalar_tensor_tensor(out=h[:, k, lo:hi], in0=x[:, k, lo:hi], scalar=amul[:, k, gq:gq + 1],
                                                in1=rstd[:, lo:hi], op0=ALU.mult, op1=ALU.mult).then_inc(hm_done, 1)

            norm_vector(0, 'norm1', 8)
            for c in range(4):
                sl.next()
            for c in range(4):
                g = sl.next()
                got(g)
                vv.tensor_scalar(two(a_k[:, c, :]), halves(g[0]), V('a_k', c), P ** -0.5, ALU.add, ALU.mult)\
                    .then_inc(free[g[0]], 1)
            mark().then_inc(S("a_k_ready"), 4)
            dve.wait_ge(phload, 32)
            for c in range(2):
                for t in range(NT):
                    g = sl.next()
                    got(g)
                    vv.tensor_tensor(a_v[:, t, c * 256:(c + 1) * 256], bank(g[0])[:, 0:256],
                                     a_vb[:, c * 256:(c + 1) * 256], ALU.add).then_inc(free[g[0]], 1)
            mark().then_inc(S("a_v_ready"), 2 * NT)
            for c in range(4):
                sl.next()
            for d in range(2):
                for which in range(2):
                    g = sl.next()
                    got(g)
                    vv.tensor_scalar(two((a_rI, a_rF)[which][:, d, :]), ps[0:4, 2 * g[0]:2 * g[0] + 2, 0:HALF],
                                     rowv[0:4, 2 + d * 2 + which:3 + d * 2 + which], None, ALU.add)\
                        .then_inc(free[g[0]], 1)
            mark().then_inc(S("a_rows_raw"), 4)
            dve.wait_ge(S("a_rows_ln"), 1)
            link(vv.scalar_tensor_tensor(out=a_rF, in0=a_rF, scalar=0.0, in1=a_rM, op0=ALU.min, op1=ALU.subtract))
            one4 = ones[0:4, 0:1]

            def seqs(ap, d):
                a, b = ap[:, d, 0:TS], ap[:, d, TS:TOK]
                return (a, b) if d == 0 else (a[:, ::-1], b[:, ::-1])

            for d in range(2):
                for q in range(2):
                    f = seqs(a_rF, d)[q]
                    vv.tensor_tensor_scan(out=seqs(a_rW, d)[q], data0=one4.to_broadcast([4, f.shape[1]]), data1=f,
                                          initial=0.0, op0=ALU.mult, op1=ALU.add)
            link(mark())
            vv.tensor_tensor(a_rG, a_rI, a_rW, ALU.subtract).then_inc(S("a_rows_g"), 1)
            dve.wait_ge(S("a_rows_g"), 1)
            for d in range(2):
                for q in range(2):
                    gg = seqs(a_rG, d)[q]
                    vv.tensor_tensor_scan(out=seqs(a_rM, d)[q], data0=one4.to_broadcast([4, gg.shape[1]]), data1=gg,
                                          initial=rowv[0:4, d:d + 1] if q == 0 else 0.0, op0=ALU.mult, op1=ALU.max)
            link(mark())
            link(vv.tensor_tensor(a_rI, a_rW, a_rM, ALU.add))
            vv.tensor_scalar(a_rFl, a_rI, -1.0, 80.0, ALU.mult, ALU.min).then_inc(S("a_rows_m"), 1)
            gkt = sl.next()
            g = sl.next()
            got(g)
            dve.wait_ge(free[gkt[0]], gkt[1])
            vv.tensor_copy(a_gc.rearrange("p d n h -> p (d n h)"), bank(g[0])[:, 0:40]).then_inc(free[g[0]], 1)
            sl.r = 0
            for d in range(2):
                for hh in range(4):
                    n = d * 4 + hh
                    g = sl.next((0, 1))
                    got(g)
                    if n:
                        dve.wait_ge(S("a_state_used"), n)
                    vv.tensor_tensor(a_qt, a_q[:, hh, 0:TS], bank(g[0]), ALU.mult).then_inc(free[g[0]], 1)
                    mark().then_inc(S("a_qt_ready"), 1)
                    gm = sl.next((0, 1))
                    gf = sl.next((0, 1))
                    dve.wait_ge(free[gm[0]], gm[1])
                    over = C('over0') if d == 0 else C('over1')
                    order = ([0, 1, 2, 3] if d == 0 else [3, 2, 1, 0]) + [4]

                    def dm(idx):
                        it = n * 5 + idx
                        if it >= 2:
                            dve.wait_ge(S("a_E"), it - 1)
                        i = order[idx]
                        vv.tensor_tensor(a_dm[:, it % 2, :], a_Mb[:, i * P:(i + 1) * P], over, ALU.add)\
                            .then_inc(S("a_dm"), 1)

                    dm(0)
                    for idx, i in enumerate(order):
                        it = n * 5 + idx
                        lo, hi = a_range(d, i)
                        if idx < 4:
                            dm(idx + 1)
                        g = sl.next((0, 1))
                        got(g)
                        dve.wait_ge(S("a_E"), it + 1)
                        if it >= 2:
                            dve.wait_ge(S("a_pv"), it - 1)
                        vv.tensor_tensor(a_P[:, it % 2, lo:hi], bank(g[0])[:, 0:hi - lo], a_E[:, it % 2, lo:hi],
                                         ALU.mult).then_inc(free[g[0]], 1)
                    last = TOK - 1 if d == 0 else TS
                    if n:
                        dve.wait_ge(full[gst[0]], gst[1])
                    vv.tensor_scalar(a_kw, a_kT[:, hh * P:(hh + 1) * P], a_E[:, it % 2, last:last + 1], None, ALU.mult)\
                        .then_inc(S("a_kw_ready"), 1)
                    gst = sl.next((0, 1))
                    dve.wait_ge(S("a_pv"), 5 * (n + 1))
                    dve.wait_ge(free[gf[0]], gf[1])
                    vv.tensor_tensor(a_D[:, 0:TS], bank(den), a_Fb[:, 0:TS], ALU.max)
                    link(vv.tensor_tensor(a_D[:, TS:TOK], bank2(den)[:, 0:P], a_Fb[:, TS:TOK], ALU.max))
                    for q, dd in (((0, TS), bank(den)), ((TS, TOK), bank2(den)[:, 0:P])):
                        ins = vv.scalar_tensor_tensor(out=a_D[:, q[0]:q[1]], in0=dd, scalar=-1.0,
                                                      in1=a_D[:, q[0]:q[1]], op0=ALU.mult, op1=ALU.max)
                    link(ins)
                    link(vv.reciprocal(a_D, a_D))
                    dst = a_ha[:, hh, :] if d == 0 else a_T
                    vv.tensor_tensor(dst[:, 0:TS], a_D[:, 0:TS], bank(num), ALU.mult)
                    vv.tensor_tensor(dst[:, TS:TOK], a_D[:, TS:TOK], bank2(num)[:, 0:P], ALU.mult)\
                        .then_inc(S("a_nd_read"), 1)
                    dve.wait_ge(S("a_nd_read"), n + 1)
                    if d == 1:
                        link(vv.tensor_tensor(a_ha[:, hh, :], a_ha[:, hh, :], a_T, ALU.add))
            mark().then_inc(S("a_ha"), 8)
            for hh in range(4):
                head_norm(dve, link, sl.next((0, 1)), a_ha[:, hh, :], a_o[:, hh, :], sq[:, 4 + hh, :], a_T)
            mark().then_inc(phase_v, 1)
            phase(dve, 1)
            TT, TSC, STT = vv.tensor_tensor, vv.tensor_scalar, vv.scalar_tensor_tensor

            def gl_core(m, n):
                J, d = m['J'], n % 2
                last = P - 1 if d == 0 else 0
                X, b, q, k = m['X'], m['b'], m['q'], m['k']
                for j in range(J):
                    bj = b[:, j * TOK:(j + 1) * TOK]
                    rs = C('reset0') if d == 0 else C('reset1')
                    if d:
                        bj, rs = bj[:, ::-1], rs[:, ::-1]
                    ins = vv.tensor_tensor_scan(out=bj, data0=rs, data1=bj, initial=0.0, op0=ALU.mult, op1=ALU.add)
                link(ins)
                mark().then_inc(S("g_in"), 1)
                used = []

                def sub(li):
                    w = LEVELS[li]
                    if li >= 2:
                        dve.wait_ge(full[used[li - 2][0]], used[li - 2][1])
                    bv = b.rearrange("p (n s w) -> p n s w", s=2, w=w)
                    xv = X[li % 2].rearrange("p (n s w) -> p n s w", s=2, w=w)
                    nb = J * TOK // (2 * w)
                    ref = (bv[:, :, 0, w - 1:w] if d == 0 else bv[:, :, 1, 0:1]).to_broadcast([P, nb, w])
                    fut, past = (1, 0) if d == 0 else (0, 1)
                    TT(xv[:, :, fut, :], bv[:, :, fut, :], ref, ALU.subtract)
                    TT(xv[:, :, past, :], ref, bv[:, :, past, :], ALU.subtract).then_inc(S("g_Z"), 1)

                def mul(li):
                    w = LEVELS[li]
                    dve.wait_ge(S("g_E"), n * 7 + li + 1)
                    xv = X[li % 2].rearrange("p (n s w) -> p n s w", s=2, w=w)
                    fut, past = (1, 0) if d == 0 else (0, 1)
                    TT(xv[:, :, fut, :], xv[:, :, fut, :], q.rearrange("p (n s w) -> p n s w", s=2, w=w)[:, :, fut, :],
                       ALU.mult)
                    TT(xv[:, :, past, :], xv[:, :, past, :],
                       k.rearrange("p (n s w) -> p n s w", s=2, w=w)[:, :, past, :], ALU.mult).then_inc(S("g_X"), 1)

                sub(0)
                for t in range(NT):
                    g = sl.next()
                    got(g)
                    TT(heads_row(J, m['P'][:, t, :]), heads_psum(J, g), heads_same(J, ident), ALU.mult).then_inc(free[g[0]], 1)
                mul(0)
                for li in range(len(LEVELS)):
                    if li + 1 < len(LEVELS):
                        sub(li + 1)
                    for t in range(NT):
                        g = sl.next()
                        got(g)
                        dve.wait_ge(free[pw[t][0]], pw[t][1]) if li else None
                        vv.copy_predicated(heads_row(J, m['P'][:, t, :]), heads_same(J, lvl[:, d, li, :]),
                                           heads_psum(J, g)).then_inc(free[g[0]], 1)
                        pw[t] = g
                    used.append(g)
                    if li + 1 < len(LEVELS):
                        mul(li + 1)
                dve.wait_ge(S("g_EB"), n + 1)
                TT(X[1], X[1], q, ALU.mult).then_inc(S("g_X"), 1)
                dve.wait_ge(S("g_EK"), n + 1)
                TT(X[0], X[0], k, ALU.mult).then_inc(S("g_X"), 1)
                dve.wait_ge(S("g_X"), n * 9 + 9)
                mark().then_inc(S("g_free"), 1)
                for idx, t in enumerate(tiles_of(d)):
                    sl.next()
                    g = sl.next()
                    got(g)
                    o = m['o'][:, :, t * P:(t + 1) * P]
                    if J == 2:
                        o = o.rearrange("p (j a) t -> p a j t", a=2)
                    pv = heads_psum(J, g)
                    if d == 0:
                        vv.tensor_copy(o, pv).then_inc(free[g[0]], 1)
                    else:
                        TT(o, o, pv, ALU.add).then_inc(free[g[0]], 1)
                    if idx == 3:
                        continue
                    g = sl.next()
                    got(g)
                    if 0 < idx < 4:
                        dve.wait_ge(free[gkp[0]], gkp[1])
                    for hh in range(HEADS):
                        j, r = rows(J, hh)
                        kv = bank(g[0])[r, hh * P:(hh + 1) * P]
                        if t < 4:
                            ins = STT(out=m['S'][r, d, j, :], in0=m['S'][r, d, j, :],
                                      scalar=m['dec'][r, j * NT + t:j * NT + t + 1], in1=kv, op0=ALU.mult, op1=ALU.add)
                        else:
                            ins = vv.tensor_copy(m['Snew'][r, d, j, :], kv)
                    ins.then_inc(free[g[0]], 1)
                    gkp = g

            def gl_end(m, k, gate):
                link(mark())
                mark().then_inc(S("g_o"), 1)
                for hh in range(HEADS):
                    head_norm(dve, link, sl.next((0, 1)), m['o'][:, hh, :], gate[:, hh, :], sq[:, 4 + hh, :],
                              m['P'].rearrange("p n c -> p (n c)")[:, 0:TOK])
                mark().then_inc(phase_v, 1)

            pw = {}
            sl.r = 0
            lb = V('lb', 0, 8)
            TT(lbw[:, 0:8], lb, lb, ALU.subtract).then_inc(S("lb_in"), 1)
            dve.wait_ge(S("lb_exp"), 1)
            link(vv.reciprocal(lbw[:, 24:32], lbw[:, 8:16]))
            link(TT(lbw[:, 8:16], lbw[:, 8:16], lbw[:, 24:32], ALU.mult))
            link(TT(lbw[:, 16:24], lbw[:, 8:16], lbw[:, 8:16], ALU.subtract))
            link(TSC(lbw[:, 24:32], lbw[:, 16:24], -1.0, 1.0, ALU.mult, ALU.add))
            for c in range(4):
                g = sl.next()
                got(g)
                TSC(two(mB['q'][:, c * TOK:(c + 1) * TOK]), halves(g[0]), V('b_q', c), P ** -0.5, ALU.add, ALU.mult)\
                    .then_inc(free[g[0]], 1)
            dve.wait_ge(phload, 16 * LOADS['B'])
            for c in range(2):
                for t in range(NT):
                    g = sl.next()
                    got(g)
                    TT(mB['v'][:, t, c * 256:(c + 1) * 256], bank(g[0])[:, 0:256], mB['vb'][:, c * 256:(c + 1) * 256],
                       ALU.add).then_inc(free[g[0]], 1)
            for c in range(4):
                sl.next()
            for d in range(2):
                for c in range(4):
                    g = sl.next()
                dve.wait_ge(free[g[0]], g[1])
                TSC(mB['X'][1], mB['k'], -80.0, None, ALU.max).then_inc(S("b_zc"), 1)
                dve.wait_ge(S("g_L"), d + 1)
                link(STT(out=mB['b'], in0=mB['k'], scalar=0.0, in1=mB['X'][0], op0=ALU.min, op1=ALU.subtract))
                dve.wait_ge(S("b_L2"), d + 1)
                TT(mB['b'], mB['b'], mB['X'][1], ALU.add).then_inc(S("b_lf"), 1)
                dve.wait_ge(S("b_lf"), d + 1)
                dve.wait_ge(S("b_sig"), d + 1)
                for c in range(4):
                    kc = mB['k'][:, c * TOK:(c + 1) * TOK]
                    ins = TSC(kc, kc, lbw[:, 24 + 4 * d + c:25 + 4 * d + c], None, ALU.mult)
                link(ins)
                gl_core(mB, d)
            gl_end(mB, 0, ybr[:, 1])
            phase(dve, 2)
            sl.r = 0
            for c in range(2):
                g = sl.next()
                got(g)
                TSC(two(mC['q'][:, c * TOK:(c + 1) * TOK]), halves(g[0]), V('c_q', c), 64 ** -0.5, ALU.add, ALU.mult)\
                    .then_inc(free[g[0]], 1)
            for c in range(2):
                g = sl.next()
                got(g)
                TSC(two(mC['k'][:, c * TOK:(c + 1) * TOK]), halves(g[0]), V('c_k', c), None, ALU.add)\
                    .then_inc(free[g[0]], 1)
            dve.wait_ge(phload, 16 * LOADS['C'])
            for c in range(2):
                for t in range(NT):
                    g = sl.next()
                    got(g)
                    TT(mC['v'][:, t, c * 256:(c + 1) * 256], bank(g[0])[:, 0:256], mC['vb'][:, c * 256:(c + 1) * 256],
                       ALU.add).then_inc(free[g[0]], 1)
            for c in range(4):
                sl.next()
            for d in range(2):
                g = sl.next()
                got(g)
                TSC(two(c_lr[:, d, :]), ps[0:16, 2 * g[0]:2 * g[0] + 2, 0:HALF], rowv[0:16, 6 + d:7 + d], None, ALU.add)\
                    .then_inc(free[g[0]], 1)
            mark().then_inc(S("c_lr"), 1)
            for d in range(2):
                for j in range(2):
                    g = sl.next()
                dve.wait_ge(free[g[0]], g[1])
                dve.wait_ge(S("g_L"), 3 + d)
                link(STT(out=mC['b'], in0=mC['b'], scalar=0.0, in1=mC['X'][0], op0=ALU.min, op1=ALU.subtract))
                link(TSC(mC['b'], mC['b'], 1.0 / 16.0, None, ALU.mult))
                gl_core(mC, 2 + d)
            gl_end(mC, 1, ybr[:, 2])
            phase(dve, 3)
            sl.r = 0
            for c in range(8):
                sl.next()
            dve.wait_ge(S("d_x"), 1)
            for hh in range(HEADS):
                cw = lambda w: V('conv_w', 4 * w + hh)
                TSC(d_xd[:, hh, :], d_x[:, hh, :], cw(1), V('conv_b', hh), ALU.mult, ALU.add)
            link(mark())
            for w, o in ((0, -1), (2, 1), (3, 2)):
                for hh in range(HEADS):
                    for lo, hi in ((0, TS), (TS, TOK)):
                        a, b_ = max(lo, lo - o), min(hi, hi - o)
                        ins = STT(out=d_xd[:, hh, a:b_], in0=d_x[:, hh, a + o:b_ + o],
                                  scalar=V('conv_w', 4 * w + hh), in1=d_xd[:, hh, a:b_], op0=ALU.mult, op1=ALU.add)
                link(ins)
            dve.wait_ge(phload, 16 * LOADS['D'])
            mark().then_inc(S("d_conv"), 1)
            dve.wait_ge(S("d_sp"), 1)
            link(TSC(d_spl, V('lam', 0, 8), -1.0, 0.0, ALU.mult, ALU.max))
            link(TT(d_spl, d_spl, d_tmp, ALU.add))
            link(TSC(d_nspl, d_spl, 8.0, None, ALU.mult))
            TSC(d_spl, d_spl, -8.0, None, ALU.mult).then_inc(S("d_spl"), 1)
            for d in range(2):
                for _ in range(8):
                    g = sl.next()
                dve.wait_ge(S("d_a"), d + 1)
                link(TT(d_Q, d_R, d_R, ALU.mult))
                link(STT(out=d_T, in0=d_Q, scalar=1.0, in1=d_T, op0=ALU.add, op1=ALU.mult))
                TSC(d_T, d_T, 0.0, None, ALU.max).then_inc(S("d_w2"), 1)
                link(TT(d_U, d_U, d_xd, ALU.mult))
                dve.wait_ge(S("d_rt"), d + 1)
                link(TT(d_U, d_U, d_T, ALU.mult))
                dst = d_H if d == 0 else d_Q
                for hh in range(HEADS):
                    for q, (lo, hi) in enumerate(((0, TS), (TS, TOK))):
                        o_, a_, u_ = dst[:, hh, lo:hi], d_R[:, hh, lo:hi], d_U[:, hh, lo:hi]
                        if d:
                            o_, a_, u_ = o_[:, ::-1], a_[:, ::-1], u_[:, ::-1]
                        vv.tensor_tensor_scan(out=o_, data0=a_, data1=u_,
                                              initial=V('h0', 4 * d + hh) if q == 0 else 0.0,
                                              op0=ALU.mult, op1=ALU.add)
                link(mark())
                lastc = TOK - 1 if d == 0 else TS
                vv.tensor_copy(d_new[:, 4 * d:4 * d + 4], dst[:, :, lastc]).then_inc(S("d_scanned"), 1)
            link(TT(d_H, d_H, d_Q, ALU.add))
            link(TT(ybr[:, 3], ybr[:, 3], d_H, ALU.mult))
            mark().then_inc(phase_v, 1)
            phase(dve, 4)
            sl.r = 0
            for j in range(KD):
                for n in range(NBR):
                    e = 4 * j + n
                    gg = sl.next()
                    g = sl.next()
                    dve.wait_ge(free[gg[0]], gg[1])
                    got(g)
                    o_ = mrg[:, j, :] if n == 0 else m_tmp
                    TT(two(o_), halves(g[0]), two(m_sg[:, e % 2, :]), ALU.mult).then_inc(free[g[0]], 1)
                    dve.wait_ge(free[g[0]], g[1])
                    if n:
                        link(TT(mrg[:, j, :], mrg[:, j, :], m_tmp, ALU.add))
                mark().then_inc(S("m_done"), 1)
            for j in range(KD):
                g = sl.next()
                got(g)
                STT(out=x[:, j, 0:TS], in0=bank(g[0]), scalar=modv[:, 16 + j, 0:1], in1=x[:, j, 0:TS], op0=ALU.mult,
                    op1=ALU.add)
                STT(out=x[:, j, TS:TOK], in0=bank2(g[0])[:, 0:TP], scalar=modv[:, 16 + j, 1:2], in1=x[:, j, TS:TOK],
                    op0=ALU.mult, op1=ALU.add).then_inc(free[g[0]], 1)
                dve.wait_ge(free[g[0]], g[1])
                mark().then_inc(x_ready, 1)
            norm_vector(1, 'norm2', 32)
            sl.r = 0
            for _ in range(32):
                sl.next()
            sl.r = 0
            dve.wait_ge(S("r_scores"), 1)
            NEG = -3.0e38
            gq = []

            def top16(vals, out, idx, tmp):
                link(vv.max(out[:, 0:8], vals))
                vv.max_index(idx[:, 0:8], out[:, 0:8], vals)
                link(vv.match_replace(tmp, out[:, 0:8], vals, NEG))
                link(vv.max(out[:, 8:16], tmp))
                link(vv.max_index(idx[:, 8:16], out[:, 8:16], tmp))

            for t in range(NT):
                for hp in range(16):
                    top16(r_s[:, t, hp, :], r_v[:, hp, :], r_i[:, hp, :], r_s2[:, 0:P])
                link(vv.tensor_copy(r_if, r_i))
                vh = r_v.rearrange("p (h s) k -> p h s k", s=2)
                for hh in range(PH):
                    ins = TT(r_c[:, hh, :].rearrange("p (a b) -> p a b", a=TOPK),
                             vh[:, hh, 0, :].unsqueeze(2).to_broadcast([P, TOPK, TOPK]),
                             vh[:, hh, 1, :].unsqueeze(1).to_broadcast([P, TOPK, TOPK]), ALU.add)
                link(ins)
                for hh in range(PH):
                    top16(r_c[:, hh, :], r_t[:, hh, :], r_p[:, hh, :], r_s2)
                link(TSC(r_sum[:, 0:8], r_t[:, :, 0], 0.0, None, ALU.add))
                TT(r_t, r_t, r_sum[:, 0:8].unsqueeze(2).to_broadcast([P, PH, TOPK]), ALU.subtract).then_inc(S("r_sub"), 1)
                pos = r_p.rearrange("p h k -> p (h k)")
                TSC(r_ab[:, 0, :], pos, 4, None, ALU.logical_shift_right)
                link(TSC(r_ab[:, 1, :], pos, 15, None, ALU.bitwise_and))
                link(vv.tensor_copy(r_abf, r_ab))
                dve.wait_ge(S("r_exp"), t + 1)
                link(vv.tensor_reduce(r_sum[:, 0:8], r_t, AX.X, ALU.add))
                link(vv.reciprocal(r_sum[:, 8:16], r_sum[:, 0:8]))
                if t:
                    dve.wait_ge(full[gT[0]], gT[1])
                link(TT(r_e[:, 2, :].rearrange("p (h k) -> p h k", h=PH), r_t,
                        r_sum[:, 8:16].unsqueeze(2).to_broadcast([P, PH, TOPK]), ALU.mult))
                for w in range(2):
                    oh = g_one.rearrange("p (c j) -> p c j", j=16)
                    link(TT(oh, r_abf[:, w, :].unsqueeze(2).to_broadcast([P, P, 16]),
                            C('jota').unsqueeze(1).to_broadcast([P, P, 16]), ALU.is_equal))
                    for hh in range(PH):
                        o8 = oh[:, hh * 16:(hh + 1) * 16, :]
                        ins = TT(o8, o8, r_if[:, 2 * hh + w, :].unsqueeze(1).to_broadcast([P, 16, 16]), ALU.mult)
                    link(ins)
                    ins = vv.tensor_reduce(r_e[:, w, :], oh, AX.X, ALU.add)
                    if w == 0:
                        link(ins)
                ins.then_inc(S("r_e"), 1)
                dve.wait_ge(S("r_e"), t + 1)
                gT = sl.next()
                map_slots['T'].append(gT)
                dve.wait_ge(free[gT[0]], gT[1])
                for q in range(P // 4):
                    gq.append(sl.next())
                    map_slots['q'].append(gq[-1])
                    n = t * P + q * 4
                    if len(gq) > 2:
                        dve.wait_ge(full[gq[-3][0]], gq[-3][1])
                    for i in range(4):
                        ins = TSC(r_L[:, (n + i) % NOH, :], C('iota'), r_T[:, t % 2, 0, q * 4 + i:q * 4 + i + 1],
                                  r_T[:, t % 2, 2, q * 4 + i:q * 4 + i + 1], ALU.is_equal, ALU.mult)
                    ins.then_inc(S("r_L"), 1)
            base = list(sl.n)

            def first(b, r, lot):
                dve.wait_ge(g_sem[r], lot)
                for c in range(4):
                    s = c % 2
                    dve.wait_ge(free[s], base[s] + b * 2 + c // 2 + 1)
                    TT(p_a[:, r, c, :].rearrange("p (q n) -> p q n", q=2 * NT), p_g[:, r, :, c, :],
                       p_t[:, c % 2, :].rearrange("p (q n) -> p q n", q=2 * NT), ALU.mult).then_inc(S("p_A"), 1)

            def second(b, r, lot):
                for j in range(KD):
                    s = 2 + j % 2
                    dve.wait_ge(full[s], base[s] + b * 4 + j // 2 + 1)
                    STT(out=x[:, j, 0:TS], in0=bank(s), scalar=modv[:, 40 + j, 0:1], in1=x[:, j, 0:TS],
                        op0=ALU.mult, op1=ALU.add)
                    STT(out=x[:, j, TS:TOK], in0=bank2(s)[:, 0:TP], scalar=modv[:, 40 + j, 1:2], in1=x[:, j, TS:TOK],
                        op0=ALU.mult, op1=ALU.add).then_inc(free[s], 1)

            first(0, 0, 16)
            with dve.Fori(0, NB // 2 - 1) as i:
                dve.wait_ge(free[3], base[3] + i * 8)
                first(i * 2 + 1, 1, i * 16 + 16)
                second(i * 2, 0, i * 16 + 16)
                first(i * 2 + 2, 0, i * 16 + 32)
                dve.wait_ge(free[3], base[3] + i * 8 + 4)
                second(i * 2 + 1, 1, i * 16 + 16)
            dve.wait_ge(free[3], base[3] + 4 * (NB - 2))
            first(NB - 1, 1, 8 * NB)
            second(NB - 2, 0, 8 * NB)
            dve.wait_ge(free[3], base[3] + 4 * (NB - 1))
            second(NB - 1, 1, 8 * NB)
            dve.wait_ge(free[3], base[3] + 4 * NB)
            sl.n = [base[s] + (2 * NB if s < 2 else 4 * NB) for s in range(4)]
            sl.r = 0
            mark().then_inc(x_ready, 8)
            TSC(amul[:, :, 0], V('normf', 0, 8), D ** 0.5, None, ALU.mult).then_inc(vch, 1)
            ch[0] += 1
            dve.wait_ge(vch, ch[0])
            g = sl.next()
            dve.wait_ge(free[g[0]], g[1])
            link(vv.reciprocal(rstd, rstd))
            for k in range(KD):
                STT(out=h[:, k, :], in0=x[:, k, :], scalar=amul[:, k, 0:1], in1=rstd, op0=ALU.mult, op1=ALU.mult)\
                    .then_inc(S("y_done"), 1)

        @block.gpsimd
        def _(pool):
            for t in range(NT):
                gT = map_slots['T'][t]
                pool.wait_ge(free[gT[0]], gT[1])
                for q in range(P // 4):
                    e = t * (P // 4) + q
                    n = e * 4
                    if e >= 2:
                        gp = map_slots['q'][e - 2]
                        pool.wait_ge(full[gp[0]], gp[1])
                    for i in range(4):
                        ins = nc.gpsimd.tensor_scalar(r_R[:, (n + i) % NOH, :], C('iota'),
                                                      r_T[:, t % 2, 1, q * 4 + i:q * 4 + i + 1], None, ALU.is_equal)
                    ins.then_inc(S("r_R"), 1)

        @block.sync
        def _(sp):
            sp.dma_start(vec[:], vec_in).then_inc(load, 16)
            sp.dma_start(cst[:], cst_in).then_inc(load, 16)
            sp.dma_start(lvl_f, lvl_in).then_inc(load, 16)
            sp.dma_start(wsm, wsm_in).then_inc(load, 16)
            sp.dma_start(rowv, rowv_in).then_inc(load, 16)
            loaded = 0
            for i in range(NSLAB):
                if i >= RING:
                    j = i - RING
                    if j < 23:
                        sp.wait_ge(S("mod_slab_used"), j + 1)
                    elif j in slab_last:
                        s, u = slab_last[j]
                        sp.wait_ge(full[s], u)
                    else:
                        break
                sp.dma_start(wring[:, i % RING, :], slabs[i]).then_inc(slab_in[i % RING], 16)
                loaded += 1
            mp = gmap.rearrange("b p q c n -> p q b c n")
            for hf in range(2 * NT):
                g = map_slots['q'][hf * 16 + 15]
                for gg in map_slots['q'][hf * 16 + 12:hf * 16 + 16]:
                    sp.wait_ge(free[gg[0]], gg[1])
                sp.dma_start(mp[:, hf].rearrange("p b c n -> p b (c n)"),
                             g_stage[:, hf % 2].rearrange("p (b c) n -> p b (c n)", c=4)).then_inc(map_out[hf % 2], 16)
            for m in map_out:
                sp.wait_ge(m, 16 * NT)
            base = map_slots['base']

            def block_loads(b, r):
                sp.dma_start(p_u[:, r].rearrange("p c k e -> p (c k e)"),
                             u_in[bass.ds(b, 1)].rearrange("o p c k e -> p (o c k e)")).then_inc(u_sem[r], 16)
                sp.dma_start(p_g[:, r].rearrange("p q c n -> p (q c n)"),
                             gmap[bass.ds(b, 1)].rearrange("o p q c n -> p (o q c n)")).then_inc(g_sem[r], 16)
                sp.dma_start(p_v[:, r].rearrange("p c d -> p (c d)"),
                             v_in[bass.ds(b, 1)].rearrange("o p c d -> p (o c d)")).then_inc(v_sem[r], 16)

            block_loads(0, 0)
            block_loads(1, 1)

            def refill(b, r):
                sp.wait_ge(full[1], base[1] + b * 2 - 2)
                sp.wait_ge(S("p_A"), b * 4 - 4)
                sp.dma_start(p_u[:, r].rearrange("p c k e -> p (c k e)"),
                             u_in[bass.ds(b, 1)].rearrange("o p c k e -> p (o c k e)")).then_inc(u_sem[r], 16)
                sp.dma_start(p_g[:, r].rearrange("p q c n -> p (q c n)"),
                             gmap[bass.ds(b, 1)].rearrange("o p q c n -> p (o q c n)")).then_inc(g_sem[r], 16)
                sp.wait_ge(full[3], base[3] + b * 4 - 4)
                sp.dma_start(p_v[:, r].rearrange("p c d -> p (c d)"),
                             v_in[bass.ds(b, 1)].rearrange("o p c d -> p (o c d)")).then_inc(v_sem[r], 16)

            with sp.Fori(1, NB // 2) as i:
                refill(i * 2, 0)
                refill(i * 2 + 1, 1)
            for r in range(RING):
                sp.wait_ge(slab_in[r], 16 * sum(1 for k in range(loaded) if k % RING == r))
            sp.wait_ge(stored, 16 * STORES[0])


def kernel(**inputs):
    import concourse.bacc as bacc
    from concourse.bass_utils import run_bass_kernel_spmd

    I = {k: np.ascontiguousarray(np.asarray(v)) for k, v in inputs.items()}
    f = np.float32

    def chan(v):
        return v.reshape(-1, P).T

    def slab_cols(w, c0, n):
        return [w[:, c0 + 256 * i:c0 + 256 * (i + 1)].reshape(KD, P, 256).transpose(1, 0, 2).reshape(P, SLAB)
                for i in range(n)]

    w_in, b_in = I['w_in'][0], I['b_in'][0]
    wb = I['w_branch'][0]
    sl = slab_cols(I['w_mod'][0], 0, 24)
    for name in ('a_q', 'a_k', 'a_v', 'a_o', 'b_q', 'b_i', 'b_g', 'b_f', 'c_q', 'c_k', 'c_v', 'c_g', 'd_x', 'd_g'):
        a, b = COL[name]
        sl += slab_cols(w_in, a, (b - a) // 256)
    gates = w_in[:, COL['gates'][0]:].reshape(KD, P, NBR, KD, P)
    for j in range(KD):
        gj = gates[:, :, :, j, :].transpose(1, 0, 2, 3)
        sl += [gj[:, :, 0:2].reshape(P, SLAB), gj[:, :, 2:4].reshape(P, SLAB)]
        sl.append(wb.reshape(NBR, 4, P, KD, P)[:, :, :, j, :].transpose(2, 0, 1, 3).reshape(P, SLAB))
    sl += slab_cols(I['w_out'][0], 0, 4)
    sl += slab_cols(I['peer_w_q'][0], 0, 8)
    slabs = np.stack(sl)
    assert len(slabs) == NSLAB

    quarter = D // 4
    omega = (f(1.0) / (f(10000.0) ** (np.arange(quarter, dtype=f) / f(quarter)))).astype(f)

    def enc(n):
        ang = np.arange(n, dtype=f)[None, :] * omega[:, None]
        return np.concatenate([np.sin(ang), np.cos(ang)], 0).astype(f)

    def ptab(n):
        return enc(n).reshape(4, P, n).transpose(1, 0, 2).reshape(P, 4 * n)

    def seg(name):
        return chan(b_in[COL[name][0]:COL[name][1]])

    parts = {
        'b_mod': chan(I['b_mod'][0]), 'norm1': chan(I['norm1_g'][0]), 'norm2': chan(I['norm2_g'][0]),
        'normf': chan(I['final_norm_g']), 'a_q': seg('a_q'), 'a_k': seg('a_k'), 'a_o': seg('a_o'),
        'b_q': seg('b_q'), 'b_f': seg('b_f'), 'b_g': seg('b_g'), 'c_q': seg('c_q'), 'c_k': seg('c_k'),
        'c_g': seg('c_g'), 'd_x': seg('d_x'), 'd_g': seg('d_g'), 'gates': seg('gates'),
        'b_up': chan(I['b_gla_up'][0].reshape(-1)), 'lb': chan(I['hgrn_lower_bounds'][0].reshape(-1)),
        'conv_w': chan(I['conv_w'][0].reshape(-1)), 'conv_b': chan(I['conv_b'][0]),
        'lru_b_a': chan(I['lru_b_a'][0].reshape(-1)), 'lru_b_x': chan(I['lru_b_x'][0].reshape(-1)),
        'lam': chan(I['lru_lambda'][0].reshape(-1)), 'h0': chan(I['state_lru_h'][0, 0].reshape(-1)),
        'n0': chan(I['state_mlstm_n'][0, 0].reshape(-1)),
        'cond': np.stack([chan(I['c'][0]), chan(I['c_ctx'])], 2).reshape(P, 16),
        'pos_r': ptab(TS // GRID_W), 'pos_c': ptab(GRID_W),
    }
    vec = np.concatenate([parts[n] for n in VEC], 1).astype(f)

    r = np.arange(P)
    reset0 = np.tile((r != 0).astype(f), NT)[None, :].repeat(P, 0)
    reset1 = np.tile((r != P - 1).astype(f), NT)[None, :].repeat(P, 0)
    sel = np.zeros((P, 4, P), f)
    for i in range(4):
        sel[i, i, :] = 1.0
    s_, t_ = r[:, None], r[None, :]
    csts = {
        'ident': np.eye(P, dtype=f), 'ones': np.ones((P, P), f), 'iota': np.broadcast_to(r.astype(f), (P, P)),
        'over0': np.where(s_ <= t_, 0, 1e30).astype(f), 'over1': np.where(s_ >= t_, 0, 1e30).astype(f),
        'reset0': reset0, 'reset1': reset1, 'sel': sel.reshape(P, -1),
        'jota': np.broadcast_to(np.arange(16, dtype=f), (P, 16)),
        'epsD': np.full((P, 1), D * EPS, f), 'epsP': np.full((P, 1), P * EPS, f),
    }
    cst = np.concatenate([csts[n] for n in CST], 1).astype(f)
    lv = np.zeros((P, 2, len(LEVELS), P), f)
    for i, w in enumerate(LEVELS):
        m = (s_ // (2 * w) == t_ // (2 * w)) & (s_ % (2 * w) < w) & (t_ % (2 * w) >= w)
        lv[:, 0, i], lv[:, 1, i] = m, m.T

    small = np.concatenate([w_in[:, COL[n][0]:COL[n][1]] for n in ('a_i', 'a_f', 'c_lr')], 1)
    wsm = small.reshape(KD, P, 48).transpose(1, 0, 2).reshape(P, KD * 48)
    rowv = np.zeros((16, 8), f)
    rowv[0:4, 0:2] = I['state_mlstm_m'][0, 0].T
    bi, bf = (b_in[COL[n][0]:COL[n][1]].reshape(2, 4) for n in ('a_i', 'a_f'))
    for d in range(2):
        rowv[0:4, 2 + 2 * d], rowv[0:4, 3 + 2 * d] = bi[d], bf[d]
    rowv[:, 6:8] = b_in[COL['c_lr'][0]:COL['c_lr'][1]].reshape(2, 16).T
    tokb = np.stack([np.broadcast_to(b_in[COL[n][0]:COL[n][1]], (P, W)) for n in ('a_v', 'b_i', 'c_v')])
    x = np.concatenate([I['x_sample'][0].T, I['x_prompt'][0].T], 1).reshape(KD, P, TOK).transpose(1, 0, 2)
    sc = I['state_gla_S'][0, 0].reshape(2, 2, 2, 64, P).transpose(2, 3, 0, 1, 4).reshape(P, 2, 2, P)
    lruw = np.stack([I['lru_w_a'][0], I['lru_w_x'][0]]).transpose(3, 0, 1, 2, 4)
    ex_u = I['peer_u'][0].reshape(NKEY, NKEY // 4, 4, KD, P).transpose(1, 4, 2, 3, 0)
    ex_v = I['peer_v'][0].reshape(NKEY, NKEY // 4, 4, D).transpose(1, 0, 2, 3)
    arrays = {
        'x': x, 'slabs': slabs, 'vec': vec, 'cst': cst, 'lvl': lv, 'wsm': wsm, 'rowv': rowv,
        'up': I['w_gla_up'][0].transpose(1, 0, 2), 'tokb': tokb,
        'c0': I['state_mlstm_C'][0, 0].transpose(2, 0, 1, 3), 's0b': I['state_hgrn_S'][0, 0].transpose(2, 0, 1, 3),
        's0c': sc, 'lruw': lruw, 'sk': I['peer_sub_keys'][0].reshape(16, P, P).transpose(2, 0, 1),
        'u': ex_u, 'v': ex_v,
    }
    nc = bacc.Bacc("TRN2", target_bir_lowering=False, num_devices=1)
    args, feed = [], {}
    for name, a in arrays.items():
        feed[name + '_in'] = np.ascontiguousarray(a)
        args.append(nc.dram_tensor(name + '_in', a.shape, mybir.dt.from_np(a.dtype), kind="ExternalInput").ap())
    outs = {'y': (P, KD, TOK), 'C': (8, P, P), 'n': (8, P, 1), 'm': (2, 4, 1), 'Sb': (8, P, P), 'Sc': (8, 64, P),
            'h': (8, P, 1)}
    for name, shape in outs.items():
        args.append(nc.dram_tensor(name + '_out', shape, F32, kind="ExternalOutput").ap())
    args.append(nc.dram_tensor('expert_map', (NKEY // 4, P, 2 * NT, 4, 64), F32, kind="Internal").ap())
    build_kernel(nc, *args)
    res = run_bass_kernel_spmd(nc, [feed], core_ids=[0]).results[0]
    y = np.asarray(res['y_out']).transpose(1, 0, 2).reshape(D, TOK)
    return (y[:, TS:].T[None], y[:, :TS].T[None], res['C_out'].reshape(1, 1, 2, 4, P, P),
            res['n_out'].reshape(1, 1, 2, 4, P), res['m_out'].reshape(1, 1, 2, 4),
            res['Sb_out'].reshape(1, 1, 2, 4, P, P), res['Sc_out'].reshape(1, 1, 2, 4, 64, P),
            res['h_out'].reshape(1, 1, 2, W))
```

```python
from contextlib import ExitStack

import numpy as np
import concourse.bass as bass
from concourse import mybir

F32 = mybir.dt.float32
F32R = mybir.dt.float32r
U32 = mybir.dt.uint32
U8 = mybir.dt.uint8
ALU = mybir.AluOpType
ACT = mybir.ActivationFunctionType
AX = mybir.AxisListType

P = 128
D = 1024
KD = D // P
TS, TP = 512, 128
TOK = TS + TP
NT = TOK // P
W = 512
HEADS = 4
HALF = TOK // 2
EPS = 1e-6
LEVELS = [64, 32, 16, 8, 4, 2, 1]
GRID_W = 64
NBR = 4
PH = 8
TOPK = 16
NKEY = 128
RING = 4
SLAB = KD * 256
NB = NKEY // 4
STAGES = ((0, 16, 4), (20, 16, 4), (40, 16, 4), (60, 16, 4), (80, 16, 4), (100, 16, 12))
assert sum(m + t for _, m, t in STAGES) == NKEY and len(STAGES) == NT + 1

SEG = (('a_q', 512), ('a_k', 512), ('a_v', 512), ('a_o', 512), ('a_i', 8), ('a_f', 8), ('b_q', 512), ('b_f', 1024),
       ('b_i', 512), ('b_g', 512), ('c_q', 256), ('c_k', 256), ('c_v', 512), ('c_g', 512), ('c_lr', 32),
       ('d_x', 512), ('d_g', 512), ('gates', 4096))
COL = {}
_at = 0
for _n, _w in SEG:
    COL[_n] = (_at, _at + _w)
    _at += _w

MOD1 = 8
SLABS = {}
_at = 0
for _n, _c in (('mod', MOD1), ('a_q', 2), ('a_k', 2), ('a_v', 2), ('a_o', 2), ('b_q', 2), ('b_i', 2), ('b_g', 2),
               ('b_f0', 2), ('mod0', 4), ('b_f1', 2), ('mod1', 4), ('c_q', 1), ('c_k', 1), ('c_v', 2), ('c_g', 2),
               ('mod2', 4), ('mod3', 4), ('d_x', 2), ('d_g', 2),
               ('merge', 24), ('w_out', 4), ('w_q', 8)):
    SLABS[_n] = _at
    _at += _c
NSLAB = _at

VEC = {}
_at = 0
for _n, _c in (('b_mod', 48), ('norm1', 8), ('norm2', 8), ('normf', 8), ('a_q', 4), ('a_k', 4), ('a_o', 4),
               ('b_q', 4), ('b_f', 8), ('b_g', 4), ('c_q', 2), ('c_k', 2), ('c_g', 4), ('d_x', 4), ('d_g', 4),
               ('gates', 32), ('b_up', 4), ('lb', 8), ('conv_w', 16), ('conv_b', 4), ('lru_b_a', 8),
               ('lru_b_x', 8), ('lam', 8), ('h0', 8), ('n0', 8), ('cond', 16), ('pos_r', 32), ('pos_c', 256)):
    VEC[_n] = (_at, _at + _c)
    _at += _c
NVEC = _at

CST = {}
_at = 0
for _n, _c in (('ident', 128), ('ones', 128), ('iota', 128), ('over0', 128), ('over1', 128), ('reset0', 640),
               ('reset1', 640), ('sel', 512), ('jota', 16), ('epsD', 1), ('epsP', 1)):
    CST[_n] = (_at, _at + _c)
    _at += _c
NCST = _at


def mod_of(ntile, j):
    return ntile * KD + j


def build_kernel(nc, x_in, slabs, vec_in, cst_in, lvl_in, wsm_in, rowv_in, up_in, tokb_in, c0_in, s0b_in, s0c_in,
                 lruw_in, sk_in, u_in, v_in, y_out, c_out, n_out, m_out, sb_out, sc_out, h_out, gmap, tmap, xpark):
    with ExitStack() as ctx:
        def sem(name):
            return ctx.enter_context(nc.semaphore(name))

        def sb(name, shape, dt=F32):
            return ctx.enter_context(nc.sbuf_tensor(name, shape, dt))

        ps = ctx.enter_context(nc.psum_tensor("ps", [P, 8, 512], F32))

        def at(name, word, shape, dt=F32):
            return nc.alloc_sbuf_tensor_at(name, shape, dt, offset=at0 + 4 * word)

        x = sb("x", [P, KD, TOK])
        at0 = nc.sbuf_base - 4 * KD * TOK
        h = sb("h", [P, KD, TOK])
        ybr = sb("ybr", [P, NBR, HEADS, TOK])
        wring = sb("wring", [P, RING, SLAB])
        work = sb("work", [P, 20750])
        assert nc.sbuf_base - at0 - 4 * (28672 + 20750) < 128
        vec = sb("vec", [P, NVEC])
        cst = sb("cst", [P, NCST])
        lvl = sb("lvl", [P, 2, len(LEVELS), P], U8)
        modv = sb("modv", [P, 48, 2])
        cs = sb("cs", [P, KD, 2])
        amul = sb("amul", [P, KD, 2])
        small = sb("small", [P, 64])
        scr = sb("scr", [P, 128])

        def V(name, j=0, n=1):
            return vec[:, VEC[name][0] + j:VEC[name][0] + j + n]

        def C(name):
            return cst[:, CST[name][0]:CST[name][1]]

        ident, ones = C('ident'), C('ones')
        cepsD, cepsP = C('epsD'), C('epsP')

        class Carve:
            def __init__(self, base, size):
                self.base, self.at, self.size = base, 0, size

            def take(self, n, part=P):
                a = self.base[0:part, self.at:self.at + n]
                self.at += n
                assert self.at <= self.size, self.at
                return a

        y2 = ybr[:].rearrange("p n h t -> p n (h t)")

        def gl_memory(J):
            lo = Carve(work, 5760)
            hi = Carve(work[:, 6152:], 20750 - 6152)
            m = {'J': J, 'X': [lo.take(J * TOK) for _ in range(2)], 'dec': work[:, 5120:5120 + J * NT]}
            m['q'] = hi.take(J * TOK)
            m['k'] = hi.take(J * TOK)
            m['b'] = hi.take(J * TOK)
            m['P'] = hi.take(NT * W).rearrange("p (n c) -> p n c", n=NT)
            m['v'] = hi.take(NT * W).rearrange("p (n c) -> p n c", n=NT)
            m['kT'] = [hi.take(J * P) for _ in range(2)]
            m['hi'] = hi
            src = Carve(y2[:, 2, :], 2560) if J == 4 else hi
            m['S'] = src.take(2 * J * P).rearrange("p (d j e) -> p d j e", d=2, j=J)
            m['Snew'] = src.take(2 * J * P).rearrange("p (d j e) -> p d j e", d=2, j=J)
            m['vb'] = src.take(512)
            m['o'] = y2[:, 3, :].rearrange("p (h t) -> p h t", h=4)
            return m

        mB, mC = gl_memory(4), gl_memory(2)
        c_lr = mC['hi'].take(2 * TOK, 16).rearrange("p (d t) -> p d t", d=2)
        c_up = mC['hi'].take(512, 16).rearrange("p (d c) -> p d c", d=2)
        lbw = work[:, 5200:5232]

        def rows(J, hh):
            return (hh, slice(0, P)) if J == 4 else (hh // 2, slice((hh % 2) * 64, (hh % 2) * 64 + 64))

        def place(J, hh):
            return hh if J == 4 else (hh % 2) * 2 + hh // 2

        def head_out(J, g, hh):
            if J == 4:
                return ps[:, 2 * g[0], hh * P:(hh + 1) * P]
            return ps[:, 2 * g[0] + hh % 2, (hh // 2) * P:(hh // 2 + 1) * P]

        def heads_psum(J, g):
            if J == 4:
                return ps[:, 2 * g[0], :].rearrange("p (h t) -> p h t", t=P)
            return ps[:, 2 * g[0]:2 * g[0] + 2, 0:2 * P].rearrange("p a (j t) -> p a j t", t=P)

        def heads_row(J, ap):
            return ap.rearrange("p (h t) -> p h t", t=P) if J == 4 else ap.rearrange("p (a j t) -> p a j t", t=P, a=2)

        def heads_same(J, ap):
            if J == 4:
                return ap.unsqueeze(1).to_broadcast([P, 4, P])
            return ap.unsqueeze(1).unsqueeze(1).to_broadcast([P, 2, 2, P])

        def tiles_of(d):
            return ([0, 1, 2, 3] if d == 0 else [3, 2, 1, 0]) + [4]

        dk = Carve(work, 20750)
        d_x, d_xd, d_R, d_U, d_T, d_Q, d_H = (dk.take(2560).rearrange("p (h t) -> p h t", h=4) for _ in range(7))
        d_w = dk.take(2048).rearrange("p (w d h j) -> p w d h j", w=2, d=2, h=4)
        d_new = dk.take(8)
        d_spl = dk.take(8)
        d_tmp = dk.take(8)
        d_nspl = dk.take(8)

        mrg = work[:, 6152:11272].rearrange("p (k t) -> p k t", k=KD)
        m_sg = work[:, 11272:12552].rearrange("p (r t) -> p r t", r=2)
        m_tmp = work[:, 12552:13192]

        r_sk = work[:, 13192:15240].rearrange("p (g e) -> p g e", g=16)
        r_qT = work[:, 15240:16520].rearrange("p (r t) -> p r t", r=2)
        r_s = ybr[:].rearrange("p n h t -> p (n h t)").rearrange("p (n g e) -> p n g e", n=NT, g=16)
        rk = Carve(at("routing", 20480, [P, 9104])[:], 9104)
        r_v = rk.take(256).rearrange("p (g k) -> p g k", g=16)
        r_i = rk.take(256).bitcast(U32).rearrange("p (g k) -> p g k", g=16)
        r_if = rk.take(256).rearrange("p (g k) -> p g k", g=16)
        r_s2 = rk.take(256)
        r_c = rk.take(2048).rearrange("p (h c) -> p h c", h=PH)
        r_t = rk.take(128).rearrange("p (h k) -> p h k", h=PH)
        r_p = rk.take(128).bitcast(U32).rearrange("p (h k) -> p h k", h=PH)
        r_ab = rk.take(256).bitcast(U32).rearrange("p (w c) -> p w c", w=2)
        r_abf = rk.take(256).rearrange("p (w c) -> p w c", w=2)
        r_e = rk.take(384).rearrange("p (w c) -> p w c", w=3)
        r_sum = rk.take(16)
        r_T = rk.take(768).rearrange("p (r w c) -> p r w c", r=2, w=3)
        NOH = 16
        r_L = rk.take(NOH * P).rearrange("p (r c) -> p r c", r=NOH)
        r_R = rk.take(NOH * P).rearrange("p (r c) -> p r c", r=NOH)
        QT = 32
        g_stage = at("map_stage", 41104, [P, 2, P, QT])
        g_one = r_c.rearrange("p h c -> p (h c)")

        e_h = at("expert_h", 0, [P, 2, KD, TOK], F32R)
        e_u = at("expert_u_parts", 31632, [P, 4, 2, D], F32R)
        e_uraw = at("expert_u", 29584, [P, 2, D])
        e_t = at("activations", 39824, [P, 2, TOK])
        e_w = at("weight_parts", 45192, [P, 2, 2, D], F32R)
        e_a = at("expert_a_parts", 5120, [P, 2, 2, 4 * TOK], F32R)
        e_T = at("activations_back", 15360, [P, 2, 4 * TOK])
        e_G = at("map_back", 20480, [P, 2, 4 * TOK])
        e_vraw = at("expert_v", 25600, [P, 4, D])
        e_v = at("expert_v_parts", 29696, [P, 2, 2, 4, D], F32R)
        PARTS = ((0, 0), (1, 0), (0, 1))

        marks = [0]

        def mark():
            marks[0] += 1
            return nc.vector.memset(scr[:, marks[0] - 1:marks[0]], 0.0)

        full = [sem(f"psum_full{i}") for i in range(4)]
        free = [sem(f"psum_free{i}") for i in range(4)]
        slab_in = [sem(f"slab_in{i}") for i in range(RING)]
        load = sem("loaded")
        load_x = sem("loaded_x")
        phase_v, phase_a = sem("phase_vector"), sem("phase_scalar")
        vch, ach = sem("vector_chain"), sem("scalar_chain")
        silu_done = sem("cond_silu_done")
        x_ready = sem("x_ready")
        sq_done = sem("squares_done")
        hm_done = sem("h_scaled")
        h_done = sem("h_ready")
        stored = sem("stored")
        phload = sem("phase_loads")
        names = {}

        def S(name):
            if name not in names:
                names[name] = sem(name)
            return names[name]

        class Slots:
            def __init__(self):
                self.n, self.r = [0] * 4, 0

            def next(self, among=(0, 1, 2, 3)):
                s = among[self.r % len(among)]
                self.r += 1
                self.n[s] += 1
                return s, self.n[s]

        def halves(slot):
            return ps[:, 2 * slot:2 * slot + 2, 0:HALF]

        def two(ap):
            return ap.rearrange("p (a b) -> p a b", a=2)

        def bank(slot):
            return ps[:, 2 * slot, :]

        def bank2(slot):
            return ps[:, 2 * slot + 1, :]

        slab_last = {}

        def half_of(m):
            if m < KD * NBR:
                return SLABS['merge'] + 3 * (m // NBR) + m % NBR // 2, m % 2 * P
            return SLABS['w_q'] + (m - KD * NBR) // 2, m % 2 * P

        def slab(i):
            return wring[:, i % RING, :].rearrange("p (k c) -> p k c", k=KD)

        lvl_f = ybr[:, 0].rearrange("p h t -> p (h t)")[:, 0:2 * len(LEVELS) * P]\
            .rearrange("p (d l t) -> p d l t", d=2, l=len(LEVELS))

        wk = Carve(work, 20750)
        sq = wk.take(5120).rearrange("p (k t) -> p k t", k=KD)
        rstd = wk.take(TOK)
        wsm = wk.take(KD * 48).rearrange("p (k c) -> p k c", k=KD)

        wk = Carve(work, 20750)
        wk.take(5120 + TOK)
        wk.take(KD * 48)
        rowv = wk.take(8, 16)
        a_q = wk.take(2560).rearrange("p (h t) -> p h t", h=4)
        a_k = wk.take(2560).rearrange("p (h t) -> p h t", h=4)
        a_v = wk.take(2560).rearrange("p (n c) -> p n c", n=NT)
        a_C0 = wk.take(1024).rearrange("p (d h e) -> p d h e", d=2, h=4)
        a_kT = wk.take(512)
        a_gc = wk.take(40).rearrange("p (d n h) -> p d n h", d=2, n=NT)
        a_st = wk.take(8 * 129).rearrange("p (g e) -> p g e", g=8)
        a_E = wk.take(1280).rearrange("p (r t) -> p r t", r=2)
        a_P = wk.take(1280).rearrange("p (r t) -> p r t", r=2)
        a_o = y2[:, 0, :].rearrange("p (h t) -> p h t", h=4)
        a_ha = y2[:, 1, :].rearrange("p (h t) -> p h t", h=4)
        yk = Carve(y2[:, 2, :], 2560)
        a_rI = yk.take(1280, 4).rearrange("p (d t) -> p d t", d=2)
        a_rF = yk.take(1280, 4).rearrange("p (d t) -> p d t", d=2)
        wk2 = Carve(work, 5120)
        a_rG = wk2.take(1280, 4).rearrange("p (d t) -> p d t", d=2)
        a_rM = wk2.take(1280, 4).rearrange("p (d t) -> p d t", d=2)
        a_rFl = wk2.take(1280, 4).rearrange("p (d t) -> p d t", d=2)
        a_rW = wk2.take(1280, 4).rearrange("p (d t) -> p d t", d=2)
        yk = Carve(y2[:, 3, :], 2560)
        a_Mb = yk.take(640)
        a_Fb = yk.take(640)
        a_D = yk.take(640)
        a_qt = yk.take(512)
        a_n0 = yk.take(128)
        wk3 = Carve(work[:, 5120:5760], 640)
        a_dm = wk3.take(256).rearrange("p (r t) -> p r t", r=2)
        a_kw = wk3.take(128)
        a_vb = wk.take(512)
        a_T = wk.take(640)

        def a_range(d, i):
            if i == 4:
                return TS, TOK
            return (i * P, TS) if d == 0 else (0, (i + 1) * P)

        num, den = 2, 3

        def head_roots(sl, got):
            for hh in range(HEADS):
                g = sl.next((0, 1))
                got(g)
                nc.scalar.activation(two(sq[:, 4 + hh, :]), halves(g[0]), ACT.Sqrt, bias=cepsP)\
                    .then_inc(free[g[0]], 1)

        def head_norm(dve, link, g, val, gate, r, t):
            vv = nc.vector
            dve.wait_ge(free[g[0]], g[1])
            link(vv.reciprocal(r, r))
            link(vv.scalar_tensor_tensor(out=t, in0=r, scalar=P ** 0.5, in1=val, op0=ALU.mult, op1=ALU.mult))
            link(vv.tensor_tensor(gate, gate, t, ALU.mult))

        STORES = [0]
        LOADS = {'B': 4, 'C': 7, 'D': 8, 'sk': 9}
        map_slots = {}
        u_sem, t_sem, g_sem = ([sem(f'{n}_in{i}') for i in range(2)] for n in ('expert_u', 'activations', 'map'))
        v_sem = [sem(f'expert_v_in{i}') for i in range(4)]
        t_out = [sem(f'activations_out{i}') for i in range(2)]
        map_out = [sem(f'map_out{i}') for i in range(2)]
        block = ctx.enter_context(nc.Block())

        def group_use(t, q, before):
            e = t * 32 + q - before
            t, q = e // 32, e % 32
            return map_slots['base'][2 + q % 2] + (17 * t + 1 if q % 2 == 0 else 16 * t) + q // 2 + 1

        def phase(eng, k):
            eng.wait_ge(phase_v, k)
            eng.wait_ge(phase_a, k)

        @block.tensor
        def _(pe):
            sl = Slots()

            def slab_wait(i):
                pe.wait_ge(slab_in[i % RING], 16 * (i // RING + 1))

            def claim(g):
                if g[1] > 1:
                    pe.wait_ge(free[g[0]], g[1] - 1)

            def wide(g, pairs, m=P):
                claim(g)
                for a in range(2):
                    for i, (lhs, rhs) in enumerate(pairs):
                        mm = nc.tensor.matmul(ps[0:m, 2 * g[0] + a, 0:HALF], lhs, rhs[:, a * HALF:(a + 1) * HALF],
                                              start=(i == 0), stop=(i == len(pairs) - 1))
                mm.then_inc(full[g[0]], 1)

            def project(name, base=0, n=None):
                for c in range(n):
                    i = SLABS[name] + (base + c) // 2
                    slab_wait(i)
                    w = slab(i)
                    o = ((base + c) % 2) * P
                    g = sl.next()
                    wide(g, [(w[:, k, o:o + P], h[:, k, :]) for k in range(KD)])
                    slab_last[i] = g

            def wide_parts(g, m, ready=None):
                claim(g)
                pe.wait_ge(S("w_rounded"), m + 1)
                pe.wait_ge(S("w_rest"), m + 1)
                for a in range(2):
                    for k in range(KD):
                        if ready and not a:
                            ready(k)
                        for i, (wp, dp) in enumerate(PARTS):
                            mm = nc.tensor.matmul(ps[:, 2 * g[0] + a, 0:HALF], e_w[:, m % 2, wp, k * P:(k + 1) * P],
                                                  e_h[:, dp, k, a * HALF:(a + 1) * HALF], start=(k == 0 and i == 0),
                                                  stop=(k == KD - 1 and i == 2))
                mm.then_inc(full[g[0]], 1)

            def project_tok(name):
                for c in range(2):
                    i = SLABS[name] + c
                    slab_wait(i)
                    for t in range(NT):
                        g = sl.next()
                        claim(g)
                        for k in range(KD):
                            mm = nc.tensor.matmul(bank(g[0])[:, 0:256], h[:, k, t * P:(t + 1) * P], slab(i)[:, k, :],
                                                  start=(k == 0), stop=(k == KD - 1))
                        mm.then_inc(full[g[0]], 1)
                        slab_last[i] = g

            def norm_sum(base):
                g = sl.next()
                claim(g)
                for k in range(KD):
                    pe.wait_ge(sq_done, base + k + 1)
                    for a in range(2):
                        mm = nc.tensor.matmul(ps[:, 2 * g[0] + a, 0:HALF], ones, sq[:, k, a * HALF:(a + 1) * HALF],
                                              start=(k == 0), stop=(k == KD - 1))
                mm.then_inc(full[g[0]], 1)

            pe.wait_ge(load, 16 * 5)
            pe.wait_ge(silu_done, 1)
            g = sl.next()
            for c in range(2 * MOD1):
                i = SLABS['mod'] + c // 2
                slab_wait(i)
                for k in range(KD):
                    mm = nc.tensor.matmul(bank(g[0])[:, 2 * c:2 * c + 2], slab(i)[:, k, (c % 2) * P:(c % 2) * P + P],
                                          cs[:, k, :], start=(k == 0), stop=(k == KD - 1))
                if c % 2 and c < 2 * MOD1 - 1:
                    mm.then_inc(S("mod_slab_used"), 1)
            mm.then_inc(full[g[0]], 1)
            slab_last[MOD1 - 1] = g
            norm_sum(0)
            pe.wait_ge(h_done, 16)

            project('a_q', 0, 4)
            project('a_k', 0, 4)
            project_tok('a_v')
            project('a_o', 0, 4)
            for d in range(2):
                for which in range(2):
                    g = sl.next()
                    o = which * 8 + d * 4
                    wide(g, [(wsm[:, k, o:o + 4], h[:, k, :]) for k in range(KD)], m=4)
            g = sl.next()
            claim(g)
            pe.wait_ge(S("a_k_ready"), 4)
            for hh in range(4):
                mm = nc.tensor.transpose(bank(g[0])[:, hh * P:(hh + 1) * P], a_k[:, hh, TS:TOK], ident)
            mm.then_inc(full[g[0]], 1)
            g = sl.next()
            claim(g)
            pe.wait_ge(S("a_rows_g"), 1)
            for d in range(2):
                for t in range(NT):
                    o = (d * NT + t) * 4
                    mm = nc.tensor.matmul(bank(g[0])[:, o:o + 4], a_rG[:, d, t * P:(t + 1) * P], ident[0:4, 0:4],
                                          start=True, stop=True)
            mm.then_inc(full[g[0]], 1)
            pe.wait_ge(S("a_rows_w"), 1)
            pe.wait_ge(S("a_v_ready"), 2 * NT)
            pe.wait_ge(S("a_q_ready"), 4)
            for s in (2, 3):
                pe.wait_ge(free[s], sl.n[s])
            sl.r = 0
            num, den = 2, 3
            for d in range(2):
                for hh in range(4):
                    n = d * 4 + hh
                    sel = cst[0:4, CST['sel'][0] + hh * P:CST['sel'][0] + (hh + 1) * P]
                    g = sl.next((0, 1))
                    claim(g)
                    nc.tensor.matmul(bank(g[0]), sel, a_rW[:, d, 0:TS], start=True, stop=True).then_inc(full[g[0]], 1)
                    for r in (a_rM, a_rFl):
                        g = sl.next((0, 1))
                        wide(g, [(sel, r[:, d, :])])
                    if n:
                        pe.wait_ge(S("a_nd_read"), n)
                    pe.wait_ge(S("a_qt_ready"), n + 1)
                    pe.wait_ge(S("a_n0_ready"), n + 1)
                    nc.tensor.matmul(bank(num), a_C0[:, d, hh, :], a_qt, start=True, stop=False)
                    nc.tensor.matmul(bank(den), a_n0, a_qt, start=True, stop=False).then_inc(S("a_state_used"), 1)
                    order = ([0, 1, 2, 3] if d == 0 else [3, 2, 1, 0]) + [4]

                    def pv(idx, gs):
                        i = order[idx]
                        lo, hi = a_range(d, i)
                        pe.wait_ge(free[gs[0]], gs[1])
                        it = n * 5 + idx
                        po = a_P[:, it % 2, lo:hi]
                        if i < 4:
                            onum, oden = bank(num)[:, lo:hi], bank(den)[:, lo:hi]
                        else:
                            onum, oden = bank2(num)[:, 0:P], bank2(den)[:, 0:P]
                        nc.tensor.matmul(onum, a_v[:, i, hh * P:(hh + 1) * P], po, start=(i == 4), stop=(idx >= 3))
                        nc.tensor.matmul(oden, ones, po, start=(i == 4), stop=(idx >= 3)).then_inc(S("a_pv"), 1)

                    prev = None
                    for idx, i in enumerate(order):
                        lo, hi = a_range(d, i)
                        g = sl.next((0, 1))
                        claim(g)
                        nc.tensor.matmul(bank(g[0])[:, 0:hi - lo], a_k[:, hh, i * P:(i + 1) * P], a_q[:, hh, lo:hi],
                                         start=True, stop=True).then_inc(full[g[0]], 1)
                        if prev is not None:
                            pv(idx - 1, prev)
                        prev = g
                    pv(4, prev)
                    g = sl.next((0, 1))
                    claim(g)
                    pe.wait_ge(S("a_kw_ready"), n + 1)
                    nc.tensor.matmul(bank(g[0])[:, 0:P], a_kw, a_v[:, 4, hh * P:(hh + 1) * P], start=True, stop=True)
                    nc.tensor.matmul(bank(g[0])[:, P:P + 1], a_kw, ones[:, 0:1], start=True, stop=True)\
                        .then_inc(full[g[0]], 1)
            for hh in range(4):
                pe.wait_ge(S("a_sq"), hh + 1)
                g = sl.next((0, 1))
                wide(g, [(ones, sq[:, hh, :])])

            def gl_core(m, n):
                J, d = m['J'], n % 2
                g = sl.next()
                claim(g)
                for c in range(8):
                    i = SLABS[f'mod{n}'] + c // 2
                    slab_wait(i)
                    for k in range(KD):
                        mm = nc.tensor.matmul(bank(g[0])[:, 2 * c:2 * c + 2], slab(i)[:, k, (c % 2) * P:(c % 2) * P + P],
                                              cs[:, k, :], start=(k == 0), stop=(k == KD - 1))
                    slab_last[i] = g
                mm.then_inc(full[g[0]], 1)
                t_ = lambda ap, j, t: ap[:, j * TOK + t * P:j * TOK + (t + 1) * P]
                pe.wait_ge(S("g_in"), n + 1)
                level_used = map_slots.setdefault('levels', [])
                for t in range(NT):
                    g = sl.next()
                    claim(g)
                    for hh in range(HEADS):
                        j, r = rows(J, hh)
                        mm = nc.tensor.matmul(head_out(J, g, hh), t_(m['k'], j, t)[r],
                                              t_(m['q'], j, t)[r], start=True, stop=True)
                    mm.then_inc(full[g[0]], 1)
                for li in range(len(LEVELS)):
                    pe.wait_ge(S("g_X"), n * 9 + li + 1)
                    for t in range(NT):
                        g = sl.next()
                        claim(g)
                        for hh in range(HEADS):
                            j, r = rows(J, hh)
                            xt = t_(m['X'][li % 2], j, t)[r]
                            mm = nc.tensor.matmul(head_out(J, g, hh), xt, xt, start=True, stop=True)
                        mm.then_inc(full[g[0]], 1)
                    level_used.append(g)
                glast = g
                pe.wait_ge(S("g_X"), n * 9 + 9)
                pe.wait_ge(free[glast[0]], glast[1])
                for idx, t in enumerate(tiles_of(d)):
                    gt = sl.next()
                    claim(gt)
                    for j in range(J):
                        mm = nc.tensor.transpose(bank(gt[0])[:, j * P:(j + 1) * P], t_(m['X'][0], j, t), ident)
                    mm.then_inc(full[gt[0]], 1)
                    g = sl.next()
                    claim(g)
                    if 0 < idx < 4:
                        pe.wait_ge(free[gk[0]], gk[1])
                    for hh in range(HEADS):
                        j, r = rows(J, hh)
                        mm = nc.tensor.matmul(head_out(J, g, hh), m['v'][:, t, hh * P:(hh + 1) * P],
                                              m['P'][:, t, place(J, hh) * P:(place(J, hh) + 1) * P], start=True, stop=(t == 4))
                        if t < 4:
                            mm = nc.tensor.matmul(head_out(J, g, hh), m['S'][r, d, j, :],
                                                  t_(m['X'][1], j, t)[r], start=False, stop=True)
                    mm.then_inc(full[g[0]], 1)
                    if idx != 3:
                        gk = sl.next()
                        claim(gk)
                        pe.wait_ge(free[gt[0]], gt[1])
                        for hh in range(HEADS):
                            j, r = rows(J, hh)
                            mm = nc.tensor.matmul(bank(gk[0])[:, hh * P:(hh + 1) * P],
                                                  m['kT'][idx % 2][:, j * P:(j + 1) * P],
                                                  m['v'][:, t, hh * P:(hh + 1) * P], start=True, stop=True)
                        mm.then_inc(full[gk[0]], 1)

            sl.r = 0
            project('b_q', 0, 4)
            phase(pe, 1)
            project_tok('b_i')
            project('b_g', 0, 4)
            for d in range(2):
                project(f'b_f{d}', 0, 4)
                gl_core(mB, d)
            for hh in range(HEADS):
                pe.wait_ge(S("g_sq"), hh + 1)
                wide(sl.next((0, 1)), [(ones, sq[:, hh, :])])
            sl.r = 0
            project('c_q', 0, 2)
            project('c_k', 0, 2)
            phase(pe, 2)
            project_tok('c_v')
            project('c_g', 0, 4)
            for d in range(2):
                wide(sl.next(), [(wsm[:, k, 16 + 16 * d:32 + 16 * d], h[:, k, :]) for k in range(KD)], m=16)
            for d in range(2):
                pe.wait_ge(S("c_lr"), 1)
                for j in range(2):
                    wide(sl.next(), [(c_up[:, d, j * P:(j + 1) * P], c_lr[:, d, :])])
                gl_core(mC, 2 + d)
            for hh in range(HEADS):
                pe.wait_ge(S("g_sq"), 4 + hh + 1)
                wide(sl.next((0, 1)), [(ones, sq[:, hh, :])])
            sl.r = 0
            project('d_x', 0, 4)
            phase(pe, 3)
            project('d_g', 0, 4)
            map_slots['h_read'] = slab_last[SLABS['d_g'] + 1]
            pe.wait_ge(S("d_conv"), 1)
            for d in range(2):
                for hh in range(HEADS):
                    for w in range(2):
                        wide(sl.next(), [(d_w[:, w, d, hh, :], d_xd[:, hh, :])])
            phase(pe, 4)
            sl.r = 0
            pe.wait_ge(S("h1_rest"), 1)
            for j in range(KD):
                s0 = SLABS['merge'] + 3 * j
                wb = wring[:, (s0 + 2) % RING, :].rearrange("p (k c) -> p k c", k=16)
                for n in range(NBR):
                    g = sl.next()
                    wide_parts(g, 4 * j + n)
                    slab_last[s0 + n // 2] = g
                    slab_wait(s0 + 2)
                    g = sl.next()
                    wide(g, [(wb[:, 4 * n + k, :], ybr[:, n, k, :]) for k in range(HEADS)])
                    slab_last[s0 + 2] = g

            def wide2(g, pairs):
                claim(g)
                for o, lo, hi in ((bank(g[0]), 0, TS), (bank2(g[0])[:, 0:TP], TS, TOK)):
                    for i, (lhs, rhs) in enumerate(pairs):
                        mm = nc.tensor.matmul(o, lhs, rhs[:, lo:hi], start=(i == 0), stop=(i == len(pairs) - 1))
                mm.then_inc(full[g[0]], 1)

            for j in range(KD):
                i = SLABS['w_out'] + j // 2
                slab_wait(i)
                g = sl.next()
                pe.wait_ge(S("m_done"), 8)
                wide2(g, [(slab(i)[:, k, (j % 2) * P:(j % 2) * P + P], mrg[:, k, :]) for k in range(KD)])
                slab_last[i] = g
            norm_sum(8)
            sl.r = 0

            def score(hp, gq):
                g = sl.next()
                claim(g)
                pe.wait_ge(free[gq[0]], gq[1])
                for t in range(NT):
                    o = bank(g[0])[:, t * P:(t + 1) * P] if t < 4 else bank2(g[0])[:, 0:P]
                    mm = nc.tensor.matmul(o, r_qT[:, hp % 2, t * P:(t + 1) * P], r_sk[:, hp, :], start=True, stop=True)
                mm.then_inc(full[g[0]], 1)

            gq = None
            pe.wait_ge(phload, 16 * LOADS['sk'])
            for hp in range(16):
                i = SLABS['w_q'] + hp // 2
                g = sl.next()
                wide_parts(g, KD * NBR + hp, None if hp else lambda k: pe.wait_ge(S("h2_rest"), k + 1))
                slab_last[i] = g
                if gq:
                    score(hp - 1, gq)
                gq = g
            score(15, gq)
            for s in (0, 1, 2, 3):
                pe.wait_ge(free[s], sl.n[s])
            base = list(sl.n)
            map_slots['base'] = base

            def first(c, use, r):
                s = r % 2
                pe.wait_ge(free[s], base[s] + use)
                pe.wait_ge(S("u_rounded"), c + 1)
                pe.wait_ge(S("u_rest"), c + 1)
                for a in range(2):
                    for i, (wp, dp) in enumerate(PARTS):
                        for k in range(KD):
                            mm = nc.tensor.matmul(ps[:, 2 * s + a, 0:HALF], e_u[:, r, wp, k * P:(k + 1) * P],
                                                  e_h[:, dp, k, a * HALF:(a + 1) * HALF], start=(i == 0 and k == 0),
                                                  stop=(i == 2 and k == KD - 1))
                mm.then_inc(full[s], 1)

            for st, (c0, main, tail) in enumerate(STAGES):
                if st:
                    t = st - 1
                    pe.wait_ge(S("r_e"), t + 1)
                    pe.wait_ge(free[2], base[2] + 17 * t)
                    for w in range(3):
                        mm = nc.tensor.transpose(bank(2)[:, w * P:(w + 1) * P], r_e[:, w, :], ident)
                    mm.then_inc(full[2], 1)
                with pe.Fori(0, main // 4) as i:
                    for r in range(4):
                        first(i * 4 + (c0 + r), i * 2 + (c0 // 2 + r // 2), r)
                        if not st:
                            continue
                        for gi in (2 * r, 2 * r + 1):
                            s = 2 + gi % 2
                            use = (17 * t + 1 if s == 2 else 16 * t) + gi // 2
                            pe.wait_ge(free[s], i * 4 + (base[s] + use))
                            pe.wait_ge(S("r_L"), i * 8 + (32 * t + gi + 1))
                            pe.wait_ge(S("r_R"), i * 8 + (32 * t + gi + 1))
                            for n in range(4):
                                o = (4 * gi + n) % NOH
                                mm = nc.tensor.matmul(bank(s)[:, n * P:(n + 1) * P], r_L[:, o, :], r_R[:, o, :],
                                                      start=True, stop=True)
                            mm.then_inc(full[s], 1)
                with pe.Fori(main // 4, (main + tail) // 4) as i:
                    for r in range(4):
                        first(i * 4 + (c0 + r), i * 2 + (c0 // 2 + r // 2), r)
            base = [base[0] + 64, base[1] + 64, base[2] + 17 * NT, base[3] + 16 * NT]
            map_slots['base2'] = base

            def second(b, use, r):
                pe.wait_ge(S("a_rest"), b + 1)
                for j in range(KD):
                    s = j % 4
                    pe.wait_ge(free[s], use + (base[s] + j // 4))
                    for a in range(2):
                        for c in range(4):
                            if j == 0 and a == 0:
                                pe.wait_ge(S(f"v_rest{c}"), b + 1)
                            for i, (wp, dp) in enumerate(PARTS):
                                o = c * TOK + a * HALF
                                mm = nc.tensor.matmul(ps[:, 2 * s + a, 0:HALF], e_v[:, r, wp, c, j * P:(j + 1) * P],
                                                      e_a[:, r, dp, o:o + HALF],
                                                      start=(c == 0 and i == 0), stop=(c == 3 and i == 2))
                    mm.then_inc(full[s], 1)

            with pe.Fori(0, NB // 2) as i:
                for r in range(2):
                    second(i * 2 + r, i * 4 + 2 * r, r)
            sl.n = [base[s] + 2 * NB for s in range(4)]
            sl.r = 0
            norm_sum(16)

        @block.scalar
        def _(act):
            sl = Slots()
            ch = [0]

            def link(ins):
                ch[0] += 1
                ins.then_inc(ach, 1)
                act.wait_ge(ach, ch[0])

            def got(g):
                act.wait_ge(full[g[0]], g[1])

            A = nc.scalar.activation
            act.wait_ge(load, 16 * 5)
            act.dma_start(x[:], x_in).then_inc(load_x, 16)
            act.dma_start(a_C0, c0_in).then_inc(phload, 16)
            act.dma_start(a_vb, tokb_in[0]).then_inc(phload, 16)
            A(cs[:], V('cond', 0, 16).rearrange("p (k g) -> p k g", g=2), ACT.Silu).then_inc(silu_done, 1)
            sl.next()

            def norm_scalar(m, shift):
                for k in range(KD):
                    act.wait_ge(x_ready, 8 * m + k + 1)
                    A(sq[:, k, :], x[:, k, :], ACT.Square).then_inc(sq_done, 1)
                act.dma_start(xpark, x[:]).then_inc(S("x_parked"), 16)
                g = sl.next()
                got(g)
                A(two(rstd), halves(g[0]), ACT.Sqrt, bias=cepsD).then_inc(free[g[0]], 1)
                for k in range(KD):
                    for gq, (lo, hi) in enumerate(((0, TS), (TS, TOK))):
                        act.wait_ge(hm_done, 16 * m + 2 * k + gq + 1)
                        A(h[:, k, lo:hi], h[:, k, lo:hi], ACT.Identity, bias=modv[:, shift + k, gq:gq + 1])\
                            .then_inc(h_done, 1)
                    if m and k:
                        round_h2(k - 1)
                if m:
                    round_h2(KD - 1)

            def round_h2(k):
                if k == 0:
                    act.wait_ge(S("x_parked"), 32)
                act.wait_ge(h_done, 16 + 2 * k + 2)
                A(e_h[:, 0, k, :], h[:, k, :], ACT.Copy).then_inc(S("h2_rounded"), 1)

            def round_w(m):
                i, o = half_of(m)
                act.wait_ge(slab_in[i % RING], 16 * (i // RING + 1))
                A(e_w[:, m % 2, 0, :].rearrange("p (k c) -> p k c", k=KD), slab(i)[:, :, o:o + P], ACT.Copy)\
                    .then_inc(S("w_rounded"), 1)

            norm_scalar(0, 0)
            for c in range(4):
                g = sl.next()
                got(g)
                A(two(a_q[:, c, :]), halves(g[0]), ACT.Identity, bias=V('a_q', c)).then_inc(free[g[0]], 1)
            act.wait_ge(free[g[0]], g[1])
            A(scr[:, 127:128], a_q[:, 0, 0:1], ACT.Copy).then_inc(S("a_q_ready"), 4)
            for c in range(4 + 2 * NT):
                sl.next()
            for c in range(4):
                g = sl.next()
                got(g)
                A(two(a_o[:, c, :]), halves(g[0]), ACT.Sigmoid, bias=V('a_o', c)).then_inc(free[g[0]], 1)
            for _ in range(4):
                sl.next()
            act.wait_ge(S("a_rows_raw"), 4)
            link(A(a_rM, a_rF, ACT.Abs))
            link(A(a_rM, a_rM, ACT.Exp, scale=-1.0))
            A(a_rM, a_rM, ACT.Ln, bias=1.0).then_inc(S("a_rows_ln"), 1)
            g = sl.next()
            got(g)
            A(a_kT, bank(g[0]), ACT.Copy).then_inc(free[g[0]], 1)
            ggc = sl.next()
            act.wait_ge(S("a_rows_m"), 1)
            link(A(a_rFl, a_rFl, ACT.Exp))
            for d in range(2):
                ins = A(a_rW[:, d, 0:TS], a_rM[:, d, 0:TS], ACT.Exp, scale=-1.0, bias=rowv[0:4, d:d + 1])
            ins.then_inc(S("a_rows_w"), 1)
            sl.r = 0
            hist = []
            act.wait_ge(phload, 32)
            act.wait_ge(free[ggc[0]], ggc[1])
            for d in range(2):
                for hh in range(4):
                    n = d * 4 + hh
                    if n:
                        act.wait_ge(S("a_state_used"), n)
                    A(a_n0, ones, ACT.Copy, scale=V('n0', n)).then_inc(S("a_n0_ready"), 1)
                    sl.next((0, 1))
                    for k, dst in enumerate((a_Mb, a_Fb)):
                        g = sl.next((0, 1))
                        got(g)
                        if n:
                            act.wait_ge(S("a_nd_read"), n)
                        A(two(dst), halves(g[0]), ACT.Copy).then_inc(free[g[0]], 1)
                        if k == 0:
                            gm = g
                    act.wait_ge(free[gm[0]], gm[1])
                    order = ([0, 1, 2, 3] if d == 0 else [3, 2, 1, 0]) + [4]
                    for idx, i in enumerate(order):
                        it = n * 5 + idx
                        lo, hi = a_range(d, i)
                        g = sl.next((0, 1))
                        hist.append(g)
                        if it >= 2:
                            act.wait_ge(free[hist[it - 2][0]], hist[it - 2][1])
                        if idx == 1 and n:
                            act.wait_ge(S("a_kw_ready"), n)
                        bias = a_gc[:, d, i, hh:hh + 1]
                        dl = i * P
                        if hi - lo > P:
                            rl, rh = (dl + P, hi) if d == 0 else (lo, dl)
                            A(a_E[:, it % 2, rl:rh], a_Mb[:, rl:rh], ACT.Exp, scale=-1.0, bias=bias)
                        act.wait_ge(S("a_dm"), it + 1)
                        A(a_E[:, it % 2, dl:dl + P], a_dm[:, it % 2, :], ACT.Exp, scale=-1.0, bias=bias)\
                            .then_inc(S("a_E"), 1)
                    g = sl.next((0, 1))
                    got(g)
                    A(a_st[:, n, :], bank(g[0])[:, 0:P + 1], ACT.Copy).then_inc(free[g[0]], 1)
            act.wait_ge(free[g[0]], g[1])
            for n in range(8):
                act.dma_start(c_out[n], a_st[:, n, 0:P]).then_inc(stored, 16)
                act.dma_start(n_out[n], a_st[:, n, P:P + 1]).then_inc(stored, 16)
            act.dma_start(m_out[0], a_rI[:, 0, TOK - 1:TOK]).then_inc(stored, 16)
            act.dma_start(m_out[1], a_rI[:, 1, TS:TS + 1]).then_inc(stored, 16)
            STORES[0] += 18
            act.wait_ge(stored, 16 * STORES[0])
            act.wait_ge(S("a_ha"), 8)
            for hh in range(4):
                A(sq[:, hh, :], a_ha[:, hh, :], ACT.Square).then_inc(S("a_sq"), 1)
            head_roots(sl, got)
            A(scr[:, 126:127], a_gc[:, 0, 0, 0:1], ACT.Copy).then_inc(phase_a, 1)
            phase(act, 1)

            def gl_core(m, n):
                J, d = m['J'], n % 2
                last = P - 1 if d == 0 else 0
                X, b = m['X'], m['b']
                g = sl.next()
                got(g)
                A(modv[:, 2 * MOD1 + 8 * n:2 * MOD1 + 8 * n + 8, :], bank(g[0])[:, 0:16].rearrange("p (m g) -> p m g", g=2),
                  ACT.Copy).then_inc(free[g[0]], 1)
                for t in range(NT):
                    sl.next()
                gs = []
                for li in range(len(LEVELS)):
                    act.wait_ge(S("g_Z"), n * 7 + li + 1)
                    act.wait_ge(S("g_Zs"), n * 7 + li + 1)
                    A(X[li % 2], X[li % 2], ACT.Exp).then_inc(S("g_E"), 1)
                    for t in range(NT):
                        gs.append(sl.next())
                bt = b.rearrange("p (n t) -> p n t", t=P)
                act.wait_ge(full[gs[29][0]], gs[29][1])
                A(X[1], b, ACT.Exp).then_inc(S("g_EB"), 1)
                act.wait_ge(full[gs[34][0]], gs[34][1])
                for e in range(J * NT):
                    A(X[0][:, e * P:(e + 1) * P], b[:, e * P:(e + 1) * P], ACT.Exp, scale=-1.0,
                      bias=b[:, e * P + last:e * P + last + 1])
                A(m['dec'], bt[:, :, last], ACT.Exp).then_inc(S("g_EK"), 1)
                for idx, t in enumerate(tiles_of(d)):
                    g = sl.next()
                    got(g)
                    if idx >= 2:
                        act.wait_ge(full[gk[idx - 2][0]], gk[idx - 2][1])
                    elif idx == 0:
                        gk = []
                    A(m['kT'][idx % 2], bank(g[0])[:, 0:J * P], ACT.Copy).then_inc(free[g[0]], 1)
                    g = sl.next()
                    if idx != 3:
                        gk.append(sl.next())
                    else:
                        gk.append(g)

            def gl_end(m, k, base):
                for hh in range(HEADS):
                    if hh == 0:
                        act.wait_ge(S("g_o"), k + 1)
                    A(sq[:, hh, :], m['o'][:, hh, :], ACT.Square).then_inc(S("g_sq"), 1)
                for d in range(2):
                    for hh in range(HEADS):
                        j, r = rows(m['J'], hh)
                        dst = (sb_out, sc_out)[k][d * 4 + hh]
                        act.dma_start(dst, m['Snew'][r, d, j, :]).then_inc(stored, 16)
                        STORES[0] += 1
                head_roots(sl, got)
                act.wait_ge(stored, 16 * STORES[0])
                A(scr[:, 125 - k:126 - k], ones[:, 0:1], ACT.Copy).then_inc(phase_a, 1)

            sl.r = 0
            act.dma_start(mB['S'], s0b_in).then_inc(phload, 16)
            act.dma_start(mB['vb'], tokb_in[1]).then_inc(phload, 16)
            act.wait_ge(S("lb_in"), 1)
            A(lbw[:, 8:16], lbw[:, 0:8], ACT.Exp).then_inc(S("lb_exp"), 1)
            for _ in range(4 + 2 * NT):
                sl.next()
            for c in range(4):
                g = sl.next()
                got(g)
                A(two(ybr[:, 1, c, :]), halves(g[0]), ACT.Silu, bias=V('b_g', c)).then_inc(free[g[0]], 1)

            def logsig(m, n, z):
                X = m['X']
                link(A(X[0], z, ACT.Abs))
                link(A(X[0], X[0], ACT.Exp, scale=-1.0))
                A(X[0], X[0], ACT.Ln, bias=1.0).then_inc(S("g_L"), 1)

            for d in range(2):
                z = mB['k']
                if d:
                    act.wait_ge(S("g_X"), 9)
                    act.wait_ge(S("g_free"), 1)
                for c in range(4):
                    g = sl.next()
                    got(g)
                    A(two(z[:, c * TOK:(c + 1) * TOK]), halves(g[0]), ACT.Identity, bias=V('b_f', 4 * d + c))\
                        .then_inc(free[g[0]], 1)
                act.wait_ge(free[g[0]], g[1])
                logsig(mB, d, z)
                act.wait_ge(S("b_zc"), d + 1)
                link(A(mB['X'][1], mB['X'][1], ACT.Exp, scale=-1.0))
                for c in range(4):
                    xc = mB['X'][1][:, c * TOK:(c + 1) * TOK]
                    ins = A(xc, xc, ACT.Ln, scale=lbw[:, 16 + 4 * d + c:17 + 4 * d + c], bias=1.0)
                ins.then_inc(S("b_L2"), 1)
                act.wait_ge(S("b_lf"), d + 1)
                A(z, z, ACT.Sigmoid, scale=-1.0).then_inc(S("b_sig"), 1)
                gl_core(mB, d)
            gl_end(mB, 0, 0)
            phase(act, 2)
            sl.r = 0
            act.dma_start(mC['S'], s0c_in).then_inc(phload, 16)
            act.dma_start(mC['vb'], tokb_in[2]).then_inc(phload, 16)
            act.dma_start(c_up, up_in).then_inc(phload, 16)
            for _ in range(4 + 2 * NT):
                sl.next()
            for c in range(4):
                g = sl.next()
                got(g)
                A(two(ybr[:, 2, c, :]), halves(g[0]), ACT.Silu, bias=V('c_g', c)).then_inc(free[g[0]], 1)
            for _ in range(2):
                sl.next()
            for d in range(2):
                if d:
                    act.wait_ge(S("g_free"), 3)
                for j in range(2):
                    g = sl.next()
                    got(g)
                    A(two(mC['b'][:, j * TOK:(j + 1) * TOK]), halves(g[0]), ACT.Identity, bias=V('b_up', 2 * d + j))\
                        .then_inc(free[g[0]], 1)
                act.wait_ge(free[g[0]], g[1])
                logsig(mC, 2 + d, mC['b'])
                gl_core(mC, 2 + d)
            gl_end(mC, 1, 4)
            phase(act, 3)
            sl.r = 0
            act.dma_start(d_w, lruw_in).then_inc(phload, 16)
            act.wait_ge(S("x_parked"), 16)
            act.wait_ge(h_done, 16)
            for k in range(KD):
                ins = A(e_h[:, 0, k, :], h[:, k, :], ACT.Copy)
            ins.then_inc(S("h1_rounded"), 1)
            for c in range(4):
                g = sl.next()
                got(g)
                A(two(d_x[:, c, :]), halves(g[0]), ACT.Identity, bias=V('d_x', c)).then_inc(free[g[0]], 1)
            act.wait_ge(free[g[0]], g[1])
            A(scr[:, 120:121], ones[:, 0:1], ACT.Copy).then_inc(S("d_x"), 1)
            for c in range(4):
                g = sl.next()
                got(g)
                A(two(ybr[:, 3, c, :]), halves(g[0]), ACT.Gelu_apprx_tanh, bias=V('d_g', c)).then_inc(free[g[0]], 1)
            link(A(d_tmp, V('lam', 0, 8), ACT.Abs))
            link(A(d_tmp, d_tmp, ACT.Exp, scale=-1.0))
            A(d_tmp, d_tmp, ACT.Ln, bias=1.0).then_inc(S("d_sp"), 1)
            for d in range(2):
                if d:
                    act.wait_ge(S("d_scanned"), 1)
                for hh in range(HEADS):
                    for w, (dst, bias) in enumerate(((d_R, 'lru_b_a'), (d_U, 'lru_b_x'))):
                        g = sl.next()
                        got(g)
                        A(two(dst[:, hh, :]), halves(g[0]), ACT.Sigmoid, bias=V(bias, 4 * d + hh))\
                            .then_inc(free[g[0]], 1)
                act.wait_ge(free[g[0]], g[1])
                gprev = (g[0] - 1) % 4
                act.wait_ge(free[gprev], g[1])
                act.wait_ge(S("d_spl"), 1)
                for hh in range(HEADS):
                    A(d_T[:, hh, :], d_R[:, hh, :], ACT.Tanh, scale=d_nspl[:, 4 * d + hh:4 * d + hh + 1])
                link(A(scr[:, 118 - d:119 - d], ones[:, 0:1], ACT.Copy))
                for hh in range(HEADS):
                    ins = A(d_R[:, hh, :], d_R[:, hh, :], ACT.Exp, scale=d_spl[:, 4 * d + hh:4 * d + hh + 1])
                ins.then_inc(S("d_a"), 1)
                act.wait_ge(S("d_w2"), d + 1)
                A(d_T, d_T, ACT.Sqrt).then_inc(S("d_rt"), 1)
            act.wait_ge(S("d_scanned"), 2)
            for n in range(8):
                act.dma_start(h_out[n], d_new[:, n:n + 1]).then_inc(stored, 16)
                STORES[0] += 1
            act.wait_ge(stored, 16 * STORES[0])
            A(scr[:, 119:120], ones[:, 0:1], ACT.Copy).then_inc(phase_a, 1)
            phase(act, 4)
            sl.r = 0
            act.dma_start(r_sk, sk_in).then_inc(phload, 16)
            gp = []
            round_w(0)
            round_w(1)
            for j in range(KD):
                for n in range(NBR):
                    e = 4 * j + n
                    g = sl.next()
                    got(g)
                    if e >= 2:
                        act.wait_ge(free[gp[-2][0]], gp[-2][1])
                    A(two(m_sg[:, e % 2, :]), halves(g[0]), ACT.Sigmoid, bias=V('gates', n * KD + j))\
                        .then_inc(free[g[0]], 1)
                    if e + 2 < KD * NBR:
                        round_w(e + 2)
                    gp.append(sl.next())
            for j in range(KD):
                sl.next()
            round_w(KD * NBR)
            round_w(KD * NBR + 1)
            norm_scalar(1, 24)
            sl.r = 0

            def score(hp):
                g = sl.next()
                got(g)
                A(r_s[:, 0:4, hp, :], bank(g[0]).rearrange("p (n e) -> p n e", n=4), ACT.Copy)
                A(r_s[:, 4, hp, :], bank2(g[0])[:, 0:P], ACT.Copy).then_inc(free[g[0]], 1)
                return g

            gs = []
            for hp in range(16):
                g = sl.next()
                got(g)
                if hp >= 2:
                    act.wait_ge(full[gs[hp - 2][0]], gs[hp - 2][1])
                A(two(r_qT[:, hp % 2, :]), halves(g[0]), ACT.Copy).then_inc(free[g[0]], 1)
                if hp < 14:
                    round_w(KD * NBR + hp + 2)
                if hp:
                    gs.append(score(hp - 1))
            g = score(15)
            act.wait_ge(free[g[0]], g[1])
            A(scr[:, 121:122], ones[:, 0:1], ACT.Copy).then_inc(S("r_scores"), 1)
            base = list(sl.n)

            def round_u(lot, use, r):
                act.wait_ge(u_sem[r % 2], lot)
                if use is not None:
                    act.wait_ge(full[r % 2], use)
                A(e_u[:, r, 0, :], e_uraw[:, r % 2, :], ACT.Copy).then_inc(S("u_rounded"), 1)

            def gelu(use, sent, r):
                s = r % 2
                act.wait_ge(full[s], use)
                if sent is not None:
                    act.wait_ge(t_out[s], sent)
                A(two(e_t[:, s, :]), halves(s), ACT.Gelu_apprx_tanh).then_inc(free[s], 1)

            mp = gmap.rearrange("b p q c n -> p q b c n")

            def chunk(i, c0, r, prefetch=True):
                if prefetch:
                    m = c0 + r + 2
                    round_u(i * 32 + (m // 2 + 1) * 16, i * 2 + (base[r % 2] + m // 2 - 1), (r + 2) % 4)
                m = c0 + r
                if m < 2 and c0 == 0:
                    gelu(i * 2 + (base[r % 2] + 1), i * 32, r)
                else:
                    gelu(i * 2 + (base[r % 2] + m // 2 + 1), i * 32 + 16 * (m // 2), r)

            round_u(16, None, 0)
            round_u(16, None, 1)
            for st, (c0, main, tail) in enumerate(STAGES):
                if st:
                    t = st - 1
                    act.wait_ge(full[2], base[2] + 17 * t + 1)
                    if t >= 2:
                        act.wait_ge(S("r_L"), 32 * (t - 1))
                        act.wait_ge(S("r_R"), 32 * (t - 1))
                    A(r_T[:, t % 2], bank(2)[:, 0:384].rearrange("p (w c) -> p w c", w=3), ACT.Copy)\
                        .then_inc(free[2], 1)
                    with act.Fori(0, main // 8) as i:
                        for r in range(8):
                            chunk(i * 2, c0 + r // 4 * 4, r % 4)
                            for gi in (2 * r, 2 * r + 1):
                                s = 2 + gi % 2
                                use = base[s] + (17 * t + 1 if s == 2 else 16 * t) + gi // 2 + 1
                                act.wait_ge(full[s], i * 8 + use)
                                if gi % 8 == 0:
                                    act.wait_ge(map_out[gi // 8], i * 16 + 32 * t)
                                n0 = gi % 8 * 4
                                A(g_stage[:, gi // 8, :, n0:n0 + 4].rearrange("p e n -> p n e"),
                                  bank(s).rearrange("p (n e) -> p n e", n=4), ACT.Copy).then_inc(free[s], 1)
                                if gi % 8 == 7:
                                    act.wait_ge(free[2], i * 8 + (use - base[3] + base[2] + t + 1))
                                    act.wait_ge(free[3], i * 8 + use)
                                    act.dma_start(
                                        mp[:, bass.ds(i * 2 + (4 * t + gi // 8), 1)].rearrange("p o b c n -> p (o b) (c n)"),
                                        g_stage[:, gi // 8].rearrange("p (b c) n -> p b (c n)", c=4))\
                                        .then_inc(map_out[gi // 8], 16)
                else:
                    with act.Fori(0, main // 4) as i:
                        for r in range(4):
                            chunk(i, c0, r)
                if st < NT:
                    act.wait_ge(S("r_sub"), st + 1)
                    A(r_t, r_t, ACT.Exp).then_inc(S("r_exp"), 1)
                last = st == NT
                with act.Fori(main // 4, (main + tail) // 4 - last) as i:
                    for r in range(4):
                        chunk(i, c0, r)
                if last:
                    for r in range(4):
                        c = NKEY - 4 + r
                        if r < 2:
                            round_u((c + 2) // 2 * 16 + 16, base[r % 2] + (c + 2) // 2 - 1, r + 2)
                        gelu(base[r % 2] + c // 2 + 1, 16 * (c // 2), r)
            base = [base[0] + 64, base[1] + 64, base[2] + 17 * NT, base[3] + 16 * NT]

            def parts(b, use, lot, r):
                act.wait_ge(S("weighted"), b + 1)
                if use is not None:
                    act.wait_ge(full[3], use)
                A(e_a[:, r, 0, :], e_T[:, r, :], ACT.Copy).then_inc(S("a_rounded"), 1)
                for c in range(4):
                    act.wait_ge(v_sem[c], lot)
                    A(e_v[:, r, 0, c, :], e_vraw[:, c, :], ACT.Copy).then_inc(S("v_rounded"), 1)

            parts(0, None, 16, 0)
            for r in range(2):
                act.wait_ge(t_out[r], 16 * NKEY // 2)
            parts(1, None, 32, 1)
            with act.Fori(1, NB // 2) as i:
                for r in range(2):
                    parts(i * 2 + r, i * 4 + (base[3] + 2 * r - 2), i * 32 + (16 * r + 16), r)
            sl.n = [base[s] + 2 * NB for s in range(4)]
            sl.r = 0
            for k in range(KD):
                act.wait_ge(x_ready, 16 + k + 1)
                A(sq[:, k, :], x[:, k, :], ACT.Square).then_inc(sq_done, 1)
            g = sl.next()
            got(g)
            A(two(rstd), halves(g[0]), ACT.Sqrt, bias=cepsD).then_inc(free[g[0]], 1)
            act.wait_ge(S("y_done"), 8)
            act.dma_start(y_out, h[:]).then_inc(stored, 16)
            STORES[0] += 1

        @block.vector
        def _(dve):
            sl = Slots()
            ch = [0]
            vv = nc.vector

            def link(ins):
                ch[0] += 1
                ins.then_inc(vch, 1)
                dve.wait_ge(vch, ch[0])

            def got(g):
                dve.wait_ge(full[g[0]], g[1])

            dve.wait_ge(load, 16 * 5)
            link(vv.tensor_copy(lvl[:], lvl_f))
            dve.wait_ge(load_x, 16)
            for k in range(4):
                xv = x[:, k, 0:TS].rearrange("p (r c) -> p r c", c=GRID_W)
                pr = V('pos_r', 8 * k, 8).unsqueeze(2).to_broadcast([P, 8, GRID_W])
                vv.tensor_tensor(xv, xv, pr, ALU.add).then_inc(x_ready, 1)
            for k in range(4):
                xv = x[:, 4 + k, 0:TS].rearrange("p (r c) -> p r c", c=GRID_W)
                pc = V('pos_c', 64 * k, 64).unsqueeze(1).to_broadcast([P, 8, GRID_W])
                vv.tensor_tensor(xv, xv, pc, ALU.add).then_inc(x_ready, 1)
            g = sl.next()
            got(g)
            link(vv.tensor_tensor(modv[:, 0:2 * MOD1], bank(g[0])[:, 0:4 * MOD1].rearrange("p (m g) -> p m g", g=2),
                                  V('b_mod', 0, 2 * MOD1).unsqueeze(2).to_broadcast([P, 2 * MOD1, 2]), ALU.add))
            mark().then_inc(free[g[0]], 1)

            def norm_vector(m, gname, scale_at):
                link(vv.tensor_scalar(amul[:], modv[:, scale_at:scale_at + 8, :], 1.0, D ** 0.5, ALU.add, ALU.mult))
                link(vv.tensor_tensor(amul[:], amul[:], V(gname, 0, 8).unsqueeze(2).to_broadcast([P, 8, 2]), ALU.mult))
                g = sl.next()
                dve.wait_ge(free[g[0]], g[1])
                link(vv.reciprocal(rstd, rstd))
                for k in range(KD):
                    for gq, (lo, hi) in enumerate(((0, TS), (TS, TOK))):
                        vv.scalar_tensor_tensor(out=h[:, k, lo:hi], in0=x[:, k, lo:hi], scalar=amul[:, k, gq:gq + 1],
                                                in1=rstd[:, lo:hi], op0=ALU.mult, op1=ALU.mult).then_inc(hm_done, 1)
                for k in range(KD if m else 0):
                    dve.wait_ge(S("h2_rounded"), k + 1)
                    vv.tensor_tensor(e_h[:, 1, k, :], h[:, k, :], e_h[:, 0, k, :].bitcast(F32), ALU.subtract)\
                        .then_inc(S("h2_rest"), 1)

            norm_vector(0, 'norm1', 8)
            for c in range(4):
                sl.next()
            for c in range(4):
                g = sl.next()
                got(g)
                vv.tensor_scalar(two(a_k[:, c, :]), halves(g[0]), V('a_k', c), P ** -0.5, ALU.add, ALU.mult)\
                    .then_inc(free[g[0]], 1)
            mark().then_inc(S("a_k_ready"), 4)
            dve.wait_ge(phload, 32)
            for c in range(2):
                for t in range(NT):
                    g = sl.next()
                    got(g)
                    vv.tensor_tensor(a_v[:, t, c * 256:(c + 1) * 256], bank(g[0])[:, 0:256],
                                     a_vb[:, c * 256:(c + 1) * 256], ALU.add).then_inc(free[g[0]], 1)
            mark().then_inc(S("a_v_ready"), 2 * NT)
            for c in range(4):
                sl.next()
            for d in range(2):
                for which in range(2):
                    g = sl.next()
                    got(g)
                    vv.tensor_scalar(two((a_rI, a_rF)[which][:, d, :]), ps[0:4, 2 * g[0]:2 * g[0] + 2, 0:HALF],
                                     rowv[0:4, 2 + d * 2 + which:3 + d * 2 + which], None, ALU.add)\
                        .then_inc(free[g[0]], 1)
            mark().then_inc(S("a_rows_raw"), 4)
            dve.wait_ge(S("a_rows_ln"), 1)
            link(vv.scalar_tensor_tensor(out=a_rF, in0=a_rF, scalar=0.0, in1=a_rM, op0=ALU.min, op1=ALU.subtract))
            one4 = ones[0:4, 0:1]

            def seqs(ap, d):
                a, b = ap[:, d, 0:TS], ap[:, d, TS:TOK]
                return (a, b) if d == 0 else (a[:, ::-1], b[:, ::-1])

            for d in range(2):
                for q in range(2):
                    f = seqs(a_rF, d)[q]
                    vv.tensor_tensor_scan(out=seqs(a_rW, d)[q], data0=one4.to_broadcast([4, f.shape[1]]), data1=f,
                                          initial=0.0, op0=ALU.mult, op1=ALU.add)
            link(mark())
            vv.tensor_tensor(a_rG, a_rI, a_rW, ALU.subtract).then_inc(S("a_rows_g"), 1)
            dve.wait_ge(S("a_rows_g"), 1)
            for d in range(2):
                for q in range(2):
                    gg = seqs(a_rG, d)[q]
                    vv.tensor_tensor_scan(out=seqs(a_rM, d)[q], data0=one4.to_broadcast([4, gg.shape[1]]), data1=gg,
                                          initial=rowv[0:4, d:d + 1] if q == 0 else 0.0, op0=ALU.mult, op1=ALU.max)
            link(mark())
            link(vv.tensor_tensor(a_rI, a_rW, a_rM, ALU.add))
            vv.tensor_scalar(a_rFl, a_rI, -1.0, 80.0, ALU.mult, ALU.min).then_inc(S("a_rows_m"), 1)
            gkt = sl.next()
            g = sl.next()
            got(g)
            dve.wait_ge(free[gkt[0]], gkt[1])
            vv.tensor_copy(a_gc.rearrange("p d n h -> p (d n h)"), bank(g[0])[:, 0:40]).then_inc(free[g[0]], 1)
            sl.r = 0
            for d in range(2):
                for hh in range(4):
                    n = d * 4 + hh
                    g = sl.next((0, 1))
                    got(g)
                    if n:
                        dve.wait_ge(S("a_state_used"), n)
                    vv.tensor_tensor(a_qt, a_q[:, hh, 0:TS], bank(g[0]), ALU.mult).then_inc(free[g[0]], 1)
                    mark().then_inc(S("a_qt_ready"), 1)
                    gm = sl.next((0, 1))
                    gf = sl.next((0, 1))
                    dve.wait_ge(free[gm[0]], gm[1])
                    over = C('over0') if d == 0 else C('over1')
                    order = ([0, 1, 2, 3] if d == 0 else [3, 2, 1, 0]) + [4]

                    def dm(idx):
                        it = n * 5 + idx
                        if it >= 2:
                            dve.wait_ge(S("a_E"), it - 1)
                        i = order[idx]
                        vv.tensor_tensor(a_dm[:, it % 2, :], a_Mb[:, i * P:(i + 1) * P], over, ALU.add)\
                            .then_inc(S("a_dm"), 1)

                    dm(0)
                    for idx, i in enumerate(order):
                        it = n * 5 + idx
                        lo, hi = a_range(d, i)
                        if idx < 4:
                            dm(idx + 1)
                        g = sl.next((0, 1))
                        got(g)
                        dve.wait_ge(S("a_E"), it + 1)
                        if it >= 2:
                            dve.wait_ge(S("a_pv"), it - 1)
                        vv.tensor_tensor(a_P[:, it % 2, lo:hi], bank(g[0])[:, 0:hi - lo], a_E[:, it % 2, lo:hi],
                                         ALU.mult).then_inc(free[g[0]], 1)
                    last = TOK - 1 if d == 0 else TS
                    if n:
                        dve.wait_ge(full[gst[0]], gst[1])
                    vv.tensor_scalar(a_kw, a_kT[:, hh * P:(hh + 1) * P], a_E[:, it % 2, last:last + 1], None, ALU.mult)\
                        .then_inc(S("a_kw_ready"), 1)
                    gst = sl.next((0, 1))
                    dve.wait_ge(S("a_pv"), 5 * (n + 1))
                    dve.wait_ge(free[gf[0]], gf[1])
                    vv.tensor_tensor(a_D[:, 0:TS], bank(den), a_Fb[:, 0:TS], ALU.max)
                    link(vv.tensor_tensor(a_D[:, TS:TOK], bank2(den)[:, 0:P], a_Fb[:, TS:TOK], ALU.max))
                    for q, dd in (((0, TS), bank(den)), ((TS, TOK), bank2(den)[:, 0:P])):
                        ins = vv.scalar_tensor_tensor(out=a_D[:, q[0]:q[1]], in0=dd, scalar=-1.0,
                                                      in1=a_D[:, q[0]:q[1]], op0=ALU.mult, op1=ALU.max)
                    link(ins)
                    link(vv.reciprocal(a_D, a_D))
                    dst = a_ha[:, hh, :] if d == 0 else a_T
                    vv.tensor_tensor(dst[:, 0:TS], a_D[:, 0:TS], bank(num), ALU.mult)
                    vv.tensor_tensor(dst[:, TS:TOK], a_D[:, TS:TOK], bank2(num)[:, 0:P], ALU.mult)\
                        .then_inc(S("a_nd_read"), 1)
                    dve.wait_ge(S("a_nd_read"), n + 1)
                    if d == 1:
                        link(vv.tensor_tensor(a_ha[:, hh, :], a_ha[:, hh, :], a_T, ALU.add))
            mark().then_inc(S("a_ha"), 8)
            for hh in range(4):
                head_norm(dve, link, sl.next((0, 1)), a_ha[:, hh, :], a_o[:, hh, :], sq[:, 4 + hh, :], a_T)
            mark().then_inc(phase_v, 1)
            phase(dve, 1)
            TT, TSC, STT = vv.tensor_tensor, vv.tensor_scalar, vv.scalar_tensor_tensor

            def gl_core(m, n):
                J, d = m['J'], n % 2
                last = P - 1 if d == 0 else 0
                X, b, q, k = m['X'], m['b'], m['q'], m['k']
                sl.next()
                for j in range(J):
                    bj = b[:, j * TOK:(j + 1) * TOK]
                    rs = C('reset0') if d == 0 else C('reset1')
                    if d:
                        bj, rs = bj[:, ::-1], rs[:, ::-1]
                    ins = vv.tensor_tensor_scan(out=bj, data0=rs, data1=bj, initial=0.0, op0=ALU.mult, op1=ALU.add)
                link(ins)
                mark().then_inc(S("g_in"), 1)
                used = []

                def sub(li):
                    w = LEVELS[li]
                    if li >= 2:
                        dve.wait_ge(full[used[li - 2][0]], used[li - 2][1])
                    bv = b.rearrange("p (n s w) -> p n s w", s=2, w=w)
                    xv = X[li % 2].rearrange("p (n s w) -> p n s w", s=2, w=w)
                    nb = J * TOK // (2 * w)
                    ref = (bv[:, :, 0, w - 1:w] if d == 0 else bv[:, :, 1, 0:1]).to_broadcast([P, nb, w])
                    fut = 1 - d
                    TT(xv[:, :, fut, :], bv[:, :, fut, :], ref, ALU.subtract).then_inc(S("g_Z"), 1)

                def mul(li):
                    w = LEVELS[li]
                    dve.wait_ge(S("g_E"), n * 7 + li + 1)
                    xv = X[li % 2].rearrange("p (n s w) -> p n s w", s=2, w=w)
                    fut, past = (1, 0) if d == 0 else (0, 1)
                    TT(xv[:, :, fut, :], xv[:, :, fut, :], q.rearrange("p (n s w) -> p n s w", s=2, w=w)[:, :, fut, :],
                       ALU.mult)
                    TT(xv[:, :, past, :], xv[:, :, past, :],
                       k.rearrange("p (n s w) -> p n s w", s=2, w=w)[:, :, past, :], ALU.mult).then_inc(S("g_X"), 1)

                sub(0)
                for t in range(NT):
                    g = sl.next()
                    got(g)
                    TT(heads_row(J, m['P'][:, t, :]), heads_psum(J, g), heads_same(J, ident), ALU.mult).then_inc(free[g[0]], 1)
                mul(0)
                for li in range(len(LEVELS)):
                    if li + 1 < len(LEVELS):
                        sub(li + 1)
                    for t in range(NT):
                        g = sl.next()
                        got(g)
                        dve.wait_ge(free[pw[t][0]], pw[t][1]) if li else None
                        vv.copy_predicated(heads_row(J, m['P'][:, t, :]), heads_same(J, lvl[:, d, li, :]),
                                           heads_psum(J, g)).then_inc(free[g[0]], 1)
                        pw[t] = g
                    used.append(g)
                    if li + 1 < len(LEVELS):
                        mul(li + 1)
                dve.wait_ge(S("g_EB"), n + 1)
                TT(X[1], X[1], q, ALU.mult).then_inc(S("g_X"), 1)
                dve.wait_ge(S("g_EK"), n + 1)
                TT(X[0], X[0], k, ALU.mult).then_inc(S("g_X"), 1)
                dve.wait_ge(S("g_X"), n * 9 + 9)
                mark().then_inc(S("g_free"), 1)
                for idx, t in enumerate(tiles_of(d)):
                    sl.next()
                    g = sl.next()
                    got(g)
                    o = m['o'][:, :, t * P:(t + 1) * P]
                    if J == 2:
                        o = o.rearrange("p (j a) t -> p a j t", a=2)
                    pv = heads_psum(J, g)
                    if d == 0:
                        vv.tensor_copy(o, pv).then_inc(free[g[0]], 1)
                    else:
                        TT(o, o, pv, ALU.add).then_inc(free[g[0]], 1)
                    if idx == 3:
                        continue
                    g = sl.next()
                    got(g)
                    if 0 < idx < 4:
                        dve.wait_ge(free[gkp[0]], gkp[1])
                    for hh in range(HEADS):
                        j, r = rows(J, hh)
                        kv = bank(g[0])[r, hh * P:(hh + 1) * P]
                        if t < 4:
                            ins = STT(out=m['S'][r, d, j, :], in0=m['S'][r, d, j, :],
                                      scalar=m['dec'][r, j * NT + t:j * NT + t + 1], in1=kv, op0=ALU.mult, op1=ALU.add)
                        else:
                            ins = vv.tensor_copy(m['Snew'][r, d, j, :], kv)
                    ins.then_inc(free[g[0]], 1)
                    gkp = g

            def gl_end(m, k, gate):
                link(mark())
                mark().then_inc(S("g_o"), 1)
                for hh in range(HEADS):
                    head_norm(dve, link, sl.next((0, 1)), m['o'][:, hh, :], gate[:, hh, :], sq[:, 4 + hh, :],
                              m['P'].rearrange("p n c -> p (n c)")[:, 0:TOK])
                mark().then_inc(phase_v, 1)

            pw = {}
            sl.r = 0
            lb = V('lb', 0, 8)
            TT(lbw[:, 0:8], lb, lb, ALU.subtract).then_inc(S("lb_in"), 1)
            dve.wait_ge(S("lb_exp"), 1)
            link(vv.reciprocal(lbw[:, 24:32], lbw[:, 8:16]))
            link(TT(lbw[:, 8:16], lbw[:, 8:16], lbw[:, 24:32], ALU.mult))
            link(TT(lbw[:, 16:24], lbw[:, 8:16], lbw[:, 8:16], ALU.subtract))
            link(TSC(lbw[:, 24:32], lbw[:, 16:24], -1.0, 1.0, ALU.mult, ALU.add))
            for c in range(4):
                g = sl.next()
                got(g)
                TSC(two(mB['q'][:, c * TOK:(c + 1) * TOK]), halves(g[0]), V('b_q', c), P ** -0.5, ALU.add, ALU.mult)\
                    .then_inc(free[g[0]], 1)
            dve.wait_ge(phload, 16 * LOADS['B'])
            for c in range(2):
                for t in range(NT):
                    g = sl.next()
                    got(g)
                    TT(mB['v'][:, t, c * 256:(c + 1) * 256], bank(g[0])[:, 0:256], mB['vb'][:, c * 256:(c + 1) * 256],
                       ALU.add).then_inc(free[g[0]], 1)
            for c in range(4):
                sl.next()
            for d in range(2):
                for c in range(4):
                    g = sl.next()
                dve.wait_ge(free[g[0]], g[1])
                TSC(mB['X'][1], mB['k'], -80.0, None, ALU.max).then_inc(S("b_zc"), 1)
                dve.wait_ge(S("g_L"), d + 1)
                link(STT(out=mB['b'], in0=mB['k'], scalar=0.0, in1=mB['X'][0], op0=ALU.min, op1=ALU.subtract))
                dve.wait_ge(S("b_L2"), d + 1)
                TT(mB['b'], mB['b'], mB['X'][1], ALU.add).then_inc(S("b_lf"), 1)
                dve.wait_ge(S("b_lf"), d + 1)
                dve.wait_ge(S("b_sig"), d + 1)
                for c in range(4):
                    kc = mB['k'][:, c * TOK:(c + 1) * TOK]
                    ins = TSC(kc, kc, lbw[:, 24 + 4 * d + c:25 + 4 * d + c], None, ALU.mult)
                link(ins)
                gl_core(mB, d)
            gl_end(mB, 0, ybr[:, 1])
            phase(dve, 2)
            sl.r = 0
            for c in range(2):
                g = sl.next()
                got(g)
                TSC(two(mC['q'][:, c * TOK:(c + 1) * TOK]), halves(g[0]), V('c_q', c), 64 ** -0.5, ALU.add, ALU.mult)\
                    .then_inc(free[g[0]], 1)
            for c in range(2):
                g = sl.next()
                got(g)
                TSC(two(mC['k'][:, c * TOK:(c + 1) * TOK]), halves(g[0]), V('c_k', c), None, ALU.add)\
                    .then_inc(free[g[0]], 1)
            dve.wait_ge(phload, 16 * LOADS['C'])
            for c in range(2):
                for t in range(NT):
                    g = sl.next()
                    got(g)
                    TT(mC['v'][:, t, c * 256:(c + 1) * 256], bank(g[0])[:, 0:256], mC['vb'][:, c * 256:(c + 1) * 256],
                       ALU.add).then_inc(free[g[0]], 1)
            for c in range(4):
                sl.next()
            for d in range(2):
                g = sl.next()
                got(g)
                TSC(two(c_lr[:, d, :]), ps[0:16, 2 * g[0]:2 * g[0] + 2, 0:HALF], rowv[0:16, 6 + d:7 + d], None, ALU.add)\
                    .then_inc(free[g[0]], 1)
            mark().then_inc(S("c_lr"), 1)
            for d in range(2):
                for j in range(2):
                    g = sl.next()
                dve.wait_ge(free[g[0]], g[1])
                dve.wait_ge(S("g_L"), 3 + d)
                link(STT(out=mC['b'], in0=mC['b'], scalar=0.0, in1=mC['X'][0], op0=ALU.min, op1=ALU.subtract))
                link(TSC(mC['b'], mC['b'], 1.0 / 16.0, None, ALU.mult))
                gl_core(mC, 2 + d)
            gl_end(mC, 1, ybr[:, 2])
            phase(dve, 3)
            sl.r = 0
            m_rest = modv[:, 2 * MOD1:48, :]
            link(TT(m_rest, m_rest, V('b_mod', 2 * MOD1, 48 - 2 * MOD1).unsqueeze(2)
                    .to_broadcast([P, 48 - 2 * MOD1, 2]), ALU.add))
            for c in range(8):
                sl.next()
            dve.wait_ge(S("d_x"), 1)
            for hh in range(HEADS):
                cw = lambda w: V('conv_w', 4 * w + hh)
                TSC(d_xd[:, hh, :], d_x[:, hh, :], cw(1), V('conv_b', hh), ALU.mult, ALU.add)
            link(mark())
            for w, o in ((0, -1), (2, 1), (3, 2)):
                for hh in range(HEADS):
                    for lo, hi in ((0, TS), (TS, TOK)):
                        a, b_ = max(lo, lo - o), min(hi, hi - o)
                        ins = STT(out=d_xd[:, hh, a:b_], in0=d_x[:, hh, a + o:b_ + o],
                                  scalar=V('conv_w', 4 * w + hh), in1=d_xd[:, hh, a:b_], op0=ALU.mult, op1=ALU.add)
                link(ins)
            dve.wait_ge(phload, 16 * LOADS['D'])
            mark().then_inc(S("d_conv"), 1)
            dve.wait_ge(S("d_sp"), 1)
            link(TSC(d_spl, V('lam', 0, 8), -1.0, 0.0, ALU.mult, ALU.max))
            link(TT(d_spl, d_spl, d_tmp, ALU.add))
            link(TSC(d_nspl, d_spl, 8.0, None, ALU.mult))
            TSC(d_spl, d_spl, -8.0, None, ALU.mult).then_inc(S("d_spl"), 1)
            for d in range(2):
                for _ in range(8):
                    g = sl.next()
                dve.wait_ge(S("d_a"), d + 1)
                link(TT(d_Q, d_R, d_R, ALU.mult))
                link(STT(out=d_T, in0=d_Q, scalar=1.0, in1=d_T, op0=ALU.add, op1=ALU.mult))
                TSC(d_T, d_T, 0.0, None, ALU.max).then_inc(S("d_w2"), 1)
                link(TT(d_U, d_U, d_xd, ALU.mult))
                dve.wait_ge(S("d_rt"), d + 1)
                link(TT(d_U, d_U, d_T, ALU.mult))
                dst = d_H if d == 0 else d_Q
                for hh in range(HEADS):
                    for q, (lo, hi) in enumerate(((0, TS), (TS, TOK))):
                        o_, a_, u_ = dst[:, hh, lo:hi], d_R[:, hh, lo:hi], d_U[:, hh, lo:hi]
                        if d:
                            o_, a_, u_ = o_[:, ::-1], a_[:, ::-1], u_[:, ::-1]
                        vv.tensor_tensor_scan(out=o_, data0=a_, data1=u_,
                                              initial=V('h0', 4 * d + hh) if q == 0 else 0.0,
                                              op0=ALU.mult, op1=ALU.add)
                link(mark())
                lastc = TOK - 1 if d == 0 else TS
                vv.tensor_copy(d_new[:, 4 * d:4 * d + 4], dst[:, :, lastc]).then_inc(S("d_scanned"), 1)
            link(TT(d_H, d_H, d_Q, ALU.add))
            link(TT(ybr[:, 3], ybr[:, 3], d_H, ALU.mult))
            mark().then_inc(phase_v, 1)
            phase(dve, 4)
            sl.r = 0
            for j in range(KD):
                for n in range(NBR):
                    e = 4 * j + n
                    gg = sl.next()
                    g = sl.next()
                    dve.wait_ge(free[gg[0]], gg[1])
                    got(g)
                    o_ = mrg[:, j, :] if n == 0 else m_tmp
                    TT(two(o_), halves(g[0]), two(m_sg[:, e % 2, :]), ALU.mult).then_inc(free[g[0]], 1)
                    dve.wait_ge(free[g[0]], g[1])
                    if n:
                        link(TT(mrg[:, j, :], mrg[:, j, :], m_tmp, ALU.add))
                mark().then_inc(S("m_done"), 1)
            dve.wait_ge(S("x_for_update"), 16)
            for j in range(KD):
                g = sl.next()
                got(g)
                STT(out=x[:, j, 0:TS], in0=bank(g[0]), scalar=modv[:, 16 + j, 0:1], in1=x[:, j, 0:TS], op0=ALU.mult,
                    op1=ALU.add)
                STT(out=x[:, j, TS:TOK], in0=bank2(g[0])[:, 0:TP], scalar=modv[:, 16 + j, 1:2], in1=x[:, j, TS:TOK],
                    op0=ALU.mult, op1=ALU.add).then_inc(free[g[0]], 1)
                dve.wait_ge(free[g[0]], g[1])
                mark().then_inc(x_ready, 1)
            norm_vector(1, 'norm2', 32)
            sl.r = 0
            for _ in range(32):
                sl.next()
            base = list(sl.n)
            dve.wait_ge(S("r_scores"), 1)
            NEG = -3.0e38

            def one_hots(t, q):
                if q == 0:
                    dve.wait_ge(free[2], base[2] + 17 * t + 1)
                if q >= 4 or t:
                    dve.wait_ge(full[2 + q % 2], group_use(t, q, 4))
                for i in range(4):
                    n = q * 4 + i
                    ins = TSC(r_L[:, n % NOH, :], C('iota'), r_T[:, t % 2, 0, n:n + 1], r_T[:, t % 2, 2, n:n + 1],
                              ALU.is_equal, ALU.mult)
                ins.then_inc(S("r_L"), 1)


            def top16(vals, out, idx, tmp):
                link(vv.max(out[:, 0:8], vals))
                vv.max_index(idx[:, 0:8], out[:, 0:8], vals)
                link(vv.match_replace(tmp, out[:, 0:8], vals, NEG))
                link(vv.max(out[:, 8:16], tmp))
                link(vv.max_index(idx[:, 8:16], out[:, 8:16], tmp))

            for t in range(NT):
                for hp in range(16):
                    top16(r_s[:, t, hp, :], r_v[:, hp, :], r_i[:, hp, :], r_s2[:, 0:P])
                    if t:
                        one_hots(t - 1, hp)
                link(vv.tensor_copy(r_if, r_i))
                vh = r_v.rearrange("p (h s) k -> p h s k", s=2)
                for hh in range(PH):
                    ins = TT(r_c[:, hh, :].rearrange("p (a b) -> p a b", a=TOPK),
                             vh[:, hh, 0, :].unsqueeze(2).to_broadcast([P, TOPK, TOPK]),
                             vh[:, hh, 1, :].unsqueeze(1).to_broadcast([P, TOPK, TOPK]), ALU.add)
                link(ins)
                for hh in range(PH):
                    top16(r_c[:, hh, :], r_t[:, hh, :], r_p[:, hh, :], r_s2)
                    if t:
                        one_hots(t - 1, 16 + 2 * hh)
                        one_hots(t - 1, 17 + 2 * hh)
                link(TSC(r_sum[:, 0:8], r_t[:, :, 0], 0.0, None, ALU.add))
                TT(r_t, r_t, r_sum[:, 0:8].unsqueeze(2).to_broadcast([P, PH, TOPK]), ALU.subtract).then_inc(S("r_sub"), 1)
                pos = r_p.rearrange("p h k -> p (h k)")
                TSC(r_ab[:, 0, :], pos, 4, None, ALU.logical_shift_right)
                link(TSC(r_ab[:, 1, :], pos, 15, None, ALU.bitwise_and))
                link(vv.tensor_copy(r_abf, r_ab))
                dve.wait_ge(S("r_exp"), t + 1)
                link(vv.tensor_reduce(r_sum[:, 0:8], r_t, AX.X, ALU.add))
                link(vv.reciprocal(r_sum[:, 8:16], r_sum[:, 0:8]))
                if t:
                    dve.wait_ge(full[2], base[2] + 17 * (t - 1) + 1)
                link(TT(r_e[:, 2, :].rearrange("p (h k) -> p h k", h=PH), r_t,
                        r_sum[:, 8:16].unsqueeze(2).to_broadcast([P, PH, TOPK]), ALU.mult))
                for w in range(2):
                    oh = g_one.rearrange("p (c j) -> p c j", j=16)
                    link(TT(oh, r_abf[:, w, :].unsqueeze(2).to_broadcast([P, P, 16]),
                            C('jota').unsqueeze(1).to_broadcast([P, P, 16]), ALU.is_equal))
                    for hh in range(PH):
                        o8 = oh[:, hh * 16:(hh + 1) * 16, :]
                        ins = TT(o8, o8, r_if[:, 2 * hh + w, :].unsqueeze(1).to_broadcast([P, 16, 16]), ALU.mult)
                    link(ins)
                    ins = vv.tensor_reduce(r_e[:, w, :], oh, AX.X, ALU.add)
                    if w == 0:
                        link(ins)
                ins.then_inc(S("r_e"), 1)
                dve.wait_ge(S("r_e"), t + 1)
            for q in range(P // 4):
                one_hots(NT - 1, q)
            base = [base[0] + 64, base[1] + 64, base[2] + 17 * NT, base[3] + 16 * NT]

            def weigh(b, lot, r):
                dve.wait_ge(t_sem[r], lot)
                dve.wait_ge(g_sem[r], lot)
                tv = e_T[:, r, :].rearrange("p (c q n) -> p q c n", c=4, n=QT)
                TT(tv, tv, e_G[:, r, :].rearrange("p (q c n) -> p q c n", c=4, n=QT), ALU.mult)\
                    .then_inc(S("weighted"), 1)
                dve.wait_ge(S("a_rounded"), b + 1)
                TT(e_a[:, r, 1, :], e_T[:, r, :], e_a[:, r, 0, :].bitcast(F32), ALU.subtract).then_inc(S("a_rest"), 1)

            def update(use, r):
                if use is not None:
                    dve.wait_ge(free[3], use + base[3])
                for j in range(KD):
                    s = j % 4
                    dve.wait_ge(full[s], (0 if use is None else use) + (base[s] + j // 4 + 1))
                    for lo, hi, gq in ((0, HALF, 0), (HALF, TS, 0), (TS, TOK, 1)):
                        o = lo // HALF * HALF
                        ins = STT(out=x[:, j, lo:hi], in0=ps[:, 2 * s + lo // HALF, lo - o:hi - o],
                                  scalar=modv[:, 40 + j, gq:gq + 1], in1=x[:, j, lo:hi], op0=ALU.mult, op1=ALU.add)
                    ins.then_inc(free[s], 1)

            weigh(0, 16, 0)
            dve.wait_ge(S("x_back"), 16)
            with dve.Fori(0, NB // 2 - 1) as i:
                weigh(i * 2 + 1, i * 16 + 16, 1)
                update(i * 4, 0)
                weigh(i * 2 + 2, i * 16 + 32, 0)
                update(i * 4 + 2, 1)
            weigh(NB - 1, 8 * NB, 1)
            update(2 * NB - 4, 0)
            update(2 * NB - 2, 1)
            dve.wait_ge(free[3], base[3] + 2 * NB)
            sl.n = [base[s] + 2 * NB for s in range(4)]
            sl.r = 0
            mark().then_inc(x_ready, 8)
            TSC(amul[:, :, 0], V('normf', 0, 8), D ** 0.5, None, ALU.mult).then_inc(vch, 1)
            ch[0] += 1
            dve.wait_ge(vch, ch[0])
            g = sl.next()
            dve.wait_ge(free[g[0]], g[1])
            link(vv.reciprocal(rstd, rstd))
            for k in range(KD):
                STT(out=h[:, k, :], in0=x[:, k, :], scalar=amul[:, k, 0:1], in1=rstd, op0=ALU.mult, op1=ALU.mult)\
                    .then_inc(S("y_done"), 1)

        @block.gpsimd
        def _(pool):
            base = map_slots['base']
            pt = nc.gpsimd
            for n in range(4):
                m, d = (mB, mC)[n // 2], n % 2
                pool.wait_ge(S("g_in"), n + 1)
                for li, w in enumerate(LEVELS):
                    if li >= 2:
                        g = map_slots['levels'][n * 7 + li - 2]
                        pool.wait_ge(full[g[0]], g[1])
                    bv = m['b'].rearrange("p (n s w) -> p n s w", s=2, w=w)
                    xv = m['X'][li % 2].rearrange("p (n s w) -> p n s w", s=2, w=w)
                    ref = (bv[:, :, 0, w - 1:w] if d == 0 else bv[:, :, 1, 0:1])\
                        .to_broadcast([P, m['J'] * TOK // (2 * w), w])
                    pt.tensor_tensor(xv[:, :, d, :], ref, bv[:, :, d, :], ALU.subtract).then_inc(S("g_Zs"), 1)
            pool.wait_ge(S("h1_rounded"), 1)
            pool.wait_ge(full[map_slots['h_read'][0]], map_slots['h_read'][1])
            pt.tensor_tensor(e_h[:, 1], h[:], e_h[:, 0].bitcast(F32), ALU.subtract).then_inc(S("h1_rest"), 1)
            for m in range(KD * NBR + 16):
                i, o = half_of(m)
                pool.wait_ge(S("w_rounded"), m + 1)
                pt.tensor_tensor(e_w[:, m % 2, 1, :].rearrange("p (k c) -> p k c", k=KD), slab(i)[:, :, o:o + P],
                                 e_w[:, m % 2, 0, :].bitcast(F32).rearrange("p (k c) -> p k c", k=KD), ALU.subtract)\
                    .then_inc(S("w_rest"), 1)

            def rest_u(c, r):
                pool.wait_ge(S("u_rounded"), c + 1)
                pt.tensor_tensor(e_u[:, r, 1, :], e_uraw[:, r % 2, :], e_u[:, r, 0, :].bitcast(F32), ALU.subtract)\
                    .then_inc(S("u_rest"), 1)

            rest_u(0, 0)
            rest_u(1, 1)
            for st, (c0, main, tail) in enumerate(STAGES):
                if st:
                    t = st - 1
                    pool.wait_ge(free[2], base[2] + 17 * t + 1)
                    for r in range(-2, main):
                        if r >= 0:
                            rest_u(c0 + r + 2, (r + 2) % 4)
                        for q in (2 * r + 4, 2 * r + 5) if r < main - 2 else ():
                            if q >= 4 or t:
                                pool.wait_ge(full[2 + q % 2], group_use(t, q, 4))
                            for i in range(4):
                                n = q * 4 + i
                                ins = pt.tensor_scalar(r_R[:, n % NOH, :], C('iota'), r_T[:, t % 2, 1, n:n + 1], None,
                                                       ALU.is_equal)
                            ins.then_inc(S("r_R"), 1)
                else:
                    with pool.Fori(0, main // 4) as i:
                        for r in range(4):
                            rest_u(i * 4 + (c0 + r + 2), (r + 2) % 4)
                last = st == NT
                with pool.Fori(main // 4, (main + tail) // 4 - last) as i:
                    for r in range(4):
                        rest_u(i * 4 + (c0 + r + 2), (r + 2) % 4)
                if last:
                    rest_u(NKEY - 2, 2)
                    rest_u(NKEY - 1, 3)
            with pool.Fori(0, NB // 2) as i:
                for r in range(2):
                    for c in range(4):
                        pool.wait_ge(S("v_rounded"), i * 8 + (4 * r + c + 1))
                        ins = pt.tensor_tensor(e_v[:, r, 1, c, :], e_vraw[:, c, :], e_v[:, r, 0, c, :].bitcast(F32),
                                               ALU.subtract)
                        ins.then_inc(S(f"v_rest{c}"), 1)

        @block.sync
        def _(sp):
            sp.dma_start(vec[:], vec_in).then_inc(load, 16)
            sp.dma_start(cst[:], cst_in).then_inc(load, 16)
            sp.dma_start(lvl_f, lvl_in).then_inc(load, 16)
            sp.dma_start(wsm, wsm_in).then_inc(load, 16)
            sp.dma_start(rowv, rowv_in).then_inc(load, 16)
            loaded = 0
            for i in range(NSLAB):
                if i >= RING:
                    j = i - RING
                    if j < MOD1 - 1:
                        sp.wait_ge(S("mod_slab_used"), j + 1)
                    elif j in slab_last:
                        s, u = slab_last[j]
                        sp.wait_ge(full[s], u)
                    else:
                        break
                    if j == SLABS['merge'] + 22:
                        sp.dma_start(x[:], xpark).then_inc(S("x_for_update"), 16)
                sp.dma_start(wring[:, i % RING, :], slabs[i]).then_inc(slab_in[i % RING], 16)
                loaded += 1
            base = map_slots['base']

            def load_u(c, r):
                sp.dma_start(e_uraw[:, r, :], u_in[bass.ds(c, 1)].rearrange("o p c -> p (o c)")).then_inc(u_sem[r], 16)

            def store_t(c, use, r):
                sp.wait_ge(free[r], use)
                sp.dma_start(tmap[bass.ds(c, 1)].rearrange("o p t -> p (o t)"), e_t[:, r, :]).then_inc(t_out[r], 16)

            sp.wait_ge(h_done, 32)
            load_u(0, 0)
            load_u(1, 1)
            def load_tg(b, r):
                sp.dma_start(e_T[:, r, :].rearrange("p (c t) -> p c t", c=4),
                             tmap.rearrange("(b c) p t -> b p c t", c=4)[bass.ds(b, 1)].rearrange("o p c t -> p (o c) t"))\
                    .then_inc(t_sem[r], 16)
                sp.dma_start(e_G[:, r, :], gmap[bass.ds(b, 1)].rearrange("o p q c n -> p (o q c n)"))\
                    .then_inc(g_sem[r], 16)

            def load_v(c, r):
                sp.dma_start(e_vraw[:, r, :], v_in[bass.ds(c, 1)].rearrange("o p d -> p (o d)")).then_inc(v_sem[r], 16)

            EARLY = 2
            with sp.Fori(0, NKEY // 2 - 1 - EARLY) as i:
                for r in range(2):
                    sp.wait_ge(S("u_rest"), i * 2 + (r + 1))
                    load_u(i * 2 + (r + 2), r)
                    store_t(i * 2 + r, i + (base[r] + 1), r)
            last = map_slots['base2']
            for s in (2, 3):
                sp.wait_ge(full[s], last[s])
                sp.wait_ge(free[s], last[s])
            for r in range(2):
                sp.wait_ge(map_out[r], 16 * 2 * NT)
                sp.wait_ge(t_out[r], 16 * 4)
            load_tg(0, 0)
            for c in range(3):
                load_v(c, c)
            for c in range(NKEY - 2 - 2 * EARLY, NKEY - 2):
                sp.wait_ge(S("u_rest"), c + 1)
                load_u(c + 2, c % 2)
                store_t(c, base[c % 2] + c // 2 + 1, c % 2)
            for r in range(2):
                store_t(NKEY - 2 + r, base[r] + NKEY // 2, r)
            base = map_slots['base2']
            for s in range(2):
                sp.wait_ge(full[s], base[s])
                sp.wait_ge(free[s], base[s])
            load_v(3, 3)
            load_tg(1, 1)
            sp.dma_start(x[:], xpark).then_inc(S("x_back"), 16)
            for r in range(2):
                sp.wait_ge(t_out[r], 16 * NKEY // 2)
            with sp.Fori(0, NB // 2 - 1) as i:
                for r in range(2):
                    for c in range(4):
                        sp.wait_ge(S(f"v_rest{c}"), i * 2 + (r + 1))
                        load_v(i * 8 + (4 * r + 4 + c), c)
                    sp.wait_ge(S("a_rest"), i * 2 + (r + 1))
                    load_tg(i * 2 + (r + 2), r)
            for c in range(4):
                sp.wait_ge(S(f"v_rest{c}"), NB - 1)
                load_v(NKEY - 4 + c, c)
            for r in range(RING):
                sp.wait_ge(slab_in[r], 16 * sum(1 for k in range(loaded) if k % RING == r))
            sp.wait_ge(stored, 16 * STORES[0])


def kernel(**inputs):
    import concourse.bacc as bacc
    from concourse.bass_utils import run_bass_kernel_spmd

    I = {k: np.ascontiguousarray(np.asarray(v)) for k, v in inputs.items()}
    f = np.float32

    def chan(v):
        return v.reshape(-1, P).T

    def slab_cols(w, c0, n):
        return [w[:, c0 + 256 * i:c0 + 256 * (i + 1)].reshape(KD, P, 256).transpose(1, 0, 2).reshape(P, SLAB)
                for i in range(n)]

    w_in, b_in = I['w_in'][0], I['b_in'][0]
    wb = I['w_branch'][0]
    sl = []
    for name in SLABS:
        if name == 'merge':
            break
        if name == 'mod':
            sl += slab_cols(I['w_mod'][0], 0, MOD1)
        elif name.startswith('mod'):
            sl += slab_cols(I['w_mod'][0], 256 * (MOD1 + 4 * int(name[3])), 4)
        elif name.startswith('b_f'):
            sl += slab_cols(w_in, COL['b_f'][0] + 512 * int(name[3]), 2)
        else:
            a, b = COL[name]
            sl += slab_cols(w_in, a, (b - a) // 256)
    gates = w_in[:, COL['gates'][0]:].reshape(KD, P, NBR, KD, P)
    for j in range(KD):
        gj = gates[:, :, :, j, :].transpose(1, 0, 2, 3)
        sl += [gj[:, :, 0:2].reshape(P, SLAB), gj[:, :, 2:4].reshape(P, SLAB)]
        sl.append(wb.reshape(NBR, 4, P, KD, P)[:, :, :, j, :].transpose(2, 0, 1, 3).reshape(P, SLAB))
    sl += slab_cols(I['w_out'][0], 0, 4)
    sl += slab_cols(I['peer_w_q'][0], 0, 8)
    slabs = np.stack(sl)
    assert len(slabs) == NSLAB

    quarter = D // 4
    omega = (f(1.0) / (f(10000.0) ** (np.arange(quarter, dtype=f) / f(quarter)))).astype(f)

    def enc(n):
        ang = np.arange(n, dtype=f)[None, :] * omega[:, None]
        return np.concatenate([np.sin(ang), np.cos(ang)], 0).astype(f)

    def ptab(n):
        return enc(n).reshape(4, P, n).transpose(1, 0, 2).reshape(P, 4 * n)

    def seg(name):
        return chan(b_in[COL[name][0]:COL[name][1]])

    parts = {
        'b_mod': chan(I['b_mod'][0]), 'norm1': chan(I['norm1_g'][0]), 'norm2': chan(I['norm2_g'][0]),
        'normf': chan(I['final_norm_g']), 'a_q': seg('a_q'), 'a_k': seg('a_k'), 'a_o': seg('a_o'),
        'b_q': seg('b_q'), 'b_f': seg('b_f'), 'b_g': seg('b_g'), 'c_q': seg('c_q'), 'c_k': seg('c_k'),
        'c_g': seg('c_g'), 'd_x': seg('d_x'), 'd_g': seg('d_g'), 'gates': seg('gates'),
        'b_up': chan(I['b_gla_up'][0].reshape(-1)), 'lb': chan(I['hgrn_lower_bounds'][0].reshape(-1)),
        'conv_w': chan(I['conv_w'][0].reshape(-1)), 'conv_b': chan(I['conv_b'][0]),
        'lru_b_a': chan(I['lru_b_a'][0].reshape(-1)), 'lru_b_x': chan(I['lru_b_x'][0].reshape(-1)),
        'lam': chan(I['lru_lambda'][0].reshape(-1)), 'h0': chan(I['state_lru_h'][0, 0].reshape(-1)),
        'n0': chan(I['state_mlstm_n'][0, 0].reshape(-1)),
        'cond': np.stack([chan(I['c'][0]), chan(I['c_ctx'])], 2).reshape(P, 16),
        'pos_r': ptab(TS // GRID_W), 'pos_c': ptab(GRID_W),
    }
    vec = np.concatenate([parts[n] for n in VEC], 1).astype(f)

    r = np.arange(P)
    reset0 = np.tile((r != 0).astype(f), NT)[None, :].repeat(P, 0)
    reset1 = np.tile((r != P - 1).astype(f), NT)[None, :].repeat(P, 0)
    sel = np.zeros((P, 4, P), f)
    for i in range(4):
        sel[i, i, :] = 1.0
    s_, t_ = r[:, None], r[None, :]
    csts = {
        'ident': np.eye(P, dtype=f), 'ones': np.ones((P, P), f), 'iota': np.broadcast_to(r.astype(f), (P, P)),
        'over0': np.where(s_ <= t_, 0, 1e30).astype(f), 'over1': np.where(s_ >= t_, 0, 1e30).astype(f),
        'reset0': reset0, 'reset1': reset1, 'sel': sel.reshape(P, -1),
        'jota': np.broadcast_to(np.arange(16, dtype=f), (P, 16)),
        'epsD': np.full((P, 1), D * EPS, f), 'epsP': np.full((P, 1), P * EPS, f),
    }
    cst = np.concatenate([csts[n] for n in CST], 1).astype(f)
    lv = np.zeros((P, 2, len(LEVELS), P), f)
    for i, w in enumerate(LEVELS):
        m = (s_ // (2 * w) == t_ // (2 * w)) & (s_ % (2 * w) < w) & (t_ % (2 * w) >= w)
        lv[:, 0, i], lv[:, 1, i] = m, m.T

    small = np.concatenate([w_in[:, COL[n][0]:COL[n][1]] for n in ('a_i', 'a_f', 'c_lr')], 1)
    wsm = small.reshape(KD, P, 48).transpose(1, 0, 2).reshape(P, KD * 48)
    rowv = np.zeros((16, 8), f)
    rowv[0:4, 0:2] = I['state_mlstm_m'][0, 0].T
    bi, bf = (b_in[COL[n][0]:COL[n][1]].reshape(2, 4) for n in ('a_i', 'a_f'))
    for d in range(2):
        rowv[0:4, 2 + 2 * d], rowv[0:4, 3 + 2 * d] = bi[d], bf[d]
    rowv[:, 6:8] = b_in[COL['c_lr'][0]:COL['c_lr'][1]].reshape(2, 16).T
    tokb = np.stack([np.broadcast_to(b_in[COL[n][0]:COL[n][1]], (P, W)) for n in ('a_v', 'b_i', 'c_v')])
    x = np.concatenate([I['x_sample'][0].T, I['x_prompt'][0].T], 1).reshape(KD, P, TOK).transpose(1, 0, 2)
    sc = I['state_gla_S'][0, 0].reshape(2, 2, 2, 64, P).transpose(2, 3, 0, 1, 4).reshape(P, 2, 2, P)
    lruw = np.stack([I['lru_w_a'][0], I['lru_w_x'][0]]).transpose(3, 0, 1, 2, 4)
    ex_u = I['peer_u'][0].reshape(NKEY, NKEY, KD, P).transpose(1, 3, 2, 0).reshape(NKEY, P, D)
    ex_v = I['peer_v'][0].reshape(NKEY, NKEY, D).transpose(1, 0, 2)
    arrays = {
        'x': x, 'slabs': slabs, 'vec': vec, 'cst': cst, 'lvl': lv, 'wsm': wsm, 'rowv': rowv,
        'up': I['w_gla_up'][0].transpose(1, 0, 2), 'tokb': tokb,
        'c0': I['state_mlstm_C'][0, 0].transpose(2, 0, 1, 3), 's0b': I['state_hgrn_S'][0, 0].transpose(2, 0, 1, 3),
        's0c': sc, 'lruw': lruw, 'sk': I['peer_sub_keys'][0].reshape(16, P, P).transpose(2, 0, 1),
        'u': ex_u, 'v': ex_v,
    }
    nc = bacc.Bacc("TRN2", target_bir_lowering=False, num_devices=1)
    args, feed = [], {}
    for name, a in arrays.items():
        feed[name + '_in'] = np.ascontiguousarray(a)
        args.append(nc.dram_tensor(name + '_in', a.shape, mybir.dt.from_np(a.dtype), kind="ExternalInput").ap())
    outs = {'y': (P, KD, TOK), 'C': (8, P, P), 'n': (8, P, 1), 'm': (2, 4, 1), 'Sb': (8, P, P), 'Sc': (8, 64, P),
            'h': (8, P, 1)}
    for name, shape in outs.items():
        args.append(nc.dram_tensor(name + '_out', shape, F32, kind="ExternalOutput").ap())
    for name, shape in (('expert_map', (NB, P, 4 * NT, 4, 32)), ('activations', (NKEY, P, TOK)), ('x_parked', (P, KD, TOK))):
        args.append(nc.dram_tensor(name, shape, F32, kind="Internal").ap())
    build_kernel(nc, *args)
    res = run_bass_kernel_spmd(nc, [feed], core_ids=[0]).results[0]
    y = np.asarray(res['y_out']).transpose(1, 0, 2).reshape(D, TOK)
    return (y[:, TS:].T[None], y[:, :TS].T[None], res['C_out'].reshape(1, 1, 2, 4, P, P),
            res['n_out'].reshape(1, 1, 2, 4, P), res['m_out'].reshape(1, 1, 2, 4),
            res['Sb_out'].reshape(1, 1, 2, 4, P, P), res['Sc_out'].reshape(1, 1, 2, 4, 64, P),
            res['h_out'].reshape(1, 1, 2, W))
```
